# Optimizing a Trainium2 kernel written in Bass

```python
import math
import jax, jax.numpy as jnp
from jax import lax
import numpy as np

D_MODEL = 1024
BATCH = 1
SEQ = 128
DEPTH = 1
DEC_BATCH = 1
DEC_SEQ = 512
PAST_LEN = 128

GRID_W = 64
D_SSD = D_MODEL
HEADDIM = 64
N_HEADS = D_SSD // HEADDIM
N_BC_GROUPS = 2
D_STATE = 128
D_CONV = 4
CHUNK = 128
CONV_DIM = D_SSD + 2 * N_BC_GROUPS * D_STATE
D_POOL = D_MODEL
POOL_WINDOWS = (2, 4, 8, 16)
N_POOL_GROUPS = len(POOL_WINDOWS)
POOL_GROUP_W = D_POOL // N_POOL_GROUPS
D_MIX = D_SSD + D_POOL
D_IN_PROJ = D_SSD + CONV_DIM + 2 * N_HEADS + D_POOL
N_EXPERTS = 16
N_EXPERT_GROUPS = 4
EXPERTS_PER_GROUP = N_EXPERTS // N_EXPERT_GROUPS
TOP_K = 2
D_FF_EXPERT = D_MODEL // 2
EPS = 1e-6

kernel_name = "hybrid_ssd_pool_moe_diffusion_step"

F32 = jnp.float32

def rmsnorm(x, w):
    xf = x.astype(F32)
    y = xf * lax.rsqrt(jnp.mean(xf * xf, axis=-1, keepdims=True) + EPS)
    return (y * w.astype(F32)).astype(x.dtype)

def centred_depthwise_conv(x, w, b):
    pad_lo = (D_CONV - 1) // 2
    pad_hi = D_CONV - 1 - pad_lo
    y = lax.conv_general_dilated(x, w.astype(x.dtype)[:, None, :], window_strides=(1,),
                                 padding=[(pad_lo, pad_hi)],
                                 dimension_numbers=("NWC", "WIO", "NWC"),
                                 feature_group_count=x.shape[-1])
    return y + b.astype(x.dtype)

def segsum(x):
    T = x.shape[-1]
    xr = jnp.broadcast_to(x[..., None], x.shape + (T,))
    xr = jnp.where(jnp.tril(jnp.ones((T, T), bool), -1), xr, 0.0)
    cs = jnp.cumsum(xr, axis=-2)
    return jnp.where(jnp.tril(jnp.ones((T, T), bool), 0), cs, -jnp.inf)

def ssd_chunked(x, dt, a, Bh, Ch, init):
    b, L, h, p = x.shape
    n = Bh.shape[-1]
    nc = L // CHUNK
    x = x.astype(F32)
    xd = (x * dt[..., None]).reshape(b, nc, CHUNK, h, p)
    A = jnp.transpose((dt * a).reshape(b, nc, CHUNK, h), (0, 3, 1, 2))
    Bc = Bh.astype(F32).reshape(b, nc, CHUNK, h, n)
    Cc = Ch.astype(F32).reshape(b, nc, CHUNK, h, n)
    A_cum = jnp.cumsum(A, axis=-1)
    scores = jnp.einsum("bclhn,bcshn->bhcls", Cc, Bc) * jnp.exp(segsum(A))
    y_diag = jnp.einsum("bhcls,bcshp->bclhp", scores, xd)
    decay_states = jnp.exp(A_cum[..., -1:] - A_cum)
    states = jnp.einsum("bclhn,bhcl,bclhp->bchpn", Bc, decay_states, xd)
    states = jnp.concatenate([init.astype(F32)[:, None], states], axis=1)
    chunk_A = jnp.pad(A_cum[..., -1], ((0, 0), (0, 0), (1, 0)))
    new_states = jnp.einsum("bhzc,bchpn->bzhpn", jnp.exp(segsum(chunk_A)), states)
    states, final = new_states[:, :-1], new_states[:, -1]
    y_off = jnp.einsum("bclhn,bchpn,bhcl->bclhp", Cc, states, jnp.exp(A_cum))
    return (y_diag + y_off).reshape(b, L, h, p), final

def ssd_direction(xs, dt_raw, Bh, Ch, dt_bias, a_log, d_skip, init, reverse):
    if reverse:
        xs, dt_raw, Bh, Ch = (jnp.flip(t, axis=1) for t in (xs, dt_raw, Bh, Ch))
    dt = jax.nn.softplus(dt_raw.astype(F32) + dt_bias.astype(F32))
    y, final = ssd_chunked(xs, dt, -jnp.exp(a_log.astype(F32)), Bh, Ch, init)
    y = y + d_skip.astype(F32)[:, None] * xs.astype(F32)
    if reverse:
        y = jnp.flip(y, axis=1)
    return y, final

def window_bounds(n, w):
    idx = np.arange(n)
    lo = np.clip(idx - w // 2, 0, n - 1)
    hi = np.clip(idx + w // 2 - 1, 0, n - 1)
    return lo, hi

def pool_mean_1d(v, w):
    L = v.shape[1]
    cs = jnp.pad(jnp.cumsum(v, axis=1), ((0, 0), (1, 0), (0, 0)))
    lo, hi = window_bounds(L, w)
    s = jnp.take(cs, hi + 1, axis=1) - jnp.take(cs, lo, axis=1)
    cnt = (hi - lo + 1).astype(np.float32)
    return s / cnt[None, :, None]

def pool_mean_2d(v, w, rows):
    b, L, C = v.shape
    v4 = v.reshape(b, rows, GRID_W, C)
    S = jnp.pad(jnp.cumsum(jnp.cumsum(v4, axis=1), axis=2), ((0, 0), (1, 0), (1, 0), (0, 0)))
    r0, r1 = window_bounds(rows, w)
    c0, c1 = window_bounds(GRID_W, w)
    Dr = jnp.take(S, r1 + 1, axis=1) - jnp.take(S, r0, axis=1)
    s = jnp.take(Dr, c1 + 1, axis=2) - jnp.take(Dr, c0, axis=2)
    cnt = ((r1 - r0 + 1)[:, None] * (c1 - c0 + 1)[None, :]).astype(np.float32)
    return (s / cnt[None, :, :, None]).reshape(b, L, C)

def pool_mixer(v, pool_w, pool_scale, grid):
    b, L, _ = v.shape
    vf = v.astype(F32)
    outs = []
    for g, w in enumerate(POOL_WINDOWS):
        vg = vf[..., g * POOL_GROUP_W:(g + 1) * POOL_GROUP_W]
        m = pool_mean_2d(vg, w, L // GRID_W) if grid else pool_mean_1d(vg, w)
        outs.append(m - vg)
    u = jnp.stack(outs, axis=2)
    u = jnp.einsum("blgc,gcd->blgd", u, pool_w.astype(F32)).reshape(b, L, D_POOL)
    return u * pool_scale.astype(F32)

def routed_moe(h, w_router, router_bias, w_gate, w_up, w_down):
    b, L, d = h.shape
    t = h.reshape(b * L, d)
    probs = jax.nn.softmax(t.astype(F32) @ w_router.astype(F32), axis=-1)
    sel = probs + router_bias.astype(F32)
    grp_score = lax.top_k(sel.reshape(-1, N_EXPERT_GROUPS, EXPERTS_PER_GROUP), TOP_K)[0].sum(-1)
    best = jnp.argmax(grp_score, axis=-1)
    in_group = (jnp.arange(N_EXPERTS) // EXPERTS_PER_GROUP)[None, :] == best[:, None]
    _, idx = lax.top_k(jnp.where(in_group, sel, -jnp.inf), TOP_K)
    gate = jnp.take_along_axis(probs, idx, axis=-1)
    gate = gate / jnp.sum(gate, axis=-1, keepdims=True)
    combine = jnp.sum(jax.nn.one_hot(idx, N_EXPERTS, dtype=F32) * gate[..., None], axis=1)
    g = jnp.einsum("td,edf->tef", t, w_gate)
    u = jnp.einsum("td,edf->tef", t, w_up)
    a = jax.nn.silu(g) * u * combine[..., None].astype(g.dtype)
    out = jnp.einsum("tef,efd->td", a, w_down)
    return out.reshape(b, L, d)

def trunk_layer(x, cvec, init_f, init_b, grid, w_ada, b_ada, norm1_w, w_in, conv_w, conv_b,
                dt_bias, a_log, d_skip, ssd_norm_w, pool_w, pool_scale, w_out, norm2_w,
                w_router, router_bias, w_gate, w_up, w_down):
    b, L, _ = x.shape
    ada = jax.nn.silu(cvec.astype(F32)) @ w_ada.astype(F32) + b_ada.astype(F32)
    shift1, scale1, gate1, shift2, scale2, gate2 = jnp.split(ada[:, None, :], 6, axis=-1)
    h = rmsnorm(x, norm1_w) * (1.0 + scale1) + shift1
    proj = h @ w_in
    z, xBC, dt_raw, v = jnp.split(proj, [D_SSD, D_SSD + CONV_DIM, D_SSD + CONV_DIM + 2 * N_HEADS], axis=-1)
    xBC = jax.nn.silu(centred_depthwise_conv(xBC, conv_w, conv_b))
    xs, Bm, Cm = jnp.split(xBC, [D_SSD, D_SSD + N_BC_GROUPS * D_STATE], axis=-1)
    xs = xs.reshape(b, L, N_HEADS, HEADDIM)
    rep = N_HEADS // N_BC_GROUPS
    Bh = jnp.repeat(Bm.reshape(b, L, N_BC_GROUPS, D_STATE), rep, axis=2)
    Ch = jnp.repeat(Cm.reshape(b, L, N_BC_GROUPS, D_STATE), rep, axis=2)
    y_f, s_f = ssd_direction(xs, dt_raw[..., :N_HEADS], Bh, Ch, dt_bias[0], a_log[0], d_skip[0], init_f, False)
    y_b, s_b = ssd_direction(xs, dt_raw[..., N_HEADS:], Bh, Ch, dt_bias[1], a_log[1], d_skip[1], init_b, True)
    y = (y_f + y_b).reshape(b, L, D_SSD)
    y = rmsnorm(y * jax.nn.silu(z.astype(F32)), ssd_norm_w)
    u = pool_mixer(v, pool_w, pool_scale, grid)
    mix = jnp.concatenate([y, u], axis=-1) @ w_out
    x = x + gate1 * mix
    h2 = rmsnorm(x, norm2_w) * (1.0 + scale2) + shift2
    x = x + gate2 * routed_moe(h2, w_router, router_bias, w_gate, w_up, w_down)
    return x, s_f, s_b

def setup_inputs(seed: int = 0) -> dict:
    key = jax.random.key(seed)
    ks = jax.random.split(key, 26)

    def nrm(k, shape, scale):
        return jax.random.normal(k, shape, jnp.float32) * scale

    dt0 = jnp.exp(jax.random.uniform(ks[10], (DEPTH, 2, N_HEADS), jnp.float32)
                  * (math.log(0.1) - math.log(0.001)) + math.log(0.001))
    return {
        "x_prompt": nrm(ks[0], (BATCH, SEQ, D_MODEL), 1.0),
        "x_sample": nrm(ks[1], (DEC_BATCH, DEC_SEQ, D_MODEL), 1.0),
        "state_ssm": nrm(ks[2], (DEC_BATCH, DEPTH, 2, N_HEADS, HEADDIM, D_STATE), 0.1),
        "c": nrm(ks[3], (DEC_BATCH, D_MODEL), 1.0),
        "c_ctx": nrm(ks[4], (D_MODEL,), 1.0),
        "w_ada": nrm(ks[5], (DEPTH, D_MODEL, 6 * D_MODEL), 0.5 * D_MODEL ** -0.5),
        "b_ada": nrm(ks[6], (DEPTH, 6 * D_MODEL), 0.02),
        "norm1_w": 1.0 + nrm(ks[7], (DEPTH, D_MODEL), 0.02),
        "w_in": nrm(ks[8], (DEPTH, D_MODEL, D_IN_PROJ), D_MODEL ** -0.5),
        "conv_w": nrm(ks[9], (DEPTH, D_CONV, CONV_DIM), D_CONV ** -0.5),
        "conv_b": nrm(ks[11], (DEPTH, CONV_DIM), 0.02),
        "dt_bias": dt0 + jnp.log(-jnp.expm1(-dt0)),
        "a_log": jnp.log(jax.random.uniform(ks[12], (DEPTH, 2, N_HEADS), jnp.float32, 1.0, 16.0)),
        "d_skip": 1.0 + nrm(ks[13], (DEPTH, 2, N_HEADS), 0.1),
        "ssd_norm_w": 1.0 + nrm(ks[14], (DEPTH, D_SSD), 0.02),
        "pool_w": nrm(ks[15], (DEPTH, N_POOL_GROUPS, POOL_GROUP_W, POOL_GROUP_W), POOL_GROUP_W ** -0.5),
        "pool_scale": 1.0 + nrm(ks[16], (DEPTH, D_POOL), 0.1),
        "w_out": nrm(ks[17], (DEPTH, D_MIX, D_MODEL), D_MIX ** -0.5),
        "norm2_w": 1.0 + nrm(ks[18], (DEPTH, D_MODEL), 0.02),
        "w_router": nrm(ks[19], (D_MODEL, N_EXPERTS), D_MODEL ** -0.5),
        "router_bias": nrm(ks[20], (N_EXPERTS,), 0.01),
        "w_gate": nrm(ks[21], (DEPTH, N_EXPERTS, D_MODEL, D_FF_EXPERT), D_MODEL ** -0.5),
        "w_up": nrm(ks[22], (DEPTH, N_EXPERTS, D_MODEL, D_FF_EXPERT), D_MODEL ** -0.5),
        "w_down": nrm(ks[23], (DEPTH, N_EXPERTS, D_FF_EXPERT, D_MODEL), D_FF_EXPERT ** -0.5),
        "final_norm_w": 1.0 + nrm(ks[24], (D_MODEL,), 0.02),
    }

def reference(x_prompt, x_sample, state_ssm, c, c_ctx, w_ada, b_ada, norm1_w, w_in, conv_w, conv_b,
              dt_bias, a_log, d_skip, ssd_norm_w, pool_w, pool_scale, w_out, norm2_w,
              w_router, router_bias, w_gate, w_up, w_down, final_norm_w):
    def layer_weights(l):
        return (w_ada[l], b_ada[l], norm1_w[l], w_in[l], conv_w[l], conv_b[l], dt_bias[l], a_log[l],
                d_skip[l], ssd_norm_w[l], pool_w[l], pool_scale[l], w_out[l], norm2_w[l],
                w_router, router_bias, w_gate[l], w_up[l], w_down[l])

    zero_state = jnp.zeros((x_prompt.shape[0], N_HEADS, HEADDIM, D_STATE), F32)
    hp = x_prompt
    ctx_states = []
    for l in range(DEPTH):
        hp, s_f, s_b = trunk_layer(hp, c_ctx[None, :], zero_state, zero_state, False, *layer_weights(l))
        ctx_states.append(jnp.stack([s_f, s_b], axis=1))
    new_state_ssm = jnp.stack(ctx_states, axis=1)
    y_prompt = rmsnorm(hp, final_norm_w)

    hs = x_sample
    for l in range(DEPTH):
        hs, _, _ = trunk_layer(hs, c, state_ssm[:, l, 0], state_ssm[:, l, 1], True, *layer_weights(l))
    y_sample = rmsnorm(hs, final_norm_w)
    return (y_prompt, y_sample, new_state_ssm)


_drawn_inputs = setup_inputs


def setup_inputs(seed=0):
    import zlib

    import numpy as np

    out = dict(_drawn_inputs(seed))
    spreads = {}
    factors = {'ssd_norm_w': 3.315, 'norm2_w': 2.959, 'final_norm_w': 2.851}
    for name, (base, spread) in spreads.items():
        noise = np.random.default_rng([zlib.crc32(name.encode()), seed]).standard_normal(out[name].shape)
        drawn = base * np.exp(spread * noise) if base else spread * noise
        out[name] = __import__('jax').numpy.asarray(drawn.astype(out[name].dtype))
    for name, factor in factors.items():
        out[name] = (out[name] * factor).astype(out[name].dtype)
    return out
```

```python
from contextlib import ExitStack

import numpy as np

import concourse.bass as bass
import concourse.mybir as mybir
from concourse.alu_op_type import AluOpType as ALU

F32 = mybir.dt.float32
BF16 = mybir.dt.bfloat16
I32 = mybir.dt.int32
ACT = mybir.ActivationFunctionType
AX_X = mybir.AxisListType.X

P = 128
D = 1024
KT = D // P
CTX, LAT = 128, 512
TOK = CTX + LAT
NJ = TOK // P
GRID_W = 64
ROWS = LAT // GRID_W
H, HD, N = 16, 64, 128
HG = H // 2
E, EG, EPG = 16, 4, 4
FF = 512
FT = FF // P
CONVF = 12
WINDOWS = (2, 4, 8, 16)
EPS = 1e-6
BIG = 1e30
MAX_TILES = 26
SLOTS = MAX_TILES * P
RING = 3
CHUNK = 4096

C_ID, C_TRIF, C_TRIB, C_ONES = 0, 128, 256, 384
C_P16, C_P4, C_ITEM, C_STEP, C_TOKEN = 512, 528, 532, 560, 564
C_ALL = 572
B_STRICT, B_MASK, B_STACK, B_ALL = 0, 128, 384, 416
XDD_ORDER = ((0, 0), (1, 0), (0, 1), (1, 4), (0, 2), (1, 3), (0, 3), (1, 2))
V_ADA, V_N1, V_N2, V_CW, V_CB, V_PS, V_SN, V_C = 0, 96, 112, 128, 176, 188, 196, 204
V_ALL = 220
R_RB, R_DTB, R_ALOG, R_DSK = 0, 16, 48, 80
R_ALL = 112
INV_ALL = 4 * TOK


class Steps:

    def __init__(self, eng, sem):
        self.eng, self.sem, self.n = eng, sem, 0

    def __call__(self, ins):
        self.n += 1
        ins.then_inc(self.sem, 1)
        self.eng.wait_ge(self.sem, self.n)


def trunk_kernel(nc, consts, bconsts, vecs, rows, inv, norm2, fnorm, x, states0, w_ring, w_late, b_late, w_dt, w_pool, w_router,
                 w_exp, y_out, s_out):
    ctx = ExitStack()
    with ctx:
        def sb(name, shape, dt=F32):
            return ctx.enter_context(nc.sbuf_tensor(name, shape, dt))

        def sem(name):
            return ctx.enter_context(nc.semaphore(name))

        ada_rows = nc.dram_tensor("ada_rows", [4, 2, D], F32).ap()
        h2_dram = nc.dram_tensor("h2_dram", [TOK, D], F32).ap()
        slot_token = nc.dram_tensor("slot_token", [SLOTS, 1], I32).ap()
        slot_out = nc.dram_tensor("slot_out", [SLOTS - P, D], F32).ap()

        ring = sb("ring", [P, RING, CHUNK])
        ex = sb("ex", [P, 12288])
        yT = sb("yT", [P, KT, TOK])
        xs = sb("xs", [P, NJ, D])
        bcT = sb("bcT", [P, 4, TOK])
        btok = sb("btok", [P, NJ, 2 * N])
        gT = sb("gT", [P, NJ, 2, P])
        uT = sb("uT", [P, KT, TOK])
        hT = sb("hT", [P, KT, TOK])
        cst = sb("cst", [P, C_ALL])
        vec = sb("vec", [P, V_ALL])
        row = sb("row", [P, R_ALL])
        idb = sb("idb", [P, P], BF16)
        maskb = sb("maskb", [P, 2, P], BF16)
        strictb = sb("strictb", [P, P], BF16)
        onesb = sb("onesb", [P, P], BF16)
        stackb = sb("stackb", [96, 32], BF16)
        silc = sb("silc", [P, 2 * KT])
        modA = sb("modA", [P, 2 * KT])
        modB = sb("modB", [P, 2 * KT])
        stat = sb("stat", [P, 26])
        eps_col = sb("eps_col", [P, 1])
        dts = sb("dts", [P, 8, NJ * 32])
        wrt = sb("wrt", [P, KT, E])
        nega = sb("nega", [P, 32])
        dsum = sb("dsum", [P, H])

        ident = cst[:, C_ID:C_ID + P]
        trif = cst[:, C_TRIF:C_TRIF + P]
        trib = cst[:, C_TRIB:C_TRIB + P]
        ones = cst[:, C_ONES:C_ONES + P]
        dt_, a_, ncum, ecum, dec, etot, sc0, sc1 = (dts[:, i, :] for i in range(8))
        dtdec = dec

        xt = ex[:, 0:NJ * D].rearrange("p (j d) -> p j d", j=NJ)
        XP = 131 + 515
        xpad = [ex[:, i * XP:(i + 1) * XP] for i in range(2)]
        cacc = [ex[:, 1300 + i * XP:1300 + i * XP + 643] for i in range(2)]
        xsT = [ex[:, 2600 + i * TOK:2600 + (i + 1) * TOK] for i in range(2)]
        pa, pb_, pc = (ex[:, 3900 + i * 960:3900 + (i + 1) * 960] for i in range(3))
        arow = ex[0:2, 5120:5120 + 2048]
        brow = ex[0:1, 6784:6784 + 512]
        n2row = ex[0:1, 7296:7296 + D]
        orow = ex[0:1, 8320:8320 + D]
        invb = ex[:, 12288 - INV_ALL:12288]
        wdt = gT[:, 0, :, :].rearrange("p a b -> p (a b)")
        st = ex[:, 0:8 * D].rearrange("p (i d) -> p i d", i=8)
        xdt = ex[:, 8192:8192 + 2 * D].rearrange("p (i d) -> p i d", i=2)
        xdd = ex[:, 10240:10240 + 2 * D].rearrange("p (i d) -> p i d", i=2)
        hf = hT[:, :, :].rearrange("p k t -> p (k t)")
        uf = uT[:, :, :].rearrange("p k t -> p (k t)")
        zf = yT[:, :, :].rearrange("p k t -> p (k t)")
        bf_ = bcT[:, :, :].rearrange("p f t -> p (f t)")
        btf = btok[:, :, :].rearrange("p j n -> p (j n)")
        adaw = [zf[:, i * 2048:(i + 1) * 2048].rearrange("p (k c) -> p k c", k=4) for i in range(2)]
        acc = [zf[:, 4096:5120], ex[:, 2600:3624]]
        gT_pw = zf[:, 0:2048].rearrange("p (g k m) -> p g k m", g=4, k=2)
        bcst = hf[:, 0:B_ALL]
        tabT = [bf_[0:96, d * 320:(d + 1) * 320].bitcast(BF16) for d in range(2)]
        yt = [bf_[:, 640:1152], ex[:, 11776:12288]]
        wbufs = [ex[:, 10240 + i * 512:10240 + (i + 1) * 512].rearrange("p (q t) -> p q t", q=4) for i in range(3)]
        sout = [zf[:, 2048 + d * D:2048 + (d + 1) * D] for d in range(2)]
        split_r = [ex[0:32, 8192 + i * TOK:8192 + (i + 1) * TOK] for i in range(2)]
        mid = zf[0:32, 4096:4416].bitcast(BF16)
        zbuf = [btf[:, i * 512:(i + 1) * 512] for i in range(2)]
        junk_x = uf[:, 0:D]
        junk_y = btf[:, 1024:1280].bitcast(BF16)
        junk_1 = dts[:, :, :].rearrange("p a b -> p (a b)")[:, 0:D]
        junk_z = zf[:, 2 * D:3 * D]
        zero_i = xs[:, 1, 0:MAX_TILES].bitcast(I32)
        zero_f = xs[:, 0, :]
        MASK4 = maskb[:, :, :].unsqueeze(1).to_broadcast([P, 2, 2, P])

        def wbuf(i):
            return wbufs[i % 3]

        psb = [ctx.enter_context(nc.psum_tensor(f"bank{i}", [P, 512], F32)) for i in range(8)]

        s_const = sem("constants_loaded")
        s_x = sem("x_loaded")
        s_ring = [sem(f"ring_{i}_loaded") for i in range(RING)]
        s_adaw = [sem(f"ada_half_{i}_loaded") for i in range(2)]
        s_brow = sem("ada_bias_loaded")
        s_n2 = sem("norm2_row_loaded")
        s_ar = sem("ada_rows_product")
        s_arc = sem("ada_rows_on_chip")
        s_adr = sem("late_ada_rows_ready")
        s_ada = sem("ada_sums")
        s_accs = sem("ada_partial_sums")
        s_acc = sem("ada_half_summed")
        s_wo3 = sem("last_output_weights_loaded")
        s_yf = sem("gated_outputs_final")
        s_used = sem("ring_chunks_used")
        s_wdt = sem("dt_weights_loaded")
        s_inv = sem("inverse_counts_loaded")
        s_pw = sem("pool_weights_loaded")
        s_st0 = sem("initial_states_loaded")
        s_cast = sem("constants_cast")
        s_rs = sem("inverse_rms_ready")
        s_dve = sem("dve_steps")
        s_pool = sem("pool_steps")
        s_silc = sem("silu_c_ready")
        s_mod = sem("modulation_ready")
        s_ss = sem("x_squares_summed")
        s_xn = sem("x_normalised")
        s_xtr = sem("x_transposed")
        s_hs = sem("h_latents_ready")
        s_hc = sem("h_context_ready")
        s_dtp = sem("dt_product")
        s_soft = sem("softplus_handover")
        s_a = sem("decay_rates_ready")
        s_cum = sem("decay_sums")
        s_dif = sem("decay_exponents_ready")
        s_dec = sem("decays_ready")
        s_fm = sem("feature_tiles_projected")
        s_pad = sem("conv_inputs_copied")
        s_conv = sem("conv_summed")
        s_cs = sem("conv_activated")
        s_ttr = sem("conv_tiles_transposed")
        s_tok = sem("conv_tiles_token_major")
        s_vr = sem("v_copied")
        s_pu = sem("windows_pooled")
        s_z = sem("z_projected")
        s_zs = sem("z_activated")
        s_pm = sem("pool_products")
        s_u = sem("pool_scaled")
        s_tab = sem("decay_tables_summed")
        s_tabs = sem("decay_tables_split")
        s_g = sem("bc_products")
        s_gs = sem("bc_products_copied")
        s_xdd = sem("x_decayed")
        s_sp = sem("state_products")
        s_st = sem("states_ready")
        s_so = sem("context_states_copied")
        s_sout = sem("context_states_stored")
        s_xdt = sem("x_dt_ready")
        s_e = sem("exponents_built")
        s_ex = sem("decays_exponentiated")
        s_w = sem("scores_decayed")
        s_dg = sem("diagonal_products")
        s_off = sem("state_outputs")
        s_yc = sem("ssd_outputs_combined")
        s_ys = sem("ssd_squares_summed")
        s_yn = sem("ssd_outputs_normalised")
        s_ytr = sem("ssd_outputs_transposed")
        s_yT = sem("ssd_outputs_ready")
        s_ads = sem("ada_rows_stored")
        s_rowl = sem("ada_rows_loaded")
        s_row2 = sem("late_rows_loaded")
        s_xr = sem("x_reloaded")
        s_op = sem("output_products")
        s_x1 = sem("residual_ready")
        s_x1s = sem("residual_squares_summed")
        s_h2 = sem("h2_ready")
        s_h2s = [sem(f"h2_stored_{i}") for i in range(2)]
        s_h2t = sem("h2_transposed")
        s_h2T = sem("h2_feature_major")
        s_lg = sem("logits_ready")
        s_wr = sem("router_weights_loaded")
        s_lm = sem("logits_shifted")
        s_le = sem("logits_exponentiated")
        s_oh = sem("choices_ready")
        s_rk = sem("ranks_ready")
        s_rt = sem("routing_ready")
        s_zero = sem("slot_tokens_cleared")
        s_sc = sem("slot_tokens_scattered")
        s_w_in = [sem(f"expert_chunk_{c}_loaded") for c in range(6)]
        s_idx = sem("slot_tokens_loaded")
        s_xg = sem("tokens_gathered")
        s_begun = sem("gathers_begun")
        s_xtp = sem("gathered_transposed")
        s_xgT = sem("gathered_feature_major")
        s_gu = sem("gate_up_products")
        s_sg = sem("gates_activated")
        s_ac = sem("expert_activations")
        s_dn = sem("down_products")
        s_yo = sem("expert_outputs_copied")
        s_yst = sem("expert_outputs_stored")
        s_yg = [sem(f"expert_rows_gathered_{i}") for i in range(2)]
        s_fin = sem("final_sum_ready")
        s_fss = sem("final_squares_summed")
        s_fo = sem("final_output_ready")
        s_ost = [sem(f"outputs_stored_{i}") for i in range(2)]
        s_fn = sem("final_norm_loaded")

        x1 = xs
        wo = [ring[:, 2, :], ring[:, 0, :], ring[:, 1, :], ex[:, 0:CHUNK]]
        g1row = hf[:, 0:2 * D].rearrange("p (c d) -> p c d", c=2)
        a2row = hf[:, 2 * D:4 * D].rearrange("p (c d) -> p c d", c=2)
        h2buf0 = hf[:, 4 * D:5 * D]
        b2row = bf_[:, 0:2 * D].rearrange("p (c d) -> p c d", c=2)
        x1t = bf_[:, 2 * D:2 * D + 512]
        gtf = gT[:, :, :, :].rearrange("p j g n -> p (j g n)")
        h2buf1 = btf[:, 0:D]
        h2bufs = [h2buf0, h2buf1]
        h2T = gtf[:, 0:D].rearrange("p (k t) -> p k t", k=KT)
        xg = zf[:, 0:D]
        xgT = zf[:, D:2 * D].rearrange("p (k t) -> p k t", k=KT)
        aT = zf[:, 2 * D:2 * D + FT * P].rearrange("p (k t) -> p k t", k=FT)
        sg = [zf[:, 2560 + i * P:2560 + (i + 1) * P] for i in range(2)]
        yo = zf[:, 3072:3072 + D]
        g2row = uf[:, 0:2 * D].rearrange("p (c d) -> p c d", c=2)
        fnrow = uf[:, 2 * D:3 * D]
        fout = [uf[:, 3 * D + i * D:3 * D + (i + 1) * D] for i in range(2)]
        ygb = hf
        ri = sb("ri", [P, 64], I32)
        idx = sb("idx", [P, 2], I32)
        gate = sb("gate", [P, 2 * NJ])
        rw = ring[:, 2, :]
        n_sh, n_ex = rw[:, 0:80], rw[:, 80:160]
        onehotb = sb("onehotb", [P, NJ * E], BF16)

        block = ctx.enter_context(nc.Block())

        NCH = 14
        @block.sync
        def _(sp):
            sp.dma_start(cst[:], consts).then_inc(s_const, 16)
            sp.dma_start(bcst, bconsts).then_inc(s_const, 16)
            sp.dma_start(vec[:], vecs).then_inc(s_const, 16)
            sp.dma_start(row[:], rows.to_broadcast([P, R_ALL])).then_inc(s_const, 16)
            for j in range(NJ):
                sp.dma_start(xt[:, j, :], x[j * P:(j + 1) * P, :]).then_inc(s_x, 16)
            sp.dma_start(n2row, norm2).then_inc(s_n2, 16)
            sp.dma_start(invb, inv.to_broadcast([P, INV_ALL])).then_inc(s_inv, 16)

            def load_ring(n):
                if n >= RING:
                    sp.wait_ge(s_used, n - RING + 1)
                sp.dma_start(ring[:, n % RING, :], w_ring[n]).then_inc(s_ring[n % RING], 16)

            def load_ada(u):
                if u >= 2:
                    sp.wait_ge(s_acc, u - 1)
                sp.dma_start(adaw[u % 2], w_late[u].rearrange("p (k c) -> p k c", k=4)).then_inc(s_adaw[u % 2], 16)
                if u % 2 == 1 and u >= 3 or u == 0:
                    q = (u - 1) // 2 if u else 0
                    if q >= 1:
                        sp.wait_ge(s_adr, q)
                    else:
                        sp.wait_ge(s_ar, 1)
                    sp.dma_start(brow, b_late[q:q + 1, :]).then_inc(s_brow, 16)

            for n in range(4):
                load_ring(n)
            sp.dma_start(wdt, w_dt).then_inc(s_wdt, 16)
            for n in (4, 5, 6):
                load_ring(n)
            for u in range(10):
                load_ada(u)
            load_ring(7)
            for u in range(10, 16):
                load_ada(u)
            for n in range(8, NCH):
                load_ring(n)
            sp.wait_ge(s_off, 2 * (NJ - 1))
            sp.dma_start(wo[3], w_ring[NCH]).then_inc(s_wo3, 16)
            sp.wait_ge(s_dg, NJ * HG)
            sp.wait_ge(s_yc, 2 * NJ)
            for c in (2, 3, 4, 5, 0, 1):
                if c == 0:
                    sp.wait_ge(s_op, 2 * NJ)
                sp.dma_start(ex[:, c * 2048:(c + 1) * 2048], w_exp[0, c]).then_inc(s_w_in[c], 16)
            sp.wait_ge(s_rt, 1)
            k_tiles = sp.value_load(ri[0:1, 60:61], min_val=16, max_val=25)
            with sp.Fori(1, k_tiles) as i:
                e = sp.value_load(ri[0:1, bass.ds(i, 1)], min_val=0, max_val=E - 1)
                for c in range(6):
                    if c < FT:
                        sp.wait_ge(s_gu, i * FT + (c + 1 - FT))
                    else:
                        sp.wait_ge(s_dn, i * 2 + (c - FT + 1))
                    sp.dma_start(ex[:, c * 2048:(c + 1) * 2048], w_exp[e, c]).then_inc(s_w_in[c], 16)
            for j in range(NJ):
                sp.wait_ge(s_fo, j + 1)
                sp.dma_start(y_out[j * P:(j + 1) * P, :], fout[j % 2]).then_inc(s_ost[j % 2], 16)
            sp.wait_ge(s_ost[0], 48)
            sp.wait_ge(s_ost[1], 32)
            sp.wait_ge(s_sout, 32)

        @block.tensor
        def _(pe):
            pe.wait_ge(s_silc, 1)
            pe.wait_ge(s_const, 64)

            for n in range(4):
                pe.wait_ge(s_ring[n % RING], 16 * (n // RING + 1))
                w = ring[:, n % RING, :].rearrange("p (k c) -> p k c", k=KT)
                for k in range(KT):
                    mm = pe.matmul(psb[n][0:2, :], silc[:, 2 * k:2 * k + 2], w[:, k, :],
                                   start=(k == 0), stop=(k == KT - 1))
                mm.then_inc(s_used, 1)
            for m in range(16):
                if m % 4 == 0:
                    pe.wait_ge(s_arc, m // 4 + 1)
                mm = pe.transpose(psb[4][:, 2 * m:2 * m + 2], arow[:, m * P:(m + 1) * P], ident[0:2, 0:2])
            mm.then_inc(s_ar, 1)
            for j in range(NJ):
                pe.wait_ge(s_xn, j + 1)
            for k in range(KT):
                if k == 0:
                    pe.wait_ge(s_arc, 4)
                if k == 1:
                    pe.wait_ge(s_mod, 1)
                if k >= 3:
                    pe.wait_ge(s_hs, k - 2)
                    pe.wait_ge(s_hc, k - 2)
                q = 2 + 2 * (k % 3)
                for j in range(NJ):
                    o = psb[q + 1][:, 0:P] if j == 0 else psb[q][:, (j - 1) * P:j * P]
                    mm = pe.transpose(o, xt[:, j, k * P:(k + 1) * P], ident)
                mm.then_inc(s_xtr, 1)
            pe.wait_ge(s_hs, KT)
            pe.wait_ge(s_hc, KT)
            pe.wait_ge(s_wdt, 16)
            for j in range(NJ):
                for k in range(KT):
                    mm = pe.matmul(psb[1][:, j * 32:(j + 1) * 32], hT[:, k, j * P:(j + 1) * P],
                                   wdt[:, k * 32:(k + 1) * 32], start=(k == 0), stop=(k == KT - 1))
            mm.then_inc(s_dtp, 1)

            def turn_conv(t):
                f = t if t < 2 else t + 2
                pe.wait_ge(s_cs, f + 1)
                if t == 0:
                    pe.wait_ge(s_adr, 8)
                if t >= 1:
                    pe.wait_ge(s_tok, t)
                src = bcT[:, t, :] if t < 2 else xsT[t % 2]
                for j in range(NJ):
                    o = psb[1][:, 0:P] if j == 0 else psb[0][:, (j - 1) * P:j * P]
                    mm = pe.transpose(o, src[:, j * P:(j + 1) * P], ident)
                mm.then_inc(s_ttr, 1)

            for f in range(20):
                n = 4 + f // 4
                pe.wait_ge(s_ring[n % RING], 16 * (n // RING + 1))
                if f >= 3:
                    pe.wait_ge(s_vr if f - 3 < KT else s_pad, f - 2 if f - 3 < KT else f - 2 - KT)
                w = ring[:, n % RING, :].rearrange("p (k c) -> p k c", k=KT)
                q = 2 + 2 * (f % 3)
                for lo, hi, o in ((0, CTX, psb[q + 1][:, 0:CTX]), (CTX, TOK, psb[q][:, :])):
                    for k in range(KT):
                        mm = pe.matmul(o, w[:, k, (f % 4) * P:(f % 4 + 1) * P], hT[:, k, lo:hi],
                                       start=(k == 0), stop=(k == KT - 1))
                mm.then_inc(s_fm, 1)
                if f % 4 == 3:
                    pe.wait_ge(s_fm, f + 1)
                    pe.sem_inc(s_used, 1)
                if f == 1:
                    pe.wait_ge(s_a, 1)
                    for j in range(NJ):
                        for d, tri in ((0, trif), (1, trib)):
                            c = j * 32 + d * H
                            pe.matmul(psb[0][:, c:c + H], tri, a_[:, c:c + H], start=True, stop=True)
                    pe.matmul(psb[0][:, 160:320], ones, a_, start=True, stop=True).then_inc(s_cum, 1)
                    pe.wait_ge(s_dif, 1)
                if 1 <= f < 9:
                    q = f - 1
                    pe.wait_ge(s_acc, 2 * (q + 1))
                    if q >= 1:
                        pe.wait_ge(s_adr, q)
                    for c in range(2):
                        mm = pe.matmul(psb[c][0:1, :], ones[:, 0:1],
                                       acc[q % 2][:, c * 512:(c + 1) * 512], start=True, stop=True)
                    mm.then_inc(s_ada, 1)
                if f == 11:
                    turn_conv(0)
                elif 13 <= f:
                    turn_conv(f - 12)
            turn_conv(8)
            turn_conv(9)

            def project_z(jg, ks):
                j, g = jg // 2, jg % 2
                w = ring[:, g, :].rearrange("p (k c) -> p k c", k=KT)
                if ks[0] == 0 and jg < 2:
                    pe.wait_ge(s_ring[g], 16 * 4)
                if ks[0] == 0 and jg >= 1:
                    pe.wait_ge(s_zs, jg)
                for k in ks:
                    mm = pe.matmul(psb[6][:, :], hT[:, k, j * P:(j + 1) * P], w[:, k, :],
                                   start=(k == 0), stop=(k == KT - 1), skip_group_check=True)
                if ks[-1] == KT - 1:
                    mm.then_inc(s_z, 1)

            pe.wait_ge(s_pad, CONVF)
            for d, tri in ((0, trif), (1, trib)):
                q = 2 + 2 * d
                for j in range(NJ):
                    o = psb[q + 1][0:32, 0:P] if j == 0 else psb[q][0:32, (j - 1) * P:j * P]
                    mm = pe.matmul(o, a_[:, j * 32:(j + 1) * 32], tri, start=True, stop=True)
                mm.then_inc(s_tab, 1)
            for j in range(NJ):
                for g in range(2):
                    i = 2 * j + g
                    if i == 8:
                        pe.wait_ge(s_tok, 10)
                    o = psb[6 + i // 4][:, (i % 4) * P:(i % 4 + 1) * P] if i < 8 else \
                        psb[1][:, (i % 4) * P:(i % 4 + 1) * P]
                    mm = pe.matmul(o, bcT[:, g, j * P:(j + 1) * P], bcT[:, 2 + g, j * P:(j + 1) * P],
                                   start=True, stop=True)
            mm.then_inc(s_g, 1)
            pe.wait_ge(s_gs, 3)
            pe.wait_ge(s_tabs, 2)
            for n, (d, j) in enumerate(XDD_ORDER):
                pe.wait_ge(s_xdd, n + 1)
                if j == 0:
                    for i in range(8):
                        mm = pe.matmul(psb[2 + 2 * d + i // 4][:, (i % 4) * P:(i % 4 + 1) * P],
                                       xdd[:, n % 2, i * P:(i + 1) * P],
                                       btok[:, 0, (i // 4) * N:(i // 4 + 1) * N], start=True, stop=True)
                else:
                    if n >= 4:
                        pe.wait_ge(s_st, n - 3)
                    for g in range(2):
                        mm = pe.matmul(psb[(6, 0)[n % 2] + g][:, :], btok[:, j, g * N:(g + 1) * N],
                                       xdd[:, n % 2, g * 512:(g + 1) * 512], start=True, stop=True)
                mm.then_inc(s_sp, 1)
            pe.wait_ge(s_so, 4)
            pe.wait_ge(s_pw, 16)
            for g in range(4):
                pe.wait_ge(s_pu, 2 * (g + 1))
                for m in range(2):
                    i = 2 * g + m
                    if i >= 2:
                        pe.wait_ge(s_u, i - 1)
                    q = 2 + 2 * (i % 2)
                    for lo, hi, o in ((0, CTX, psb[q + 1][:, 0:CTX]), (CTX, TOK, psb[q][:, :])):
                        for kk in range(2):
                            mm = pe.matmul(o, gT_pw[:, g, kk, m * P:(m + 1) * P], uT[:, 2 * g + kk, lo:hi],
                                           start=(kk == 0), stop=(kk == 1))
                    mm.then_inc(s_pm, 1)
            pe.wait_ge(s_st, 6)
            pe.wait_ge(s_u, 8)
            project_z(0, range(KT))

            def exponents(i):
                j, hh = i // HG, 2 * (i % HG)
                o = psb[4 + i % 2]
                if i >= 2:
                    pe.wait_ge(s_ex, i - 1)
                pe.matmul(o[:, :], idb[:, :], MASK4, start=True, stop=False, skip_group_check=True)
                for q in range(4):
                    h, d = hh + q // 2, q % 2
                    c = d * H + h
                    mm = pe.matmul(o[:, q * P:(q + 1) * P], stackb[:, c:c + 1].to_broadcast([96, P]),
                                   tabT[d][:, j * P:(j + 1) * P], start=False, stop=True,
                                   skip_group_check=True)
                mm.then_inc(s_e, 1)

            def diagonal(i):
                j, hh = i // HG, 2 * (i % HG)
                jg = 2 * j + hh // HG
                pe.wait_ge(s_w, i + 1)
                if hh == 0:
                    pe.wait_ge(s_xdt, j + 1)
                if hh % HG == 0 and jg >= 2:
                    pe.wait_ge(s_yc, jg - 1)
                for q in range(2):
                    h = hh + q
                    for d in range(2):
                        mm = pe.matmul(psb[jg % 2][:, (h % HG) * HD:(h % HG + 1) * HD],
                                       wbuf(i)[:, 2 * q + d, :], xdt[:, d, h * HD:(h + 1) * HD],
                                       start=(d == 0), stop=(d == 1))
                mm.then_inc(s_dg, 1)

            def from_states(jg):
                j, g = jg // 2, jg % 2
                if jg >= 3:
                    pe.wait_ge(s_yc, jg)
                for d in range(2):
                    si = j - 1 if d == 0 else 4 + j - 1
                    mm = pe.matmul(psb[2 + d][:, :], bcT[:, 2 + g, j * P:(j + 1) * P],
                                   st[:, si, g * 512:(g + 1) * 512], start=True, stop=True)
                mm.then_inc(s_off, 1)

            def turn_y(j):
                pe.wait_ge(s_yn, j + 1)
                for hf_ in range(2):
                    if 2 * j + hf_ >= 1:
                        pe.wait_ge(s_yT, 2 * j + hf_)
                    for q in range(4):
                        k = 4 * hf_ + q
                        mm = pe.transpose(psb[7][:, q * P:(q + 1) * P], xs[:, j, k * P:(k + 1) * P], ident)
                    mm.then_inc(s_ytr, 1)

            NS = NJ * HG
            for i in range(NS + 2):
                if i < NS:
                    exponents(i)
                    if i % 4 and i // 4 + 1 < 2 * NJ:
                        project_z(i // 4 + 1, ((), range(0, 3), range(3, 6), range(6, 8))[i % 4])
                        if i // 4 + 1 == 2 * NJ - 1 and i % 4 == 3:
                            pe.wait_ge(s_z, 2 * NJ)
                            pe.sem_inc(s_used, 2)
                if i >= 2:
                    k = i - 2
                    diagonal(k)
                    if k % 4 == 3 and k // 4 >= 2:
                        from_states(k // 4)
                    if k % HG == 5 and k // HG >= 1:
                        turn_y(k // HG - 1)
            turn_y(NJ - 1)

            pe.wait_ge(s_yT, 2 * NJ)
            pe.wait_ge(s_yc, 2 * NJ)
            pe.wait_ge(s_wr, 16)

            def project_out(j):
                for hf_ in range(2):
                    if j >= 2:
                        pe.wait_ge(s_x1, 2 * (j - 2) + hf_ + 1)
                    for c in range(2):
                        n = 2 * hf_ + c
                        if j == 0:
                            if n == 3:
                                pe.wait_ge(s_wo3, 16)
                            else:
                                pe.wait_ge(s_ring[(11 + n) % RING], 16 * ((11 + n) // RING + 1))
                        w = wo[n].rearrange("p (k c) -> p k c", k=KT)
                        src = yT if c == 0 else uT
                        for k in range(KT):
                            mm = pe.matmul(psb[(2 * j + hf_) % 4][:, :], src[:, k, j * P:(j + 1) * P], w[:, k, :],
                                           start=(c == 0 and k == 0), stop=(c == 1 and k == KT - 1))
                    mm.then_inc(s_op, 1)

            def turn_h2(j):
                pe.wait_ge(s_h2, j + 1)
                if j >= 1:
                    pe.wait_ge(s_h2T, 2 * j)
                for k in range(KT):
                    mm = pe.transpose(psb[4 + k // 4][:, (k % 4) * P:(k % 4 + 1) * P],
                                      h2bufs[j % 2][:, k * P:(k + 1) * P], ident)
                mm.then_inc(s_h2t, 1)

            def router(j):
                pe.wait_ge(s_h2T, 2 * (j + 1))
                for k in range(KT):
                    mm = pe.matmul(psb[6][:, j * E:(j + 1) * E], h2T[:, k, :], wrt[:, k, :],
                                   start=(k == 0), stop=(k == KT - 1))
                mm.then_inc(s_lg, 1)

            for j in range(NJ + 2):
                if j < NJ:
                    project_out(j)
                if j >= 2:
                    router(j - 2)
                if 1 <= j <= NJ:
                    turn_h2(j - 1)
            pe.wait_ge(s_oh, 1)
            for j in range(NJ):
                for i in range(j + 1):
                    pe.matmul(psb[7][:, j * E:(j + 1) * E], strictb[:, :] if i == j else onesb[:, :],
                              onehotb[:, i * E:(i + 1) * E], start=(i == 0), stop=(i == j))
            for i in range(NJ):
                mm = pe.matmul(psb[7][:, NJ * E:(NJ + 1) * E], onesb[:, :], onehotb[:, i * E:(i + 1) * E],
                               start=(i == 0), stop=(i == NJ - 1))
            mm.then_inc(s_rk, 1)

            pe.wait_ge(s_rt, 1)
            k_tiles = pe.value_load(ri[0:1, 60:61], min_val=16, max_val=25)

            def turn_tokens():
                for k in range(KT):
                    mm = pe.transpose(psb[2 + k // 4][:, (k % 4) * P:(k % 4 + 1) * P],
                                      xg[:, k * P:(k + 1) * P], ident)
                mm.then_inc(s_xtp, 1)

            pe.wait_ge(s_xg, 16)
            turn_tokens()
            pe.sem_inc(s_dn, 2)
            with pe.Fori(0, k_tiles) as i:
                pe.wait_ge(s_xgT, i * 2 + 2)
                for c in range(FT):
                    pe.wait_ge(s_w_in[c], i * 16 + 16)
                    pe.wait_ge(s_ac, i * FT + (c + 1))
                    w = ex[:, c * 2048:(c + 1) * 2048].rearrange("p (a k f) -> p a k f", a=2, k=KT)
                    for a in range(2):
                        for k in range(KT):
                            mm = pe.matmul(psb[c % 2][:, a * P:(a + 1) * P], w[:, a, k, :], xgT[:, k, :],
                                           start=(k == 0), stop=(k == KT - 1))
                    mm.then_inc(s_gu, 1)
                pe.wait_ge(s_xg, i * 16 + 32)
                turn_tokens()
                pe.wait_ge(s_ac, i * FT + (FT + 2))
                pe.wait_ge(s_yo, i * 2 + 2)
                for c in range(2):
                    pe.wait_ge(s_w_in[FT + c], i * 16 + 16)
                    w = ex[:, (FT + c) * 2048:(FT + c + 1) * 2048].rearrange("p (k d) -> p k d", k=2)
                    for k in range(2):
                        for hf_ in range(2):
                            mm = pe.matmul(psb[6 + hf_][:, :], aT[:, 2 * c + k, :],
                                           w[:, k, hf_ * 512:(hf_ + 1) * 512],
                                           start=(c == 0 and k == 0), stop=(c == 1 and k == 1),
                                           skip_group_check=True)
                    mm.then_inc(s_dn, 1)

        @block.scalar
        def _(act):
            def inverse_rms(col, n=1):
                r = stat[:, col:col + n]
                act.activation(r, r, ACT.Ln, scale=1.0 / D, bias=eps_col[:, :]).then_inc(s_rs, 1)
                rs_steps[0] += 2
                act.wait_ge(s_rs, rs_steps[0] - 1)
                act.activation(r, r, ACT.Exp, scale=-0.5).then_inc(s_rs, 1)

            rs_steps = [0]
            act.wait_ge(s_const, 64)
            act.activation(silc[:, :], vec[:, V_C:V_C + 16], ACT.Silu).then_inc(s_silc, 1)
            act.activation(nega[:, :], row[:, R_ALOG:R_ALOG + 32], ACT.Exp).then_inc(s_soft, 1)
            for j in range(NJ):
                act.wait_ge(s_x, 16 * NJ)
                act.activation(junk_x, xt[:, j, :], ACT.Square, accum_out=stat[:, j:j + 1]).then_inc(s_ss, 1)
                act.wait_ge(s_ss, j + 1)
            act.wait_ge(s_cast, 1)
            inverse_rms(0, NJ)
            for n in range(4):
                act.wait_ge(s_used, n + 1)
                act.activation(arow[:, n * 512:(n + 1) * 512], psb[n][0:2, :], ACT.Copy).then_inc(s_arc, 1)
            act.wait_ge(s_mod, 1)
            act.wait_ge(s_cast, 1)
            for k in range(KT):
                act.wait_ge(s_xtr, k + 1)
                act.activation(hT[:, k, CTX:TOK], psb[2 + 2 * (k % 3)][:, :], ACT.Identity,
                               bias=modB[:, 2 * k + 1:2 * k + 2], scale=modA[:, 2 * k + 1:2 * k + 2]).then_inc(s_hs, 1)
            act.wait_ge(s_soft, 2)
            act.activation(sc1, sc0, ACT.Exp, scale=-1.0).then_inc(s_soft, 1)
            act.wait_ge(s_soft, 4)
            act.activation(ncum, etot, ACT.Ln).then_inc(s_soft, 1)

            def silu_conv(f):
                act.wait_ge(s_conv, f + 1)
                t = f if f < 2 else f - 2
                dst = bcT[:, f, :] if f < 4 else xsT[t % 2]
                if f >= 6:
                    act.wait_ge(s_ttr, t - 1)
                act.activation(dst[:, 0:CTX], cacc[f % 2][:, 0:CTX], ACT.Silu, bias=vec[:, V_CB + f:V_CB + f + 1])
                act.activation(dst[:, CTX:TOK], cacc[f % 2][:, 131:643], ACT.Silu,
                               bias=vec[:, V_CB + f:V_CB + f + 1]).then_inc(s_cs, 1)

            def store_ada(q):
                act.wait_ge(s_adr, q + 1)
                for c in range(2):
                    act.dma_start(ada_rows[q // 2, c:c + 1, (q % 2) * 512:(q % 2 + 1) * 512],
                                  orow[:, c * 512:(c + 1) * 512]).then_inc(s_ads, 16)

            for f in range(20):
                if 2 <= f < 10:
                    store_ada(f - 2)
                act.wait_ge(s_fm, f + 1)
                q = 2 + 2 * (f % 3)
                if f < KT:
                    act.activation(uT[:, f, 0:CTX], psb[q + 1][:, 0:CTX], ACT.Copy)
                    act.activation(uT[:, f, CTX:TOK], psb[q][:, :], ACT.Copy).then_inc(s_vr, 1)
                else:
                    g = f - KT
                    if g == 0:
                        act.wait_ge(s_cast, 2)
                    if g >= 2:
                        act.wait_ge(s_conv, g - 1)
                    act.activation(xpad[g % 2][:, 1:1 + CTX], psb[q + 1][:, 0:CTX], ACT.Copy)
                    act.activation(xpad[g % 2][:, 132:132 + LAT], psb[q][:, :], ACT.Copy).then_inc(s_pad, 1)
                if f == 2:
                    act.wait_ge(s_dif, 1)
                    act.activation(ecum, ncum, ACT.Exp, scale=-1.0)
                    act.activation(dec, sc0, ACT.Exp)
                    act.activation(etot, sc1, ACT.Exp).then_inc(s_dec, 1)
                if f > KT:
                    silu_conv(f - 1 - KT)
            silu_conv(CONVF - 1)
            act.wait_ge(s_tok, 10)
            act.wait_ge(s_ads, 256)
            for d in range(2):
                act.dma_start(st[:, 0 if d == 0 else 7, :], states0[d]).then_inc(s_st0, 16)
            act.wait_ge(s_g, 1)
            gv = gT[:, :, :, :].rearrange("p j g n -> p (j g n)")
            act.activation(gv[:, 0:512], psb[6][:, :], ACT.Copy).then_inc(s_gs, 1)
            act.activation(gv[:, 512:1024], psb[7][:, :], ACT.Copy).then_inc(s_gs, 1)
            act.activation(gv[:, 1024:1280], psb[1][:, 0:256], ACT.Copy).then_inc(s_gs, 1)
            for n, (d, j) in enumerate(XDD_ORDER):
                if j == 0:
                    act.wait_ge(s_sp, n + 1)
                    for i in range(2):
                        act.activation(sout[d][:, i * 512:(i + 1) * 512], psb[2 + 2 * d + i][:, :],
                                       ACT.Copy).then_inc(s_so, 1)
                    act.wait_ge(s_so, 2 * (d + 1))
                    act.dma_start(s_out[d].rearrange("(i p) n -> p i n", p=P), sout[d].rearrange("p (i n) -> p i n", n=N)).then_inc(s_sout, 16)

            for i in range(8):
                act.wait_ge(s_pm, 2 * (i // 2 + 1))
                q = 2 + 2 * (i % 2)
                act.activation(uT[:, i, 0:CTX], psb[q + 1][:, 0:CTX], ACT.Copy, scale=vec[:, V_PS + i:V_PS + i + 1])
                act.activation(uT[:, i, CTX:TOK], psb[q][:, :], ACT.Copy,
                               scale=vec[:, V_PS + i:V_PS + i + 1]).then_inc(s_u, 1)

            def silu_z(jg):
                act.wait_ge(s_z, jg + 1)
                if jg >= 2:
                    act.wait_ge(s_yc, jg - 1)
                act.activation(zbuf[jg % 2], psb[6][:, :], ACT.Silu).then_inc(s_zs, 1)

            def exps(i):
                j, hh = i // HG, 2 * (i % HG)
                act.wait_ge(s_e, i + 1)
                if i >= 3:
                    act.wait_ge(s_dg, i - 2)
                for q in range(4):
                    c = j * 32 + (q % 2) * H + hh + q // 2
                    mm = act.activation(wbuf(i)[:, q, :], psb[4 + i % 2][:, q * P:(q + 1) * P], ACT.Exp,
                                        bias=ncum[:, c:c + 1])
                mm.then_inc(s_ex, 1)

            def square_y(j):
                act.wait_ge(s_yc, 2 * (j + 1))
                for g in range(2):
                    n = 3 * j + g
                    act.activation(junk_y, xs[:, j, g * 512:(g + 1) * 512], ACT.Square,
                                   accum_out=stat[:, 16 + 2 * j + g:17 + 2 * j + g]).then_inc(s_ys, 1)
                    act.wait_ge(s_ys, n + 1)
                act.activation(stat[:, 5 + j:6 + j], stat[:, 16 + 2 * j:17 + 2 * j], ACT.Identity,
                               bias=stat[:, 17 + 2 * j:18 + 2 * j]).then_inc(s_ys, 1)
                act.wait_ge(s_ys, 3 * j + 3)
                inverse_rms(5 + j)

            def copy_y(j):
                if j == 0:
                    act.wait_ge(s_sout, 32)
                for hf_ in range(2):
                    act.wait_ge(s_ytr, 2 * j + hf_ + 1)
                    for q in range(4):
                        k = 4 * hf_ + q
                        mm = act.activation(yT[:, k, j * P:(j + 1) * P], psb[7][:, q * P:(q + 1) * P],
                                            ACT.Copy, scale=vec[:, V_SN + k:V_SN + k + 1])
                    mm.then_inc(s_yT, 1)

            for i in range(NJ * HG):
                exps(i)
                if i % 4 == 0:
                    silu_z(i // 4)
                if i % HG == 3 and i >= HG:
                    square_y(i // HG - 1)
                if i % HG == HG - 1 and i >= 2 * HG - 1:
                    copy_y(i // HG - 1)
            square_y(NJ - 1)
            copy_y(NJ - 1)

            act.wait_ge(s_z, 2 * NJ)
            act.dma_start(g1row, ada_rows[0:1].to_broadcast([P, 2, D])).then_inc(s_rowl, 16)
            act.dma_start(a2row, ada_rows[2:3].to_broadcast([P, 2, D])).then_inc(s_rowl, 16)
            act.dma_start(wrt[:, :, :], w_router.rearrange("p (k e) -> p k e", k=KT)).then_inc(s_wr, 16)
            act.wait_ge(s_ytr, 2 * NJ)
            for j in range(NJ):
                act.dma_start(x1[:, j, :], x[j * P:(j + 1) * P, :]).then_inc(s_xr, 16)
            act.wait_ge(s_yc, 2 * NJ)
            act.dma_start(b2row, ada_rows[1:2].to_broadcast([P, 2, D])).then_inc(s_row2, 16)

            def copy_h2(j):
                act.wait_ge(s_h2t, j + 1)
                if j >= 1:
                    act.wait_ge(s_lg, j)
                act.activation(h2T[:, 0:4, :], psb[4][:, :].rearrange("p (k t) -> p k t", k=4),
                               ACT.Copy).then_inc(s_h2T, 1)
                act.dma_start(h2_dram[j * P:(j + 1) * P, :], h2bufs[j % 2]).then_inc(s_h2s[j % 2], 16)

            for j in range(NJ):
                if j >= 1:
                    copy_h2(j - 1)
                act.wait_ge(s_x1, 2 * (j + 1))
                act.activation(junk_1, x1[:, j, :], ACT.Square, accum_out=stat[:, 10 + j:11 + j]).then_inc(s_x1s, 1)
                act.wait_ge(s_x1s, j + 1)
                inverse_rms(10 + j)
            copy_h2(NJ - 1)
            act.dma_start(g2row, ada_rows[3:4].to_broadcast([P, 2, D])).then_inc(s_row2, 16)
            act.dma_start(fnrow, fnorm.to_broadcast([P, D])).then_inc(s_fn, 16)
            act.wait_ge(s_lm, 1)
            act.activation(n_ex, n_sh, ACT.Exp).then_inc(s_le, 1)

            act.wait_ge(s_rt, 1)
            k_tiles = act.value_load(ri[0:1, 60:61], min_val=16, max_val=25)

            def copy_tokens(n):
                act.wait_ge(s_xtp, n)
                act.activation(xgT[:, 0:4, :], psb[2][:, :].rearrange("p (k t) -> p k t", k=4),
                               ACT.Copy).then_inc(s_xgT, 1)

            copy_tokens(1)
            act.sem_inc(s_yo, 2)
            act.sem_inc(s_yst, 16)
            with act.Fori(0, k_tiles) as i:
                for c in range(FT):
                    act.wait_ge(s_gu, i * FT + (c + 1))
                    act.wait_ge(s_ac, i * FT + (c + 1))
                    act.activation(sg[c % 2], psb[c % 2][:, 0:P], ACT.Silu).then_inc(s_sg, 1)
                copy_tokens(i + 2)
                act.wait_ge(s_dn, i * 2 + 4)
                act.wait_ge(s_yst, i * 16 + 16)
                act.activation(yo[:, 0:512], psb[6][:, :], ACT.Copy).then_inc(s_yo, 1)
                act.wait_ge(s_yo, i * 2 + 4)
                act.dma_start(slot_out[bass.ds(i * P, P), :], yo).then_inc(s_yst, 16)
            act.wait_ge(s_yst, k_tiles * 16 + 16)
            for j in range(NJ):
                act.wait_ge(s_fin, j + 1)
                act.activation(junk_z, x1[:, j, :], ACT.Square, accum_out=stat[:, j:j + 1]).then_inc(s_fss, 1)
                act.wait_ge(s_fss, j + 1)
                inverse_rms(j)

        @block.gpsimd
        def _(pool):
            step = Steps(pool, s_pool)
            pool.wait_ge(s_const, 64)
            pool.tensor_copy(idb[:, :], ident)
            pool.tensor_copy(maskb[:, :, :], bcst[:, B_MASK:B_MASK + 256].rearrange("p (a b) -> p a b", a=2))
            pool.tensor_copy(strictb[:, :], bcst[:, B_STRICT:B_STRICT + P])
            pool.tensor_copy(onesb[:, :], ones)
            pool.tensor_copy(stackb[:, :], bcst[0:96, B_STACK:B_STACK + 32])
            pool.memset(zero_i, 0)
            pool.memset(zero_f, 0.0)
            pool.memset(eps_col[:, :], EPS)
            pool.tensor_tensor(dsum[:, :], row[:, R_DSK:R_DSK + H], row[:, R_DSK + H:R_DSK + 2 * H],
                               ALU.add).then_inc(s_cast, 1)
            pool.wait_ge(s_hs, KT)
            pool.wait_ge(s_hc, KT)
            pool.memset(xpad[0], 0.0)
            pool.memset(xpad[1], 0.0).then_inc(s_cast, 1)
            pool.wait_ge(s_cast, 1)
            pool.dma_start(slot_token.rearrange("(p c) o -> p (c o)", p=P), zero_i).then_inc(s_zero, 16)
            for t in range(E, MAX_TILES - 1):
                pool.dma_start(slot_out[t * P:(t + 1) * P, :], zero_f).then_inc(s_zero, 16)

            pool.wait_ge(s_inv, 16)
            iv = [(invb[:, g * TOK:g * TOK + CTX], invb[:, g * TOK + CTX:(g + 1) * TOK]) for g in range(4)]
            for f in range(8):
                g = f // 2
                w = WINDOWS[g]
                lw = g + 1
                v = uT[:, f, :]
                pool.wait_ge(s_vr, f + 1)
                L = CTX + w - 1
                step(pool.memset(pa[:, 0:L], 0.0))
                step(pool.tensor_copy(pa[:, w // 2:w // 2 + CTX], v[:, 0:CTX]))
                src, dst = pa, pb_
                for q in range(lw):
                    L -= 1 << q
                    step(pool.tensor_tensor(dst[:, 0:L], src[:, 0:L], src[:, (1 << q):(1 << q) + L], ALU.add))
                    src, dst = dst, (pc if dst is pb_ else pb_)
                step(pool.tensor_tensor(dst[:, 0:CTX], src[:, 0:CTX], iv[g][0], ALU.mult))
                step(pool.tensor_tensor(uT[:, f, 0:CTX], dst[:, 0:CTX], v[:, 0:CTX], ALU.subtract))
                L = GRID_W + w - 1

                def grid(b, n, ww=None):
                    ww = ww or L0
                    return b[:, 0:n * ww].rearrange("p (r c) -> p r c", r=n)

                L0 = L
                vg = v[:, CTX:TOK].rearrange("p (r c) -> p r c", r=ROWS)
                step(pool.memset(pa[:, 0:ROWS * L0], 0.0))
                step(pool.tensor_copy(grid(pa, ROWS)[:, :, w // 2:w // 2 + GRID_W], vg))
                src, dst = pa, pb_
                for q in range(lw):
                    L -= 1 << q
                    s3, d3 = grid(src, ROWS), grid(dst, ROWS)
                    step(pool.tensor_tensor(d3[:, :, 0:L], s3[:, :, 0:L], s3[:, :, (1 << q):(1 << q) + L], ALU.add))
                    src, dst = dst, (pc if dst is pb_ else pb_)
                col = grid(src, ROWS)[:, :, 0:GRID_W]
                if w // 2 >= ROWS:
                    n = ROWS // 2
                    s3 = col
                    while n:
                        d3 = grid(dst, n, GRID_W)
                        step(pool.tensor_tensor(d3, s3[:, 0:n, :], s3[:, n:2 * n, :], ALU.add))
                        s3 = d3
                        src, dst = dst, (pc if dst is pb_ else pb_)
                        n //= 2
                    total = s3.to_broadcast([P, ROWS, GRID_W])
                else:
                    n = ROWS + w - 1
                    step(pool.memset(pa[:, 0:n * GRID_W], 0.0))
                    step(pool.tensor_copy(grid(pa, n, GRID_W)[:, w // 2:w // 2 + ROWS, :], col))
                    src, dst = pa, pb_
                    for q in range(lw):
                        n -= 1 << q
                        s1, d1 = src[:, 0:(n + (1 << q)) * GRID_W], dst[:, 0:n * GRID_W]
                        step(pool.tensor_tensor(d1, s1[:, 0:n * GRID_W], s1[:, (1 << q) * GRID_W:], ALU.add))
                        src, dst = dst, (pc if dst is pb_ else pb_)
                    total = grid(src, ROWS, GRID_W)
                m3 = grid(dst, ROWS, GRID_W)
                step(pool.tensor_tensor(m3, total, iv[g][1].rearrange("p (r c) -> p r c", r=ROWS), ALU.mult))
                pool.tensor_tensor(uT[:, f, CTX:TOK].rearrange("p (r c) -> p r c", r=ROWS), m3, vg,
                                   ALU.subtract).then_inc(s_pu, 1)
                pool.wait_ge(s_pu, f + 1)
            pool.wait_ge(s_adr, 8)
            pool.dma_start(gT_pw, w_pool.rearrange("p (g k m) -> p g k m", g=4, k=2)).then_inc(s_pw, 16)

            pool.wait_ge(s_rt, 1)
            for a in range(2):
                for j in range(NJ):
                    c = a * NJ + j
                    pool.indirect_dma_start(slot_token, bass.IndirectOffsetOnAxis(ap=ri[:, 40 + c:41 + c], axis=0),
                                            ri[:, 32 + j:33 + j], None, bounds_check=SLOTS - 1,
                                            oob_is_err=False).then_inc(s_sc, 16)
            pool.wait_ge(s_sc, 160)
            k_tiles = pool.value_load(ri[0:1, 60:61], min_val=16, max_val=25)

            def gather(i, before):
                if before is not None:
                    pool.wait_ge(s_xg, before * 16 + 16)
                pool.dma_start(idx[:, 0:1], slot_token[bass.ds(i * P, P), :] if before is not None
                               else slot_token[0:P, :]).then_inc(s_idx, 16)
                pool.wait_ge(s_idx, 16 if before is None else before * 16 + 32)
                if before is not None:
                    pool.wait_ge(s_xtp, before + 1)
                pool.wait_ge(s_h2s[0], 48)
                pool.wait_ge(s_h2s[1], 32)
                pool.sem_inc(s_begun, 1)
                pool.indirect_dma_start(xg, None, h2_dram,
                                        bass.IndirectOffsetOnAxis(ap=idx[:, 0:1], axis=0),
                                        bounds_check=TOK - 1, oob_is_err=False).then_inc(s_xg, 16)

            gather(0, None)
            with pool.Fori(0, k_tiles) as i:
                gather(i + 1, i)
            pool.wait_ge(s_yst, k_tiles * 16 + 16)
            pool.sem_inc(s_begun, 1)
            pool.wait_ge(s_zero, 16 * (MAX_TILES - E))
            for j in range(NJ):
                if j >= 2:
                    pool.wait_ge(s_fin, j - 1)
                for a in range(2):
                    n = 2 * j + a
                    pool.indirect_dma_start(ygb[:, (n % 4) * D:(n % 4 + 1) * D], None, slot_out,
                                            bass.IndirectOffsetOnAxis(ap=ri[:, 40 + a * NJ + j:41 + a * NJ + j], axis=0),
                                            bounds_check=SLOTS - P - 1, oob_is_err=False).then_inc(s_yg[j % 2], 16)

        @block.vector
        def _(dve):
            step = Steps(dve, s_dve)
            tt, ts, stt = dve.tensor_tensor, dve.tensor_scalar, dve.scalar_tensor_tensor
            dve.wait_ge(s_const, 64)
            dve.wait_ge(s_rs, 2 * (1))
            for j in range(NJ):
                ts(xt[:, j, :], xt[:, j, :], stat[:, j:j + 1], None, ALU.mult).then_inc(s_xn, 1)
            dve.wait_ge(s_ar, 1)
            tt(modB[:, :], psb[4][:, 0:16], vec[:, V_ADA:V_ADA + 16], ALU.add)
            step(tt(modA[:, :], psb[4][:, 16:32], vec[:, V_ADA + 16:V_ADA + 32], ALU.add))
            stt(modA[:, :], modA[:, :], 1.0, vec[:, V_N1:V_N1 + 16], ALU.add, ALU.mult).then_inc(s_mod, 1)
            dve.wait_ge(s_mod, 1)
            for k in range(KT):
                dve.wait_ge(s_xtr, k + 1)
                ts(hT[:, k, 0:CTX], psb[3 + 2 * (k % 3)][:, 0:CTX], modA[:, 2 * k:2 * k + 1], modB[:, 2 * k:2 * k + 1],
                   ALU.mult, ALU.add).then_inc(s_hc, 1)
            dve.wait_ge(s_dtp, 1)
            step(tt(dt_.rearrange("p (j h) -> p j h", j=NJ), psb[1][:, 0:160].rearrange("p (j h) -> p j h", j=NJ),
                    row[:, R_DTB:R_DTB + 32].unsqueeze(1).to_broadcast([P, NJ, 32]), ALU.add))
            dve.wait_ge(s_soft, 1)
            step(ts(sc0, dt_, -1.0, None, ALU.mult))
            tt(sc0, sc0, dt_, ALU.max).then_inc(s_soft, 1)
            dve.wait_ge(s_soft, 2)
            step(ts(dt_, dt_, 0.0, None, ALU.max))
            dve.wait_ge(s_soft, 3)
            ts(etot, sc1, 1.0, None, ALU.add).then_inc(s_soft, 1)
            dve.wait_ge(s_soft, 4)
            step(ts(sc0, etot, -1.0, None, ALU.add))
            step(tt(sc0, sc1, sc0, ALU.subtract))
            step(dve.reciprocal(sc1, etot))
            step(tt(sc0, sc0, sc1, ALU.mult))
            dve.wait_ge(s_soft, 5)
            step(tt(sc0, sc0, ncum, ALU.add))
            step(tt(dt_, dt_, sc0, ALU.add))
            step(tt(a_.rearrange("p (j h) -> p j h", j=NJ), dt_.rearrange("p (j h) -> p j h", j=NJ),
                    nega[:, :].unsqueeze(1).to_broadcast([P, NJ, 32]), ALU.mult))
            ts(a_, a_, -1.0, None, ALU.mult).then_inc(s_a, 1)
            def ada_half(u):
                q = u // 2
                if u % 2 == 0 and q >= 2:
                    dve.wait_ge(s_ada, q - 1)
                dve.wait_ge(s_adaw[u % 2], 16 * (u // 2 + 1))
                for kk in range(4):
                    k = 4 * (u % 2) + kk
                    for c in range(2):
                        a = acc[q % 2][:, c * 512:(c + 1) * 512]
                        w, s_c = adaw[u % 2][:, kk, :], silc[:, 2 * k + c:2 * k + c + 1]
                        if k:
                            dve.wait_ge(s_accs, 16 * q + 2 * k + c - 1)
                            ins = stt(a, w, s_c, a, ALU.mult, ALU.add)
                        else:
                            ins = ts(a, w, s_c, None, ALU.mult)
                        ins.then_inc(s_accs, 1)
                dve.wait_ge(s_accs, 16 * q + 8 * (u % 2) + 8)
                dve.sem_inc(s_acc, 1)

            def ada_rows_out(q):
                dve.wait_ge(s_ada, q + 1)
                dve.wait_ge(s_brow, 16 * (q + 1))
                if q >= 1:
                    dve.wait_ge(s_ads, 32 * q)
                for c in range(2):
                    o = orow[:, c * 512:(c + 1) * 512]
                    ins = tt(o, psb[c][0:1, :], brow, ALU.add)
                    if q // 2 == 2:
                        step(ins)
                        dve.wait_ge(s_n2, 16)
                        ins = stt(o, o, 1.0, n2row[:, (q % 2) * 512:(q % 2 + 1) * 512], ALU.add, ALU.mult)
                ins.then_inc(s_adr, 1)

            dve.wait_ge(s_silc, 1)
            ada_half(0)
            ada_half(1)
            dve.wait_ge(s_cum, 1)
            step(ts(ncum, psb[0][:, 0:160], -1.0, None, ALU.mult))
            tt(sc0, psb[0][:, 160:320], ncum, ALU.add)
            dve.tensor_copy(sc1, psb[0][:, 160:320]).then_inc(s_dif, 1)

            for q in range(1, 8):
                ada_half(2 * q)
                ada_half(2 * q + 1)
                ada_rows_out(q - 1)
            ada_rows_out(7)

            dve.wait_ge(s_zero, 16 * (MAX_TILES - E))

            def token_major(t):
                dve.wait_ge(s_ttr, t + 1)
                dst = btok[:, :, t * N:(t + 1) * N] if t < 2 else xs[:, :, (t - 2) * P:(t - 1) * P]
                dve.tensor_copy(dst[:, 0, :], psb[1][:, 0:P])
                dve.tensor_copy(dst[:, 1:NJ, :], psb[0][:, :].rearrange("p (j n) -> p j n", n=P)).then_inc(s_tok, 1)

            for f in range(CONVF):
                dve.wait_ge(s_pad, f + 1)
                if f >= 2:
                    dve.wait_ge(s_cs, f - 1)
                for q in range(4):
                    wq = vec[:, V_CW + 4 * f + q:V_CW + 4 * f + q + 1]
                    if q == 0:
                        step(ts(cacc[f % 2], xpad[f % 2][:, 0:643], wq, None, ALU.mult))
                    else:
                        ins = stt(cacc[f % 2], xpad[f % 2][:, q:q + 643], wq, cacc[f % 2], ALU.mult, ALU.add)
                        if q < 3:
                            step(ins)
                        else:
                            ins.then_inc(s_conv, 1)
                if f == 4:
                    token_major(0)
                if f >= 5:
                    token_major(f - 4)
            token_major(8)
            token_major(9)
            for d in range(2):
                dve.wait_ge(s_tab, d + 1)
                dve.wait_ge(s_g, 1)
                t = tabT[d]
                for lo, hi, src in ((0, CTX, psb[3 + 2 * d][0:32, 0:CTX]), (CTX, TOK, psb[2 + 2 * d][0:32, :])):
                    if d == 0 and lo == 0:
                        dve.wait_ge(s_ads, 256)
                    r1, r2 = split_r[0][:, lo:hi], split_r[1][:, lo:hi]
                    step(dve.tensor_copy(t[0:32, lo:hi], src))
                    step(tt(r1, src, t[0:32, lo:hi], ALU.subtract))
                    step(dve.tensor_copy(mid[:, lo:hi], r1))
                    step(dve.tensor_copy(t[32:64, lo:hi], mid[:, lo:hi]))
                    step(tt(r2, r1, mid[:, lo:hi], ALU.subtract))
                    ins = dve.tensor_copy(t[64:96, lo:hi], r2)
                    if lo == 0:
                        step(ins)
                ins.then_inc(s_tabs, 1)
                dve.wait_ge(s_tabs, d + 1)
            dve.wait_ge(s_dec, 1)
            step(tt(dtdec, dt_, dec, ALU.mult))
            dve.wait_ge(s_st0, 32)
            dve.wait_ge(s_pu, 8)

            def heads(ap):
                return ap.rearrange("p (h d) -> p h d", d=HD)

            def state(n):
                d, j = XDD_ORDER[n]
                if j == 0:
                    return
                dve.wait_ge(s_sp, n + 1)
                b = (6, 0)[n % 2]
                si = j - 1 if d == 0 else 4 + j - 1
                so = si + 1 if d == 0 else si - 1
                c = j * 32 + d * H
                step(tt(heads(st[:, so, :]), heads(st[:, si, :]),
                        etot[:, c:c + H].unsqueeze(2).to_broadcast([P, H, HD]), ALU.mult))
                tt(st[:, so, 0:512], st[:, so, 0:512], psb[b][:, :], ALU.add)
                ins = tt(st[:, so, 512:1024], st[:, so, 512:1024], psb[b + 1][:, :], ALU.add)
                ins.then_inc(s_st, 1)
                dve.wait_ge(s_st, n - 1)

            for n, (d, j) in enumerate(XDD_ORDER):
                if n >= 2:
                    dve.wait_ge(s_sp, n - 1)
                c = j * 32 + d * H
                tt(heads(xdd[:, n % 2, :]), heads(xs[:, j, :]),
                   dtdec[:, c:c + H].unsqueeze(2).to_broadcast([P, H, HD]), ALU.mult).then_inc(s_xdd, 1)
                if n >= 1:
                    state(n - 1)
            state(len(XDD_ORDER) - 1)

            def x_dt(j):
                if j >= 1:
                    dve.wait_ge(s_dg, j * HG)
                for d in range(2):
                    c = j * 32 + d * H
                    ins = tt(heads(xdt[:, d, :]), heads(xs[:, j, :]),
                             dt_[:, c:c + H].unsqueeze(2).to_broadcast([P, H, HD]), ALU.mult)
                ins.then_inc(s_xdt, 1)

            def decay_scores(i):
                j, hh = i // HG, 2 * (i % HG)
                dve.wait_ge(s_ex, i + 1)
                if i == 0:
                    dve.wait_ge(s_gs, 3)
                tt(wbuf(i)[:, :, :], wbuf(i)[:, :, :],
                   gT[:, j, hh // HG, :].unsqueeze(1).to_broadcast([P, 4, P]), ALU.mult).then_inc(s_w, 1)

            def combine(jg):
                j, g = jg // 2, jg % 2
                cols = slice(g * 512, (g + 1) * 512)
                c = j * 32 + g * HG

                def per_head(ap):
                    return ap.unsqueeze(2).to_broadcast([P, HG, HD])

                step(tt(heads(yt[0]), heads(xs[:, j, cols]), per_head(dsum[:, g * HG:(g + 1) * HG]), ALU.mult))
                if j:
                    dve.wait_ge(s_off, jg - 1)
                    for d in range(2):
                        step(tt(heads(yt[1]), heads(psb[2 + d][:, :]), per_head(ecum[:, c + d * H:c + d * H + HG]),
                                ALU.mult))
                        step(tt(yt[0], yt[0], yt[1], ALU.add))
                dve.wait_ge(s_dg, 4 * (jg + 1))
                step(tt(yt[0], yt[0], psb[jg % 2][:, :], ALU.add))
                dve.wait_ge(s_zs, jg + 1)
                tt(xs[:, j, cols], zbuf[jg % 2], yt[0], ALU.mult).then_inc(s_yc, 1)
                dve.wait_ge(s_yc, jg + 1)

            def norm_y(j):
                dve.wait_ge(s_rs, 2 * (2 + j))
                r = stat[:, 5 + j:6 + j]
                ts(xs[:, j, :], xs[:, j, :], r, None, ALU.mult).then_inc(s_yn, 1)

            for i in range(NJ * HG):
                if i % HG == 0 and i == 0:
                    x_dt(0)
                decay_scores(i)
                if i % 4 == 2 and i >= 4:
                    combine(i // 4 - 1)
                if i % HG == HG - 1 and i // HG + 1 < NJ:
                    x_dt(i // HG + 1)
                if i % HG == 4 and i >= HG:
                    norm_y(i // HG - 1)
            combine(2 * NJ - 1)
            norm_y(NJ - 1)

            dve.wait_ge(s_rowl, 32)
            dve.wait_ge(s_xr, 16 * NJ)

            def h2_copy(j):
                dve.wait_ge(s_h2t, j + 1)
                if j >= 1:
                    dve.wait_ge(s_lg, j)
                dve.tensor_copy(h2T[:, 4:8, :], psb[5][:, :].rearrange("p (k t) -> p k t", k=4)).then_inc(s_h2T, 1)

            for j in range(NJ):
                cd = min(j, 1)
                if j >= 1:
                    h2_copy(j - 1)
                for hf_ in range(2):
                    cols = slice(hf_ * 512, (hf_ + 1) * 512)
                    n = 2 * j + hf_
                    dve.wait_ge(s_op, n + 1)
                    step(tt(x1t, psb[n % 4][:, :], g1row[:, cd, cols], ALU.mult))
                    tt(x1[:, j, cols], x1[:, j, cols], x1t, ALU.add).then_inc(s_x1, 1)
                    dve.wait_ge(s_x1, n + 1)
                if j == 0:
                    dve.wait_ge(s_row2, 16)
                dve.wait_ge(s_rs, 2 * (2 + NJ + j))
                r = stat[:, 10 + j:11 + j]
                if j >= 2:
                    dve.wait_ge(s_h2s[j % 2], 16 * (j // 2))
                    dve.wait_ge(s_h2t, j - 1)
                step(stt(h2bufs[j % 2], x1[:, j, :], r, a2row[:, cd, :], ALU.mult, ALU.mult))
                tt(h2bufs[j % 2], h2bufs[j % 2], b2row[:, cd, :], ALU.add).then_inc(s_h2, 1)
                dve.wait_ge(s_h2, j + 1)
            h2_copy(NJ - 1)

            dve.wait_ge(s_lg, NJ)
            at = [160]

            def new(*shape):
                n = int(np.prod(shape))
                at[0] += n
                v = rw[:, at[0] - n:at[0]]
                return v if len(shape) == 1 else v.rearrange("p (a b) -> p a b", b=shape[1])

            def je(ap):
                return ap.rearrange("p (j e) -> p j e", j=NJ)

            def over(ap, n):
                return ap.unsqueeze(2).to_broadcast([P, ap.shape[1], n])

            def across(ap, n):
                return ap.unsqueeze(1).to_broadcast([P, n, ap.shape[1]])

            def largest(out, in_):
                step(dve.tensor_reduce(out, in_, AX_X, ALU.max))

            def total(out, in_):
                step(dve.tensor_reduce(out, in_, AX_X, ALU.add))

            logits = je(psb[6][:, 0:NJ * E])
            top = new(NJ)
            largest(top, logits)
            tt(je(n_sh), logits, over(top, E), ALU.subtract).then_inc(s_lm, 1)
            dve.wait_ge(s_le, 1)
            probs, sel, norm = new(NJ, E), new(NJ, E), new(NJ)
            total(norm, je(n_ex))
            step(dve.reciprocal(norm, norm))
            step(tt(probs, je(n_ex), over(norm, E), ALU.mult))
            step(tt(sel, probs, across(row[:, R_RB:R_RB + E], NJ), ALU.add))
            s4 = sel.rearrange("p j (g e) -> p (j g) e", g=EG)
            pairs = new(NJ * EG, 6)
            tt(pairs[:, :, 0:3], s4[:, :, 0:3], s4[:, :, 1:4], ALU.add)
            tt(pairs[:, :, 3:5], s4[:, :, 0:2], s4[:, :, 2:4], ALU.add)
            step(tt(pairs[:, :, 5:6], s4[:, :, 0:1], s4[:, :, 3:4], ALU.add))
            score, pick, in_group = new(NJ * EG), new(NJ, EG), new(NJ, EG)
            largest(score, pairs)
            s5 = score.rearrange("p (j g) -> p j g", g=EG)
            largest(top, s5)
            step(tt(pick, s5, over(top, EG), ALU.is_equal))
            step(tt(pick, pick, across(cst[:, C_P4:C_P4 + EG], NJ), ALU.mult))
            largest(top, pick)
            step(tt(in_group, pick, over(top, EG), ALU.is_equal))
            low, cand = new(NJ * EG), new(NJ, E)
            ing = in_group.rearrange("p j g -> p (j g)")
            step(ts(low, ing, BIG, -BIG, ALU.mult, ALU.add))
            c4 = cand.rearrange("p j (g e) -> p (j g) e", g=EG)
            step(tt(c4, s4, over(ing, EPG), ALU.mult))
            step(tt(c4, c4, over(low, EPG), ALU.add))
            prio, chosen, weight = new(NJ, E), [new(NJ, E), new(NJ, E)], [new(NJ), new(NJ)]
            for a in range(2):
                largest(top, cand)
                step(tt(prio, cand, over(top, E), ALU.is_equal))
                step(tt(prio, prio, across(cst[:, C_P16:C_P16 + E], NJ), ALU.mult))
                largest(top, prio)
                step(tt(chosen[a], prio, over(top, E), ALU.is_equal))
                if a == 0:
                    step(stt(cand, chosen[0], -3 * BIG, cand, ALU.mult, ALU.add))
                step(tt(prio, chosen[a], probs, ALU.mult))
                total(weight[a], prio)
            tt(je(onehotb[:, :]), chosen[0], chosen[1], ALU.add).then_inc(s_oh, 1)
            step(tt(norm, weight[0], weight[1], ALU.add))
            step(dve.reciprocal(norm, norm))
            for a in range(2):
                step(tt(gate[:, a * NJ:(a + 1) * NJ], weight[a], norm, ALU.mult))
            dve.wait_ge(s_rk, 1)
            tiles, ends, base, steps = new(E), new(E), new(E), new(E, 4)
            step(tt(steps, over(psb[7][:, NJ * E:(NJ + 1) * E], 4), across(cst[:, C_STEP:C_STEP + 4], E), ALU.is_gt))
            total(tiles, steps)
            step(ts(tiles, tiles, 1.0, None, ALU.add))
            step(dve.tensor_tensor_scan(ends, ones[:, 0:E], tiles, 0.0, ALU.mult, ALU.add))
            step(tt(base, ends, tiles, ALU.subtract))
            step(ts(base, base, float(P), None, ALU.mult))
            slots, mine, place = new(NJ, E), new(NJ, E), new(NJ)
            step(tt(slots, je(psb[7][:, 0:NJ * E]), across(base, NJ), ALU.add))
            for a in range(2):
                step(tt(mine, chosen[a], slots, ALU.mult))
                total(place, mine)
                step(dve.tensor_copy(ri[:, 40 + a * NJ:40 + (a + 1) * NJ], place))
            past, owner = new(28, E), new(28)
            step(tt(past, across(ends, 28), over(cst[:, C_ITEM:C_ITEM + 28], E), ALU.is_le))
            total(owner, past)
            step(ts(owner, owner, float(E - 1), None, ALU.min))
            dve.tensor_copy(ri[:, 0:28], owner)
            dve.tensor_copy(ri[:, 32:32 + NJ], cst[:, C_TOKEN:C_TOKEN + NJ])
            dve.tensor_copy(ri[:, 60:61], ends[:, E - 1:E]).then_inc(s_rt, 1)

            dve.wait_ge(s_rt, 1)
            k_tiles = dve.value_load(ri[0:1, 60:61], min_val=16, max_val=25)
            dve.sem_inc(s_ac, 2)

            def copy_tokens(n):
                dve.wait_ge(s_xtp, n)
                dve.tensor_copy(xgT[:, 4:8, :], psb[3][:, :].rearrange("p (k t) -> p k t", k=4)).then_inc(s_xgT, 1)

            copy_tokens(1)
            with dve.Fori(0, k_tiles) as i:
                dve.wait_ge(s_dn, i * 2 + 2)
                for c in range(FT):
                    dve.wait_ge(s_sg, i * FT + (c + 1))
                    tt(aT[:, c, :], sg[c % 2], psb[c % 2][:, P:2 * P], ALU.mult).then_inc(s_ac, 1)
                copy_tokens(i + 2)
                dve.wait_ge(s_dn, i * 2 + 4)
                dve.wait_ge(s_yst, i * 16 + 16)
                dve.tensor_copy(yo[:, 512:1024], psb[7][:, :]).then_inc(s_yo, 1)

            dve.wait_ge(s_row2, 32)
            dve.wait_ge(s_fn, 16)
            for j in range(NJ):
                cd = min(j, 1)
                dve.wait_ge(s_yg[j % 2], 32 * (j // 2 + 1))
                ya = ygb[:, ((2 * j) % 4) * D:((2 * j) % 4 + 1) * D]
                yb = ygb[:, ((2 * j) % 4 + 1) * D:((2 * j) % 4 + 2) * D]
                step(ts(ya, ya, gate[:, j:j + 1], None, ALU.mult))
                step(stt(yb, yb, gate[:, NJ + j:NJ + j + 1], ya, ALU.mult, ALU.add))
                step(tt(yb, yb, g2row[:, cd, :], ALU.mult))
                tt(x1[:, j, :], x1[:, j, :], yb, ALU.add).then_inc(s_fin, 1)
                dve.wait_ge(s_rs, 2 * (2 + 2 * NJ + j))
                r = stat[:, j:j + 1]
                if j >= 2:
                    dve.wait_ge(s_ost[j % 2], 16 * (j // 2))
                stt(fout[j % 2], x1[:, j, :], r, fnrow, ALU.mult, ALU.mult).then_inc(s_fo, 1)


def layout(a):
    f = np.float32
    p = np.arange(P)
    cst = np.zeros((P, C_ALL), f)
    cst[:, C_ID:C_ID + P] = np.eye(P)
    cst[:, C_TRIF:C_TRIF + P] = p[:, None] <= p[None]
    cst[:, C_TRIB:C_TRIB + P] = p[:, None] >= p[None]
    cst[:, C_ONES:C_ONES + P] = 1
    cst[:, C_P16:C_P16 + E] = E - np.arange(E)
    cst[:, C_P4:C_P4 + EG] = EG - np.arange(EG)
    cst[:, C_ITEM:C_ITEM + 28] = np.arange(28)
    cst[:, C_STEP:C_STEP + 4] = P * (1 + np.arange(4))
    cst[:, C_TOKEN:C_TOKEN + NJ] = p[:, None] + P * np.arange(NJ)
    bc = np.zeros((P, B_ALL), f)
    bc[:, B_STRICT:B_STRICT + P] = p[:, None] < p[None]
    bc[:, B_MASK:B_MASK + P] = np.where(p[:, None] > p[None], -BIG, 0)
    bc[:, B_MASK + P:B_MASK + 2 * P] = np.where(p[:, None] < p[None], -BIG, 0)
    bc[:96, B_STACK:B_STACK + 32] = np.arange(96)[:, None] % 32 == np.arange(32)

    def cols(v, n):
        return np.asarray(v, f).reshape(n, P).T

    vec = np.zeros((P, V_ALL), f)
    vec[:, V_ADA:V_ADA + 96] = np.repeat(cols(a["b_ada"][0], 48), 2, axis=1)
    vec[:, V_N1:V_N1 + 16] = np.repeat(cols(a["norm1_w"][0], KT), 2, axis=1)
    vec[:, V_N2:V_N2 + 16] = np.repeat(cols(a["norm2_w"][0], KT), 2, axis=1)
    order = np.r_[D:D + 512, 0:D]
    vec[:, V_CW:V_CW + 48] = a["conv_w"][0][:, order].reshape(4, CONVF, P).transpose(2, 1, 0).reshape(P, 48)
    vec[:, V_CB:V_CB + CONVF] = cols(a["conv_b"][0][order], CONVF)
    vec[:, V_PS:V_PS + 8] = cols(a["pool_scale"][0], KT)
    vec[:, V_SN:V_SN + 8] = cols(a["ssd_norm_w"][0], KT)
    vec[:, V_C:V_C + 16] = np.stack([cols(a["c_ctx"], KT), cols(a["c"][0], KT)], axis=2).reshape(P, 16)
    row = np.concatenate([np.asarray(a["router_bias"], f), a["dt_bias"][0].reshape(-1), a["a_log"][0].reshape(-1),
                          a["d_skip"][0].reshape(-1)])[None]

    def count(n, w):
        i = np.arange(n)
        return np.clip(i + w // 2 - 1, 0, n - 1) - np.clip(i - w // 2, 0, n - 1) + 1

    inv = np.concatenate([np.concatenate([1 / count(CTX, w), (1 / np.outer(count(ROWS, w), count(GRID_W, w))).ravel()])
                          for w in WINDOWS]).astype(f)[None]
    w_ada, w_in, w_out = a["w_ada"][0], a["w_in"][0], a["w_out"][0]

    def chunk(w, c0):
        return w[:, c0:c0 + 512].reshape(KT, P, 512).transpose(1, 0, 2).reshape(P, CHUNK)

    x0 = D
    v0 = D + D + 512 + 32
    parts = [chunk(w_ada, 512 * i) for i in range(4)]
    parts += [chunk(w_in, c0) for c0 in (v0, v0 + 512, x0 + D, x0, x0 + 512, 0, 512)]
    w_late = np.stack([chunk(w_ada, 512 * q)[:, i * 2048:(i + 1) * 2048] for q in range(4, 12) for i in range(2)])
    parts += [chunk(w_out[c * D:(c + 1) * D], h * 512) for h in range(2) for c in range(2)]
    w_dt = w_in[:, v0 - 32:v0].reshape(KT, P, 32).transpose(1, 0, 2).reshape(P, KT * 32)
    w_pool = a["pool_w"][0].reshape(4, 2, P, 256).transpose(2, 0, 1, 3).reshape(P, 2048)
    gu = np.stack([a["w_gate"][0], a["w_up"][0]], axis=1).reshape(E, 2, KT, P, FT, P)
    gu = gu.transpose(0, 4, 3, 1, 2, 5).reshape(E, FT, P, 2048)
    dn = a["w_down"][0].reshape(E, 2, 2, P, D).transpose(0, 1, 3, 2, 4).reshape(E, 2, P, 2048)
    return {
        "consts": cst, "bconsts": bc, "vecs": vec, "rows": row, "inv": inv,
        "w_late": w_late, "b_late": a["b_ada"][0][2 * D:].reshape(8, 512), "norm2": a["norm2_w"],
        "fnorm": a["final_norm_w"][None], "x": np.concatenate([a["x_prompt"][0], a["x_sample"][0]]),
        "states0": a["state_ssm"][0, 0].transpose(0, 3, 1, 2).reshape(2, N, D),
        "w_ring": np.stack(parts), "w_dt": w_dt, "w_pool": w_pool,
        "w_router": a["w_router"].reshape(KT, P, E).transpose(1, 0, 2).reshape(P, KT * E),
        "w_exp": np.concatenate([gu, dn], axis=1),
    }


_OUTS = {"y_out": (TOK, D), "s_out": (2, D, N)}


def kernel(**inputs):
    import concourse.bacc as bacc
    from concourse.bass_utils import run_bass_kernel_spmd

    nc = bacc.Bacc("TRN2", target_bir_lowering=False, num_devices=1)
    a = {k: np.asarray(v) for k, v in inputs.items()}
    arrays = {k: np.ascontiguousarray(v) for k, v in layout(a).items()}
    aps = {k: nc.dram_tensor(k, v.shape, mybir.dt.from_np(v.dtype), kind="ExternalInput").ap()
           for k, v in arrays.items()}
    for name, shape in _OUTS.items():
        aps[name] = nc.dram_tensor(name, shape, F32, kind="ExternalOutput").ap()
    trunk_kernel(nc, **aps)
    r = run_bass_kernel_spmd(nc, [arrays], core_ids=[0]).results[0]
    y, s = np.asarray(r["y_out"]), np.asarray(r["s_out"])
    return y[None, :CTX], y[None, CTX:], s.reshape(1, 1, 2, H, HD, N)
```

```python
from contextlib import ExitStack

import numpy as np

import concourse.bass as bass
import concourse.mybir as mybir
from concourse.alu_op_type import AluOpType as ALU

F32 = mybir.dt.float32
BF16 = mybir.dt.bfloat16
I32 = mybir.dt.int32
ACT = mybir.ActivationFunctionType
AX_X = mybir.AxisListType.X

P = 128
D = 1024
KT = D // P
CTX, LAT = 128, 512
TOK = CTX + LAT
NJ = TOK // P
GRID_W = 64
ROWS = LAT // GRID_W
H, HD, N = 16, 64, 128
HG = H // 2
E, EG, EPG = 16, 4, 4
FF = 512
FT = FF // P
CONVF = 12
WINDOWS = (2, 4, 8, 16)
EPS = 1e-6
BIG = 1e30
MAX_TILES = 26
SLOTS = MAX_TILES * P
RING = 3
CHUNK = 4096

C_ID, C_TRIF, C_TRIB, C_ONES = 0, 128, 256, 384
C_P16, C_P4, C_ITEM, C_STEP, C_TOKEN, C_START, C_POS = 512, 528, 532, 560, 564, 574, 602
C_ALL = 730
B_STRICT, B_MASK, B_STACK, B_ALL = 0, 128, 384, 416
XDD_ORDER = ((0, 0), (1, 0), (0, 1), (1, 4), (0, 2), (1, 3), (0, 3), (1, 2))
V_ADA, V_N1, V_N2, V_CW, V_CB, V_PS, V_SN, V_C = 0, 96, 112, 128, 176, 188, 196, 204
V_ALL = 220
R_RB, R_DTB, R_ALOG, R_DSK = 0, 16, 48, 80
R_ALL = 112
INV_ALL = 4 * TOK


class Steps:

    def __init__(self, eng, sem):
        self.eng, self.sem, self.n = eng, sem, 0

    def __call__(self, ins):
        self.n += 1
        ins.then_inc(self.sem, 1)
        self.eng.wait_ge(self.sem, self.n)


def trunk_kernel(nc, consts, bconsts, vecs, rows, inv, norm2, fnorm, x, states0, w_ring, w_late, b_late, w_dt, w_pool, w_router,
                 w_exp, y_out, s_out):
    ctx = ExitStack()
    with ctx:
        def sb(name, shape, dt=F32):
            return ctx.enter_context(nc.sbuf_tensor(name, shape, dt))

        def sem(name):
            return ctx.enter_context(nc.semaphore(name))

        ada_rows = nc.dram_tensor("ada_rows", [4, 2, D], F32).ap()
        h2_dram = nc.dram_tensor("h2_dram", [TOK, D], F32).ap()
        slot_out = nc.dram_tensor("slot_out", [SLOTS - P, D], F32).ap()

        ring = sb("ring", [P, RING, CHUNK])
        ex = sb("ex", [P, 12288])
        yT = sb("yT", [P, KT, TOK])
        xs = sb("xs", [P, NJ, D])
        bcT = sb("bcT", [P, 4, TOK])
        btok = sb("btok", [P, NJ, 2 * N])
        gT = sb("gT", [P, NJ, 2, P])
        uT = sb("uT", [P, KT, TOK])
        hT = sb("hT", [P, KT, TOK])
        cst = sb("cst", [P, C_ALL])
        vec = sb("vec", [P, V_ALL])
        row = sb("row", [P, R_ALL])
        idb = sb("idb", [P, P], BF16)
        maskb = sb("maskb", [P, 2, P], BF16)
        strictb = sb("strictb", [P, P], BF16)
        onesb = sb("onesb", [P, P], BF16)
        stackb = sb("stackb", [96, 32], BF16)
        nstackb = sb("nstackb", [96, 32], BF16)
        silc = sb("silc", [P, 2 * KT])
        modA = sb("modA", [P, 2 * KT])
        modB = sb("modB", [P, 2 * KT])
        stat = sb("stat", [P, 27])
        eps_col = sb("eps_col", [P, 1])
        dts = sb("dts", [P, 8, NJ * 32])
        nega = sb("nega", [P, 32])
        dsum = sb("dsum", [P, H])

        ident = cst[:, C_ID:C_ID + P]
        trif = cst[:, C_TRIF:C_TRIF + P]
        trib = cst[:, C_TRIB:C_TRIB + P]
        ones = cst[:, C_ONES:C_ONES + P]
        dt_, a_, ncum, ecum, dec, etot, sc0, sc1 = (dts[:, i, :] for i in range(8))
        dtdec = dec

        xt = ex[:, 0:NJ * D].rearrange("p (j d) -> p j d", j=NJ)
        XP = 131 + 515
        xpad = [ex[:, i * XP:(i + 1) * XP] for i in range(2)]
        cacc = [ex[:, 1300 + i * XP:1300 + i * XP + 643] for i in range(2)]
        xsT = [ex[:, 2600 + i * TOK:2600 + (i + 1) * TOK] for i in range(2)]
        pa, pb_, pc = (ex[:, 3900 + i * 960:3900 + (i + 1) * 960] for i in range(3))
        arow = ex[0:2, 5120:5120 + 2048]
        brow = ex[0:1, 6784:6784 + 512]
        n2row = ex[0:1, 7296:7296 + D]
        orow = ex[0:1, 8320:8320 + D]
        invb = ex[:, 12288 - INV_ALL:12288]
        wdt = gT[:, 0, :, :].rearrange("p a b -> p (a b)")
        st = ex[:, 0:8 * D].rearrange("p (i d) -> p i d", i=8)
        xdt = ex[:, 8192:8192 + 2 * D].rearrange("p (i d) -> p i d", i=2)
        xdd = ex[:, 10240:10240 + 2 * D].rearrange("p (i d) -> p i d", i=2)
        hf = hT[:, :, :].rearrange("p k t -> p (k t)")
        uf = uT[:, :, :].rearrange("p k t -> p (k t)")
        zf = yT[:, :, :].rearrange("p k t -> p (k t)")
        bf_ = bcT[:, :, :].rearrange("p f t -> p (f t)")
        btf = btok[:, :, :].rearrange("p j n -> p (j n)")
        adaw = [zf[:, i * 2048:(i + 1) * 2048].rearrange("p (k c) -> p k c", k=4) for i in range(2)]
        acc = [zf[:, 4096:5120], ex[:, 2600:3624]]
        gT_pw = zf[:, 0:2048].rearrange("p (g k m) -> p g k m", g=4, k=2)
        bcst = hf[:, 0:B_ALL]
        tabT = [bf_[0:96, d * 320:(d + 1) * 320].bitcast(BF16) for d in range(2)]
        yt = [bf_[:, 640:1152], ex[:, 11776:12288]]
        wbufs = [ex[:, 10240 + i * 512:10240 + (i + 1) * 512].rearrange("p (q t) -> p q t", q=4) for i in range(3)]
        sout = [zf[:, 2048 + d * D:2048 + (d + 1) * D] for d in range(2)]
        split_r = [ex[0:32, 8192 + i * TOK:8192 + (i + 1) * TOK] for i in range(2)]
        mid = zf[0:32, 4096:4416].bitcast(BF16)
        zbuf = [btf[:, i * 512:(i + 1) * 512] for i in range(2)]
        junk_x = uf[:, 0:D]
        junk_y = btf[:, 1024:1280].bitcast(BF16)
        junk_1 = dts[:, :, :].rearrange("p a b -> p (a b)")[:, 768:1280].bitcast(BF16)
        junk_z = zf[:, 2 * D:3 * D]
        zero_f = xs[:, 0, :]
        MASK4 = maskb[:, :, :].unsqueeze(1).to_broadcast([P, 2, 2, P])

        def wbuf(i):
            return wbufs[i % 3]

        def pooled_banks(i):
            if i < 4:
                return (psb[1][:, 256:384], psb[0][:, :]) if i % 2 == 0 else (psb[7][:, 0:CTX], psb[6][:, :])
            return psb[3 + 2 * (i % 2)][:, 0:CTX], psb[2 + 2 * (i % 2)][:, :]

        psb = [ctx.enter_context(nc.psum_tensor(f"bank{i}", [P, 512], F32)) for i in range(8)]

        s_const = sem("constants_loaded")
        s_x = sem("x_loaded")
        s_ring = [sem(f"ring_{i}_loaded") for i in range(RING)]
        s_adaw = [sem(f"ada_half_{i}_loaded") for i in range(2)]
        s_brow = sem("ada_bias_loaded")
        s_n2 = sem("norm2_row_loaded")
        s_ar = sem("ada_rows_product")
        s_g2w = [sem(f"gate2_chunk_{i}_loaded") for i in range(2)]
        s_g2d = sem("gate2_rows_stored")
        s_g2p = sem("gate2_products")
        s_g2c = sem("gate2_rows_ready")
        s_g2b = sem("gate2_bias_loaded")
        s_arc = sem("ada_rows_on_chip")
        s_adr = sem("late_ada_rows_ready")
        s_ada = sem("ada_sums")
        s_accs = sem("ada_partial_sums")
        s_acc = sem("ada_half_summed")
        s_wo3 = sem("last_output_weights_loaded")
        s_yf = sem("gated_outputs_final")
        s_used = sem("ring_chunks_used")
        s_wdt = sem("dt_weights_loaded")
        s_inv = sem("inverse_counts_loaded")
        s_pw = sem("pool_weights_loaded")
        s_st0 = sem("initial_states_loaded")
        s_cast = sem("constants_cast")
        s_rs = sem("rms_ready")
        s_dve = sem("dve_steps")
        s_pool = sem("pool_steps")
        s_silc = sem("silu_c_ready")
        s_mod = sem("modulation_ready")
        s_ss = sem("x_squares_summed")
        s_xn = sem("x_normalised")
        s_xtr = sem("x_transposed")
        s_hs = sem("h_latents_ready")
        s_hc = sem("h_context_ready")
        s_dtp = sem("dt_product")
        s_soft = sem("softplus_handover")
        s_a = sem("decay_rates_ready")
        s_cum = sem("decay_sums")
        s_dif = sem("decay_exponents_ready")
        s_dtd = sem("dt_decays_ready")
        s_dec = sem("decays_ready")
        s_fm = sem("feature_tiles_projected")
        s_pad = sem("conv_inputs_copied")
        s_conv = sem("conv_summed")
        s_cs = sem("conv_activated")
        s_ttr = sem("conv_tiles_transposed")
        s_tok = sem("conv_tiles_token_major")
        s_vr = sem("v_copied")
        s_pu = sem("windows_pooled")
        s_z = sem("z_projected")
        s_zt = sem("tanh_of_half_z")
        s_zs = sem("z_activated")
        s_pm = sem("pool_products")
        s_u = sem("pool_scaled")
        s_tab = sem("decay_tables_summed")
        s_tabs = sem("decay_tables_split")
        s_g = sem("bc_products")
        s_gs = sem("bc_products_copied")
        s_xdd = sem("x_decayed")
        s_sp = sem("state_products")
        s_st = sem("states_ready")
        s_so = sem("context_states_copied")
        s_sout = sem("context_states_stored")
        s_xdt = sem("x_dt_ready")
        s_e = sem("exponents_built")
        s_ex = sem("decays_exponentiated")
        s_w = sem("scores_decayed")
        s_dg = sem("diagonal_products")
        s_off = sem("state_outputs")
        s_yp = sem("ssd_state_outputs_read")
        s_yc = sem("ssd_outputs_combined")
        s_ys = sem("ssd_squares_summed")
        s_yss = sem("ssd_squares_joined")
        s_ytr = sem("ssd_outputs_transposed")
        s_yT = sem("ssd_outputs_ready")
        s_ads = sem("ada_rows_stored")
        s_rowl = sem("ada_rows_loaded")
        s_row2 = sem("late_rows_loaded")
        s_xr = sem("x_reloaded")
        s_op = sem("output_products")
        s_x1 = sem("residual_ready")
        s_x1s = sem("residual_squares_summed")
        s_h2 = sem("h2_ready")
        s_h2s = [sem(f"h2_stored_{i}") for i in range(2)]
        s_h2t = sem("h2_transposed")
        s_h2T = sem("h2_feature_major")
        s_lg = sem("logits_ready")
        s_wr = sem("router_weights_loaded")
        s_lm = sem("logits_shifted")
        s_le = sem("logits_exponentiated")
        s_oh = sem("choices_ready")
        s_rk = sem("ranks_ready")
        s_rt = sem("routing_ready")
        s_zero = sem("slot_tokens_cleared")
        s_pos = sem("slot_positions_ready")
        s_tk = sem("slot_tokens_summed")
        s_w_in = [sem(f"expert_chunk_{c}_loaded") for c in range(6)]
        s_idx = sem("slot_tokens_loaded")
        s_xg = sem("tokens_gathered")
        s_begun = sem("gathers_begun")
        s_xtp = sem("gathered_transposed")
        s_xgT = sem("gathered_feature_major")
        s_gu = sem("gate_up_products")
        s_sg = sem("gates_activated")
        s_ac = sem("expert_activations")
        s_dn = sem("down_products")
        s_yo = sem("expert_outputs_copied")
        s_yst = sem("expert_outputs_stored")
        s_yg = [sem(f"expert_rows_gathered_{j}") for j in range(NJ)]
        s_ya = sem("first_rows_weighted")
        s_fin = sem("final_sum_ready")
        s_fss = sem("final_squares_summed")
        s_fo = sem("final_output_ready")
        s_ost = [sem(f"outputs_stored_{i}") for i in range(2)]
        s_fn = sem("final_norm_loaded")

        x1 = xs
        wo = [ring[:, 2, :], ring[:, 0, :], ring[:, 1, :], hf[:, 0:CHUNK]]
        g1row = ex[:, 0:2 * D].rearrange("p (c d) -> p c d", c=2)
        a2row = ex[:, 2 * D:4 * D].rearrange("p (c d) -> p c d", c=2)
        w_g2 = [ex[:, (4 + 4 * i) * D:(8 + 4 * i) * D] for i in range(2)]
        h2buf0 = hf[:, 4 * D:5 * D]
        b2row = bf_[:, 0:2 * D].rearrange("p (c d) -> p c d", c=2)
        g2b = uf[0:2, 3 * D:4 * D].rearrange("p (i n) -> p i n", n=512)
        g2s = uf[0:2, 4 * D:5 * D].rearrange("p (i n) -> p i n", n=512)
        x1t = bf_[:, 2 * D:2 * D + 512]
        gtf = gT[:, :, :, :].rearrange("p j g n -> p (j g n)")
        h2buf1 = btf[:, 0:D]
        h2bufs = [h2buf0, h2buf1]
        wrt = gtf[:, D:D + P].rearrange("p (k e) -> p k e", e=E)
        h2T = gtf[:, 0:D].rearrange("p (k t) -> p k t", k=KT)
        xg = zf[:, 0:D]
        xgT = zf[:, D:2 * D].rearrange("p (k t) -> p k t", k=KT)
        aT = zf[:, 2 * D:2 * D + FT * P].rearrange("p (k t) -> p k t", k=FT)
        sg = [zf[:, 2560 + i * P:2560 + (i + 1) * P] for i in range(2)]
        yo = zf[:, 3072:3072 + D]
        g2row = uf[:, 0:2 * D].rearrange("p (c d) -> p c d", c=2)
        fnrow = uf[:, 2 * D:3 * D]
        fout = [uf[:, 3 * D + i * D:3 * D + (i + 1) * D] for i in range(2)]
        ygb = ex[:, 0:2 * NJ * D].rearrange("p (n d) -> p n d", d=D)
        ri = sb("ri", [P, 64], I32)
        idx = sb("idx", [P, 2], I32)
        token_of = sb("token_of", [P, MAX_TILES + 1], I32)
        gate = sb("gate", [P, 2 * NJ])
        dtf = dts[:, :, :].rearrange("p a b -> p (a b)")
        rw_a, rw_b = dtf[:, 0:768], ring[:, 2, :]
        n_sh, n_ex = rw_a[:, 0:80], rw_a[:, 80:160]
        at_pos = zf[:, 2 * D:2 * D + 2 * NJ * P].rearrange("p (i n) -> p i n", n=P)
        in_tile = zf[:, 3328:3328 + 2 * NJ * MAX_TILES].rearrange("p (i n) -> p i n", n=MAX_TILES)
        onehotb = sb("onehotb", [P, NJ * E], BF16)

        block = ctx.enter_context(nc.Block())

        NCH = 14
        @block.sync
        def _(sp):
            sp.dma_start(cst[:], consts).then_inc(s_const, 16)
            sp.dma_start(bcst, bconsts).then_inc(s_const, 16)
            sp.dma_start(vec[:], vecs).then_inc(s_const, 16)
            sp.dma_start(row[:], rows.to_broadcast([P, R_ALL])).then_inc(s_const, 16)

            def load_ring(n):
                if n >= RING:
                    sp.wait_ge(s_used, n - RING + 1)
                sp.dma_start(ring[:, n % RING, :], w_ring[n]).then_inc(s_ring[n % RING], 16)

            load_ring(0)
            for j in range(NJ):
                sp.dma_start(xt[:, j, :], x[j * P:(j + 1) * P, :]).then_inc(s_x, 16)

            def load_ada(u):
                if u >= 2:
                    sp.wait_ge(s_acc, u - 1)
                sp.dma_start(adaw[u % 2], w_late[u].rearrange("p (k c) -> p k c", k=4)).then_inc(s_adaw[u % 2], 16)
                if u % 2 == 1 and u >= 3 or u == 0:
                    q = (u - 1) // 2 if u else 0
                    if q >= 1:
                        sp.wait_ge(s_adr, q)
                    else:
                        sp.wait_ge(s_ar, 1)
                    sp.dma_start(brow, b_late[q:q + 1, :]).then_inc(s_brow, 16)

            for n in range(1, 4):
                load_ring(n)
            sp.dma_start(wdt, w_dt).then_inc(s_wdt, 16)
            for n in (4, 5):
                load_ring(n)
            sp.dma_start(n2row, norm2).then_inc(s_n2, 16)
            sp.dma_start(invb, inv.to_broadcast([P, INV_ALL])).then_inc(s_inv, 16)
            load_ring(6)
            for u in range(10):
                load_ada(u)
            load_ring(7)
            for u in (10, 11):
                load_ada(u)
            for n in range(8, NCH):
                load_ring(n)
            sp.wait_ge(s_z, 2 * NJ)
            sp.dma_start(wo[3], w_ring[NCH]).then_inc(s_wo3, 16)
            sp.wait_ge(s_dg, NJ * HG)
            sp.wait_ge(s_yc, 2 * NJ)
            sp.wait_ge(s_op, 2)
            for i in range(2):
                sp.dma_start(w_g2[i], w_ring[NCH + 1 + i]).then_inc(s_g2w[i], 16)
            sp.wait_ge(s_h2, NJ)
            for c in range(6):
                if c in (2, 4):
                    sp.wait_ge(s_g2p, c // 2)
                sp.dma_start(ex[:, c * 2048:(c + 1) * 2048], w_exp[0, c]).then_inc(s_w_in[c], 16)
            sp.wait_ge(s_rt, 1)
            k_tiles = sp.value_load(ri[0:1, 60:61], min_val=16, max_val=25)
            with sp.Fori(1, k_tiles) as i:
                e = sp.value_load(ri[0:1, bass.ds(i, 1)], min_val=0, max_val=E - 1)
                for c in range(6):
                    if c < FT:
                        sp.wait_ge(s_gu, i * FT + (c + 1 - FT))
                    else:
                        sp.wait_ge(s_dn, i * 2 + (c - FT + 1))
                    sp.dma_start(ex[:, c * 2048:(c + 1) * 2048], w_exp[e, c]).then_inc(s_w_in[c], 16)
            for j in range(NJ):
                sp.wait_ge(s_fo, j + 1)
                sp.dma_start(y_out[j * P:(j + 1) * P, :], fout[j % 2]).then_inc(s_ost[j % 2], 16)
            sp.wait_ge(s_ost[0], 48)
            sp.wait_ge(s_ost[1], 32)
            sp.wait_ge(s_sout, 32)

        @block.tensor
        def _(pe):
            pe.wait_ge(s_silc, 1)
            pe.wait_ge(s_const, 64)

            for n in range(4):
                pe.wait_ge(s_ring[n % RING], 16 * (n // RING + 1))
                w = ring[:, n % RING, :].rearrange("p (k c) -> p k c", k=KT)
                for k in range(KT):
                    mm = pe.matmul(psb[n][0:2, :], silc[:, 2 * k:2 * k + 2], w[:, k, :],
                                   start=(k == 0), stop=(k == KT - 1))
                mm.then_inc(s_used, 1)
            for m in range(16):
                if m % 4 == 0:
                    pe.wait_ge(s_arc, m // 4 + 1)
                mm = pe.transpose(psb[4][:, 2 * m:2 * m + 2], arow[:, m * P:(m + 1) * P], ident[0:2, 0:2])
            mm.then_inc(s_ar, 1)
            for j in range(NJ):
                pe.wait_ge(s_xn, j + 1)
            for k in range(KT):
                if k == 0:
                    pe.wait_ge(s_arc, 4)
                if k == 1:
                    pe.wait_ge(s_mod, 1)
                if k >= 3:
                    pe.wait_ge(s_hs, k - 2)
                    pe.wait_ge(s_hc, k - 2)
                q = 2 + 2 * (k % 3)
                for j in range(NJ):
                    o = psb[q + 1][:, 0:P] if j == 0 else psb[q][:, (j - 1) * P:j * P]
                    mm = pe.transpose(o, xt[:, j, k * P:(k + 1) * P], ident)
                mm.then_inc(s_xtr, 1)
            pe.wait_ge(s_hs, KT)
            pe.wait_ge(s_hc, KT)
            pe.wait_ge(s_wdt, 16)
            for j in range(NJ):
                for k in range(KT):
                    mm = pe.matmul(psb[1][:, j * 32:(j + 1) * 32], hT[:, k, j * P:(j + 1) * P],
                                   wdt[:, k * 32:(k + 1) * 32], start=(k == 0), stop=(k == KT - 1))
            mm.then_inc(s_dtp, 1)

            def turn_conv(t):
                f = t if t < 2 else t + 2
                pe.wait_ge(s_cs, f + 1)
                if t == 0:
                    pe.wait_ge(s_adr, 6)
                if t >= 1:
                    pe.wait_ge(s_tok, t)
                src = bcT[:, t, :] if t < 2 else xsT[t % 2]
                for j in range(NJ):
                    o = psb[1][:, 0:P] if j == 0 else psb[0][:, (j - 1) * P:j * P]
                    mm = pe.transpose(o, src[:, j * P:(j + 1) * P], ident)
                mm.then_inc(s_ttr, 1)

            for f in range(20):
                n = 4 + f // 4
                pe.wait_ge(s_ring[n % RING], 16 * (n // RING + 1))
                if f >= 3:
                    pe.wait_ge(s_vr if f - 3 < KT else s_pad, f - 2 if f - 3 < KT else f - 2 - KT)
                w = ring[:, n % RING, :].rearrange("p (k c) -> p k c", k=KT)
                q = 2 + 2 * (f % 3)
                for lo, hi, o in ((0, CTX, psb[q + 1][:, 0:CTX]), (CTX, TOK, psb[q][:, :])):
                    for k in range(KT):
                        mm = pe.matmul(o, w[:, k, (f % 4) * P:(f % 4 + 1) * P], hT[:, k, lo:hi],
                                       start=(k == 0), stop=(k == KT - 1))
                mm.then_inc(s_fm, 1)
                if f % 4 == 3:
                    pe.wait_ge(s_fm, f + 1)
                    pe.sem_inc(s_used, 1)
                if f == 1:
                    pe.wait_ge(s_a, 1)
                    for j in range(NJ):
                        for d, tri in ((0, trif), (1, trib)):
                            c = j * 32 + d * H
                            pe.matmul(psb[0][:, c:c + H], tri, a_[:, c:c + H], start=True, stop=True)
                    pe.matmul(psb[0][:, 160:320], ones, a_, start=True, stop=True).then_inc(s_cum, 1)
                    pe.wait_ge(s_dif, 1)
                if 2 <= f < 8:
                    q = f - 2
                    pe.wait_ge(s_acc, 2 * (q + 1))
                    if q >= 1:
                        pe.wait_ge(s_adr, q)
                    for c in range(2):
                        mm = pe.matmul(psb[c][0:1, :], ones[:, 0:1],
                                       acc[q % 2][:, c * 512:(c + 1) * 512], start=True, stop=True)
                    mm.then_inc(s_ada, 1)
                if f == 11:
                    turn_conv(0)
                elif 13 <= f:
                    turn_conv(f - 12)
            turn_conv(8)
            turn_conv(9)

            def project_z(jg, ks):
                j, g = jg // 2, jg % 2
                w = ring[:, g, :].rearrange("p (k c) -> p k c", k=KT)
                if ks[0] == 0 and jg < 2:
                    pe.wait_ge(s_ring[g], 16 * 4)
                if ks[0] == 0 and jg >= 1:
                    pe.wait_ge(s_zs, jg)
                for k in ks:
                    mm = pe.matmul(psb[6][:, :], hT[:, k, j * P:(j + 1) * P], w[:, k, :],
                                   start=(k == 0), stop=(k == KT - 1), skip_group_check=True)
                if ks[-1] == KT - 1:
                    mm.then_inc(s_z, 1)

            pe.wait_ge(s_pad, CONVF)
            for d, tri in ((0, trif), (1, trib)):
                q = 2 + 2 * d
                for j in range(NJ):
                    o = psb[q + 1][0:32, 0:P] if j == 0 else psb[q][0:32, (j - 1) * P:j * P]
                    mm = pe.matmul(o, a_[:, j * 32:(j + 1) * 32], tri, start=True, stop=True)
                mm.then_inc(s_tab, 1)
            for j in range(NJ):
                for g in range(2):
                    i = 2 * j + g
                    if i == 8:
                        pe.wait_ge(s_tok, 10)
                    o = psb[6 + i // 4][:, (i % 4) * P:(i % 4 + 1) * P] if i < 8 else \
                        psb[1][:, (i % 4) * P:(i % 4 + 1) * P]
                    mm = pe.matmul(o, bcT[:, g, j * P:(j + 1) * P], bcT[:, 2 + g, j * P:(j + 1) * P],
                                   start=True, stop=True)
            mm.then_inc(s_g, 1)
            def pool_product(i):
                g, m = i // 2, i % 2
                ctx_out, lat_out = pooled_banks(i)
                if i < 2:
                    pe.wait_ge(s_gs, (1, 3)[i])
                elif 2 <= i < 4 or i >= 6:
                    pe.wait_ge(s_u, i - 1)
                elif i >= 4:
                    pe.wait_ge(s_so, 2 * (i - 3))
                for lo, hi, o in ((0, CTX, ctx_out), (CTX, TOK, lat_out)):
                    for kk in range(2):
                        mm = pe.matmul(o, gT_pw[:, g, kk, m * P:(m + 1) * P], uT[:, 2 * g + kk, lo:hi],
                                       start=(kk == 0), stop=(kk == 1))
                mm.then_inc(s_pm, 1)

            pe.wait_ge(s_pw, 16)
            pe.wait_ge(s_pu, 8)
            for i in range(4):
                pool_product(i)
            pe.wait_ge(s_tabs, 2)
            for n, (d, j) in enumerate(XDD_ORDER):
                pe.wait_ge(s_xdd, n + 1)
                if j == 0:
                    for i in range(8):
                        mm = pe.matmul(psb[2 + 2 * d + i // 4][:, (i % 4) * P:(i % 4 + 1) * P],
                                       xdd[:, n % 2, i * P:(i + 1) * P],
                                       btok[:, 0, (i // 4) * N:(i // 4 + 1) * N], start=True, stop=True)
                else:
                    if n < 4:
                        pe.wait_ge(s_u, 4)
                        pe.wait_ge(s_gs, 3)
                    else:
                        pe.wait_ge(s_st, n - 3)
                    for g in range(2):
                        mm = pe.matmul(psb[(6, 0)[n % 2] + g][:, :], btok[:, j, g * N:(g + 1) * N],
                                       xdd[:, n % 2, g * 512:(g + 1) * 512], start=True, stop=True)
                mm.then_inc(s_sp, 1)
                if 2 <= n < 6:
                    pool_product(n + 2)
            pe.wait_ge(s_st, 6)
            pe.wait_ge(s_u, 8)
            project_z(0, range(KT))

            def exponents(i):
                j, hh = i // HG, 2 * (i % HG)
                o = psb[4 + i % 2]
                if i >= 2:
                    pe.wait_ge(s_ex, i - 1)
                pe.matmul(o[:, :], idb[:, :], MASK4, start=True, stop=False, skip_group_check=True)
                o4 = o[:, :].rearrange("p (h d t) -> p h d t", h=2, d=2)
                for d in range(2):
                    c = d * H + hh
                    pe.matmul(o4[:, :, d, :], tabT[d][:, j * P:(j + 1) * P],
                              nstackb[:, c:c + 2].unsqueeze(2).to_broadcast([96, 2, P]), start=False, stop=False,
                              skip_group_check=True)
                for q in range(4):
                    h, d = hh + q // 2, q % 2
                    c = d * H + h
                    mm = pe.matmul(o[:, q * P:(q + 1) * P], stackb[:, c:c + 1].to_broadcast([96, P]),
                                   tabT[d][:, j * P:(j + 1) * P], start=False, stop=True,
                                   skip_group_check=True)
                mm.then_inc(s_e, 1)

            def diagonal(i):
                j, hh = i // HG, 2 * (i % HG)
                jg = 2 * j + hh // HG
                pe.wait_ge(s_w, i + 1)
                if hh == 0:
                    pe.wait_ge(s_xdt, j + 1)
                if hh % HG == 0 and jg >= 2:
                    pe.wait_ge(s_yc, jg - 1)
                for q in range(2):
                    h = hh + q
                    for d in range(2):
                        mm = pe.matmul(psb[jg % 2][:, (h % HG) * HD:(h % HG + 1) * HD],
                                       wbuf(i)[:, 2 * q + d, :], xdt[:, d, h * HD:(h + 1) * HD],
                                       start=(d == 0), stop=(d == 1))
                mm.then_inc(s_dg, 1)

            def from_states(jg):
                j, g = jg // 2, jg % 2
                if jg >= 3:
                    pe.wait_ge(s_yp, jg)
                for d in range(2):
                    si = j - 1 if d == 0 else 4 + j - 1
                    mm = pe.matmul(psb[2 + d][:, :], bcT[:, 2 + g, j * P:(j + 1) * P],
                                   st[:, si, g * 512:(g + 1) * 512], start=True, stop=True)
                mm.then_inc(s_off, 1)

            def turn_y(jg):
                pe.wait_ge(s_yc, jg + 1)
                if jg >= 1:
                    pe.wait_ge(s_yT, jg)
                for q in range(4):
                    k = 4 * (jg % 2) + q
                    mm = pe.transpose(psb[7][:, q * P:(q + 1) * P], xs[:, jg // 2, k * P:(k + 1) * P], ident)
                mm.then_inc(s_ytr, 1)

            NS = NJ * HG
            for i in range(NS + 2):
                if i < NS:
                    exponents(i)
                    if i % 4 and i // 4 + 1 < 2 * NJ:
                        project_z(i // 4 + 1, ((), range(0, 3), range(3, 6), range(6, 8))[i % 4])
                        if i // 4 + 1 >= 2 * NJ - 2 and i % 4 == 3:
                            pe.wait_ge(s_z, i // 4 + 2)
                            pe.sem_inc(s_used, 1)
                if i >= 2:
                    k = i - 2
                    diagonal(k)
                    if k % 4 == 0 and k // 4 >= 2:
                        from_states(k // 4)
                    if k % 4 == 1 and k // 4 >= 1:
                        turn_y(k // 4 - 1)

            def project_part(j, hf_, c):
                n = 2 * hf_ + c
                if j == 0:
                    if n == 3:
                        pe.wait_ge(s_wo3, 16)
                    else:
                        pe.wait_ge(s_ring[(11 + n) % RING], 16 * ((11 + n) // RING + 1))
                w = wo[n].rearrange("p (k c) -> p k c", k=KT)
                for k in range(KT):
                    mm = pe.matmul(psb[2 * c + hf_][:, :], (yT, uT)[c][:, k, j * P:(j + 1) * P], w[:, k, :],
                                   start=(k == 0), stop=(k == KT - 1))
                return mm

            def project_out(j, hf_):
                if j >= 1:
                    pe.wait_ge(s_x1, 2 * (j - 1) + hf_ + 1)
                if j or hf_:
                    project_part(j, hf_, 1)
                project_part(j, hf_, 0).then_inc(s_op, 1)

            pe.wait_ge(s_yp, 2 * NJ)
            project_part(0, 0, 1)
            turn_y(2 * NJ - 1)
            pe.wait_ge(s_yT, 2 * NJ)
            pe.wait_ge(s_wr, 16)

            def turn_h2(j):
                pe.wait_ge(s_h2, j + 1)
                if j >= 1:
                    pe.wait_ge(s_h2T, 2 * j)
                for k in range(KT):
                    mm = pe.transpose(psb[4 + k // 4][:, (k % 4) * P:(k % 4 + 1) * P],
                                      h2bufs[j % 2][:, k * P:(k + 1) * P], ident)
                mm.then_inc(s_h2t, 1)

            def router(j):
                pe.wait_ge(s_h2T, 2 * (j + 1))
                for k in range(KT):
                    mm = pe.matmul(psb[6][:, j * E:(j + 1) * E], h2T[:, k, :], wrt[:, k, :],
                                   start=(k == 0), stop=(k == KT - 1))
                mm.then_inc(s_lg, 1)

            def gate2(i):
                if i == 1:
                    pe.wait_ge(s_x1, 2 * NJ)
                pe.wait_ge(s_g2w[i], 16)
                w = w_g2[i].rearrange("p (k c) -> p k c", k=KT)
                for k in range(KT):
                    mm = pe.matmul(psb[(7, 3)[i]][0:2, :], silc[:, 2 * k:2 * k + 2], w[:, k, :],
                                   start=(k == 0), stop=(k == KT - 1))
                mm.then_inc(s_g2p, 1)

            for j in range(NJ):
                project_out(j, 0)
                if j >= 1:
                    turn_h2(j - 1)
                project_out(j, 1)
                if j >= 1:
                    router(j - 1)
            gate2(0)
            turn_h2(NJ - 1)
            router(NJ - 1)
            gate2(1)
            pe.wait_ge(s_oh, 2)
            for j in range(NJ):
                for i in range(j + 1):
                    pe.matmul(psb[0][:, j * E:(j + 1) * E], strictb[:, :] if i == j else onesb[:, :],
                              onehotb[:, i * E:(i + 1) * E], start=(i == 0), stop=(i == j))
            for i in range(NJ):
                mm = pe.matmul(psb[0][:, NJ * E:(NJ + 1) * E], onesb[:, :], onehotb[:, i * E:(i + 1) * E],
                               start=(i == 0), stop=(i == NJ - 1))
            mm.then_inc(s_rk, 1)

            pe.wait_ge(s_pos, 1)
            for i in range(2 * NJ):
                mm = pe.matmul(psb[5][:, 0:MAX_TILES], at_pos[:, i, :], in_tile[:, i, :],
                               start=(i == 0), stop=(i == 2 * NJ - 1))
            mm.then_inc(s_tk, 1)

            pe.wait_ge(s_rt, 1)
            k_tiles = pe.value_load(ri[0:1, 60:61], min_val=16, max_val=25)

            def turn_tokens():
                for k in range(KT):
                    mm = pe.transpose(psb[2 + k // 4][:, (k % 4) * P:(k % 4 + 1) * P],
                                      xg[:, k * P:(k + 1) * P], ident)
                mm.then_inc(s_xtp, 1)

            pe.wait_ge(s_xg, 16)
            turn_tokens()
            pe.sem_inc(s_dn, 2)
            with pe.Fori(0, k_tiles) as i:
                pe.wait_ge(s_xgT, i * 2 + 2)
                for c in range(FT):
                    pe.wait_ge(s_w_in[c], i * 16 + 16)
                    pe.wait_ge(s_ac, i * FT + (c + 1))
                    w = ex[:, c * 2048:(c + 1) * 2048].rearrange("p (a k f) -> p a k f", a=2, k=KT)
                    for a in range(2):
                        for k in range(KT):
                            mm = pe.matmul(psb[c % 2][:, a * P:(a + 1) * P], w[:, a, k, :], xgT[:, k, :],
                                           start=(k == 0), stop=(k == KT - 1))
                    mm.then_inc(s_gu, 1)
                pe.wait_ge(s_xg, i * 16 + 32)
                turn_tokens()
                pe.wait_ge(s_ac, i * FT + (FT + 2))
                pe.wait_ge(s_yo, i * 2 + 2)
                for c in range(2):
                    pe.wait_ge(s_w_in[FT + c], i * 16 + 16)
                    w = ex[:, (FT + c) * 2048:(FT + c + 1) * 2048].rearrange("p (k d) -> p k d", k=2)
                    for k in range(2):
                        for hf_ in range(2):
                            mm = pe.matmul(psb[6 + hf_][:, :], aT[:, 2 * c + k, :],
                                           w[:, k, hf_ * 512:(hf_ + 1) * 512],
                                           start=(c == 0 and k == 0), stop=(c == 1 and k == 1),
                                           skip_group_check=True)
                    mm.then_inc(s_dn, 1)

        @block.scalar
        def _(act):
            def rms(col, n=1):
                r = stat[:, col:col + n]
                act.activation(r, r, ACT.Sqrt, scale=1.0 / D, bias=eps_col[:, :]).then_inc(s_rs, 1)

            def warm(func):
                act.activation(stat[:, 26:27], eps_col[:, :], func)

            act.wait_ge(s_const, 64)
            act.activation(silc[:, :], vec[:, V_C:V_C + 16], ACT.Silu).then_inc(s_silc, 1)
            act.activation(nega[:, :], row[:, R_ALOG:R_ALOG + 32], ACT.Exp).then_inc(s_soft, 1)
            for j in range(NJ):
                act.wait_ge(s_x, 16 * NJ)
                act.activation(junk_x, xt[:, j, :], ACT.Square, accum_out=stat[:, j:j + 1]).then_inc(s_ss, 1)
                act.wait_ge(s_ss, j + 1)
            act.wait_ge(s_cast, 1)
            rms(0, NJ)
            for n in range(4):
                act.wait_ge(s_used, n + 1)
                act.activation(arow[:, n * 512:(n + 1) * 512], psb[n][0:2, :], ACT.Copy).then_inc(s_arc, 1)
            act.wait_ge(s_mod, 1)
            act.wait_ge(s_cast, 1)
            for k in range(KT):
                act.wait_ge(s_xtr, k + 1)
                act.activation(hT[:, k, CTX:TOK], psb[2 + 2 * (k % 3)][:, :], ACT.Identity,
                               bias=modB[:, 2 * k + 1:2 * k + 2], scale=modA[:, 2 * k + 1:2 * k + 2]).then_inc(s_hs, 1)
            act.wait_ge(s_soft, 2)
            act.activation(sc1, sc0, ACT.Exp, scale=-1.0).then_inc(s_soft, 1)
            act.wait_ge(s_soft, 4)
            act.activation(ncum, etot, ACT.Ln).then_inc(s_soft, 1)

            def silu_conv(f):
                act.wait_ge(s_conv, f + 1)
                t = f if f < 2 else f - 2
                dst = bcT[:, f, :] if f < 4 else xsT[t % 2]
                if f >= 6:
                    act.wait_ge(s_ttr, t - 1)
                act.activation(dst[:, 0:CTX], cacc[f % 2][:, 0:CTX], ACT.Silu, bias=vec[:, V_CB + f:V_CB + f + 1])
                act.activation(dst[:, CTX:TOK], cacc[f % 2][:, 131:643], ACT.Silu,
                               bias=vec[:, V_CB + f:V_CB + f + 1]).then_inc(s_cs, 1)

            def store_ada(q):
                act.wait_ge(s_adr, q + 1)
                for c in range(2):
                    act.dma_start(ada_rows[q // 2, c:c + 1, (q % 2) * 512:(q % 2 + 1) * 512],
                                  orow[:, c * 512:(c + 1) * 512]).then_inc(s_ads, 16)

            for f in range(20):
                if 3 <= f < 9:
                    store_ada(f - 3)
                act.wait_ge(s_fm, f + 1)
                q = 2 + 2 * (f % 3)
                if f < KT:
                    act.activation(uT[:, f, 0:CTX], psb[q + 1][:, 0:CTX], ACT.Copy)
                    act.activation(uT[:, f, CTX:TOK], psb[q][:, :], ACT.Copy).then_inc(s_vr, 1)
                else:
                    g = f - KT
                    if g == 0:
                        act.wait_ge(s_cast, 2)
                    if g >= 2:
                        act.wait_ge(s_conv, g - 1)
                    act.activation(xpad[g % 2][:, 1:1 + CTX], psb[q + 1][:, 0:CTX], ACT.Copy)
                    act.activation(xpad[g % 2][:, 132:132 + LAT], psb[q][:, :], ACT.Copy).then_inc(s_pad, 1)
                if f == 2:
                    act.wait_ge(s_dif, 1)
                    act.activation(ecum, ncum, ACT.Exp, scale=-1.0)
                    act.activation(dec, sc0, ACT.Exp)
                    act.activation(etot, sc1, ACT.Exp).then_inc(s_dec, 1)
                if f > KT:
                    silu_conv(f - 1 - KT)
            silu_conv(CONVF - 1)
            act.wait_ge(s_tok, 10)
            act.wait_ge(s_ads, 192)
            for d in range(2):
                act.dma_start(st[:, 0 if d == 0 else 7, :], states0[d]).then_inc(s_st0, 16)
            act.wait_ge(s_g, 1)
            gv = gT[:, :, :, :].rearrange("p j g n -> p (j g n)")
            act.activation(gv[:, 1024:1280], psb[1][:, 0:256], ACT.Copy).then_inc(s_gs, 1)
            act.activation(gv[:, 0:512], psb[6][:, :], ACT.Copy).then_inc(s_gs, 1)
            act.activation(gv[:, 512:1024], psb[7][:, :], ACT.Copy).then_inc(s_gs, 1)
            def scale_pooled(i):
                act.wait_ge(s_pm, i + 1)
                scale = vec[:, V_PS + i:V_PS + i + 1]
                ctx_in, lat_in = pooled_banks(i)
                if i % 2 == 0:
                    act.wait_ge(s_pm, i + 2)
                act.activation(uT[:, i, 0:CTX], ctx_in, ACT.Copy, scale=scale)
                act.activation(uT[:, i, CTX:TOK], lat_in, ACT.Copy, scale=scale).then_inc(s_u, 1)

            for i in range(4):
                scale_pooled(i)
            for n, (d, j) in enumerate(XDD_ORDER):
                if j == 0:
                    act.wait_ge(s_sp, n + 1)
                    for i in range(2):
                        act.activation(sout[d][:, i * 512:(i + 1) * 512], psb[2 + 2 * d + i][:, :],
                                       ACT.Copy).then_inc(s_so, 1)
                    act.wait_ge(s_so, 2 * (d + 1))
                    act.dma_start(s_out[d].rearrange("(i p) n -> p i n", p=P), sout[d].rearrange("p (i n) -> p i n", n=N)).then_inc(s_sout, 16)
            for i in range(4, 8):
                scale_pooled(i)

            def tanh_z(jg):
                act.wait_ge(s_z, jg + 1)
                if jg >= 2:
                    act.wait_ge(s_yc, jg - 1)
                act.activation(zbuf[jg % 2], psb[6][:, :], ACT.Tanh, scale=0.5).then_inc(s_zt, 1)

            def exps(i):
                j, hh = i // HG, 2 * (i % HG)
                act.wait_ge(s_e, i + 1)
                if i >= 3:
                    act.wait_ge(s_dg, i - 2)
                act.activation(wbuf(i)[:, :, :], psb[4 + i % 2][:, :].rearrange("p (q t) -> p q t", q=4),
                               ACT.Exp).then_inc(s_ex, 1)

            def square_y(jg):
                act.wait_ge(s_yc, jg + 1)
                if jg >= 1:
                    act.wait_ge(s_ys, jg)
                act.activation(junk_y, xs[:, jg // 2, (jg % 2) * 512:(jg % 2 + 1) * 512], ACT.Square,
                               accum_out=stat[:, 16 + jg:17 + jg]).then_inc(s_ys, 1)

            for i in range(NJ * HG):
                exps(i)
                if i % 4 == 0:
                    tanh_z(i // 4)
                if i % 4 == 3 and i >= 4:
                    square_y(i // 4 - 1)
            square_y(2 * NJ - 1)
            warm(ACT.Sqrt)
            act.wait_ge(s_yss, 1)
            rms(5, NJ)

            act.dma_start(wrt[:, :, :], w_router.rearrange("p (k e) -> p k e", k=KT)).then_inc(s_wr, 16)
            act.wait_ge(s_ytr, 2 * NJ)
            act.wait_ge(s_ys, 2 * NJ)
            for j in range(NJ):
                act.dma_start(x1[:, j, :], x[j * P:(j + 1) * P, :]).then_inc(s_xr, 16)
            act.wait_ge(s_off, 2 * (NJ - 1))
            act.dma_start(g1row, ada_rows[0:1].to_broadcast([P, 2, D])).then_inc(s_rowl, 16)
            act.wait_ge(s_yc, 2 * NJ)
            act.dma_start(a2row, ada_rows[2:3].to_broadcast([P, 2, D])).then_inc(s_rowl, 16)
            act.dma_start(b2row, ada_rows[1:2].to_broadcast([P, 2, D])).then_inc(s_row2, 16)

            def copy_h2(j):
                act.wait_ge(s_h2t, j + 1)
                if j >= 1:
                    act.wait_ge(s_lg, j)
                act.activation(h2T[:, 0:4, :], psb[4][:, :].rearrange("p (k t) -> p k t", k=4),
                               ACT.Copy).then_inc(s_h2T, 1)
                act.dma_start(h2_dram[j * P:(j + 1) * P, :], h2bufs[j % 2]).then_inc(s_h2s[j % 2], 16)

            def exp_logits(part):
                act.wait_ge(s_lm, part + 1)
                lo, hi = (0, (NJ - 2) * E, NJ * E)[part:part + 2]
                act.activation(n_ex[:, lo:hi], n_sh[:, lo:hi], ACT.Exp).then_inc(s_le, 1)

            for j in range(NJ):
                if j == NJ - 1:
                    exp_logits(0)
                    warm(ACT.Sqrt)
                if j >= 1:
                    copy_h2(j - 1)
                act.wait_ge(s_x1, 2 * (j + 1))
                act.activation(junk_1, x1[:, j, :], ACT.Square, accum_out=stat[:, 10 + j:11 + j]).then_inc(s_x1s, 1)
                act.wait_ge(s_x1s, j + 1)
                rms(10 + j)
            warm(ACT.Exp)
            copy_h2(NJ - 1)
            act.dma_start(fnrow, fnorm.to_broadcast([P, D])).then_inc(s_fn, 16)
            act.dma_start(g2b, b_late[6:8, :].unsqueeze(0).to_broadcast([2, 2, 512])).then_inc(s_g2b, 16)
            exp_logits(1)
            warm(ACT.Silu)
            act.wait_ge(s_g2c, 2)
            act.dma_start(ada_rows[3, :, :].rearrange("c (i n) -> c i n", n=512), g2s).then_inc(s_g2d, 16)
            act.wait_ge(s_g2d, 16)
            act.dma_start(g2row, ada_rows[3:4].to_broadcast([P, 2, D])).then_inc(s_row2, 16)

            act.wait_ge(s_rt, 1)
            k_tiles = act.value_load(ri[0:1, 60:61], min_val=16, max_val=25)

            def copy_tokens(n):
                act.wait_ge(s_xtp, n)
                act.activation(xgT[:, 0:4, :], psb[2][:, :].rearrange("p (k t) -> p k t", k=4),
                               ACT.Copy).then_inc(s_xgT, 1)

            copy_tokens(1)
            act.sem_inc(s_yo, 2)
            act.sem_inc(s_yst, 16)
            with act.Fori(0, k_tiles) as i:
                for c in range(FT):
                    act.wait_ge(s_gu, i * FT + (c + 1))
                    act.wait_ge(s_ac, i * FT + (c + 1))
                    act.activation(sg[c % 2], psb[c % 2][:, 0:P], ACT.Silu).then_inc(s_sg, 1)
                copy_tokens(i + 2)
                act.wait_ge(s_dn, i * 2 + 4)
                act.wait_ge(s_yst, i * 16 + 16)
                act.activation(yo[:, 0:512], psb[6][:, :], ACT.Copy).then_inc(s_yo, 1)
                act.wait_ge(s_yo, i * 2 + 4)
                act.dma_start(slot_out[bass.ds(i * P, P), :], yo).then_inc(s_yst, 16)
            warm(ACT.Sqrt)
            act.wait_ge(s_yst, k_tiles * 16 + 16)

            def weigh(j):
                act.wait_ge(s_yg[j], 32)
                ya = ygb[:, 2 * j, :]
                act.activation(ya, ya, ACT.Copy, scale=gate[:, j:j + 1]).then_inc(s_ya, 1)

            weigh(0)
            for j in range(NJ):
                if j + 1 < NJ:
                    weigh(j + 1)
                act.wait_ge(s_fin, j + 1)
                act.activation(junk_z, x1[:, j, :], ACT.Square, accum_out=stat[:, j:j + 1]).then_inc(s_fss, 1)
                act.wait_ge(s_fss, j + 1)
                rms(j)

        @block.gpsimd
        def _(pool):
            step = Steps(pool, s_pool)
            pool.wait_ge(s_const, 64)
            pool.tensor_copy(idb[:, :], ident)
            pool.tensor_copy(maskb[:, :, :], bcst[:, B_MASK:B_MASK + 256].rearrange("p (a b) -> p a b", a=2))
            pool.tensor_copy(strictb[:, :], bcst[:, B_STRICT:B_STRICT + P])
            pool.tensor_copy(onesb[:, :], ones)
            pool.tensor_copy(stackb[:, :], bcst[0:96, B_STACK:B_STACK + 32])
            pool.tensor_scalar(nstackb[:, :], bcst[0:96, B_STACK:B_STACK + 32], -1.0, None, ALU.mult)
            pool.memset(zero_f, 0.0)
            pool.memset(eps_col[:, :], EPS)
            pool.tensor_tensor(dsum[:, :], row[:, R_DSK:R_DSK + H], row[:, R_DSK + H:R_DSK + 2 * H],
                               ALU.add).then_inc(s_cast, 1)
            pool.wait_ge(s_hs, KT)
            pool.wait_ge(s_hc, KT)
            pool.memset(xpad[0], 0.0)
            pool.memset(xpad[1], 0.0).then_inc(s_cast, 1)
            pool.wait_ge(s_cast, 1)
            for t in range(E, MAX_TILES - 1):
                pool.dma_start(slot_out[t * P:(t + 1) * P, :], zero_f).then_inc(s_zero, 16)

            pool.wait_ge(s_inv, 16)
            iv = [(invb[:, g * TOK:g * TOK + CTX], invb[:, g * TOK + CTX:(g + 1) * TOK]) for g in range(4)]
            for f in range(8):
                g = f // 2
                w = WINDOWS[g]
                lw = g + 1
                v = uT[:, f, :]
                pool.wait_ge(s_vr, f + 1)
                L = CTX + w - 1
                step(pool.memset(pa[:, 0:L], 0.0))
                step(pool.tensor_copy(pa[:, w // 2:w // 2 + CTX], v[:, 0:CTX]))
                src, dst = pa, pb_
                for q in range(lw):
                    L -= 1 << q
                    step(pool.tensor_tensor(dst[:, 0:L], src[:, 0:L], src[:, (1 << q):(1 << q) + L], ALU.add))
                    src, dst = dst, (pc if dst is pb_ else pb_)
                step(pool.tensor_tensor(dst[:, 0:CTX], src[:, 0:CTX], iv[g][0], ALU.mult))
                step(pool.tensor_tensor(uT[:, f, 0:CTX], dst[:, 0:CTX], v[:, 0:CTX], ALU.subtract))
                L = GRID_W + w - 1

                def grid(b, n, ww=None):
                    ww = ww or L0
                    return b[:, 0:n * ww].rearrange("p (r c) -> p r c", r=n)

                L0 = L
                vg = v[:, CTX:TOK].rearrange("p (r c) -> p r c", r=ROWS)
                step(pool.memset(pa[:, 0:ROWS * L0], 0.0))
                step(pool.tensor_copy(grid(pa, ROWS)[:, :, w // 2:w // 2 + GRID_W], vg))
                src, dst = pa, pb_
                for q in range(lw):
                    L -= 1 << q
                    s3, d3 = grid(src, ROWS), grid(dst, ROWS)
                    step(pool.tensor_tensor(d3[:, :, 0:L], s3[:, :, 0:L], s3[:, :, (1 << q):(1 << q) + L], ALU.add))
                    src, dst = dst, (pc if dst is pb_ else pb_)
                col = grid(src, ROWS)[:, :, 0:GRID_W]
                if w // 2 >= ROWS:
                    n = ROWS // 2
                    s3 = col
                    while n:
                        d3 = grid(dst, n, GRID_W)
                        step(pool.tensor_tensor(d3, s3[:, 0:n, :], s3[:, n:2 * n, :], ALU.add))
                        s3 = d3
                        src, dst = dst, (pc if dst is pb_ else pb_)
                        n //= 2
                    total = s3.to_broadcast([P, ROWS, GRID_W])
                else:
                    n = ROWS + w - 1
                    step(pool.memset(pa[:, 0:n * GRID_W], 0.0))
                    step(pool.tensor_copy(grid(pa, n, GRID_W)[:, w // 2:w // 2 + ROWS, :], col))
                    src, dst = pa, pb_
                    for q in range(lw):
                        n -= 1 << q
                        s1, d1 = src[:, 0:(n + (1 << q)) * GRID_W], dst[:, 0:n * GRID_W]
                        step(pool.tensor_tensor(d1, s1[:, 0:n * GRID_W], s1[:, (1 << q) * GRID_W:], ALU.add))
                        src, dst = dst, (pc if dst is pb_ else pb_)
                    total = grid(src, ROWS, GRID_W)
                m3 = grid(dst, ROWS, GRID_W)
                step(pool.tensor_tensor(m3, total, iv[g][1].rearrange("p (r c) -> p r c", r=ROWS), ALU.mult))
                pool.tensor_tensor(uT[:, f, CTX:TOK].rearrange("p (r c) -> p r c", r=ROWS), m3, vg,
                                   ALU.subtract).then_inc(s_pu, 1)
                pool.wait_ge(s_pu, f + 1)
            pool.wait_ge(s_adr, 6)
            pool.dma_start(gT_pw, w_pool.rearrange("p (g k m) -> p g k m", g=4, k=2)).then_inc(s_pw, 16)

            def scaled(out, j, factors):
                return pool.tensor_tensor(out.rearrange("p (h d) -> p h d", d=HD),
                                          xs[:, j, :].rearrange("p (h d) -> p h d", d=HD),
                                          factors.unsqueeze(2).to_broadcast([P, H, HD]), ALU.mult)

            pool.wait_ge(s_tok, 10)
            pool.wait_ge(s_dtd, 1)
            for n, (d, j) in enumerate(XDD_ORDER):
                if n >= 2:
                    pool.wait_ge(s_sp, n - 1)
                c = j * 32 + d * H
                scaled(xdd[:, n % 2, :], j, dtdec[:, c:c + H]).then_inc(s_xdd, 1)
            for j in range(NJ):
                if j == 0:
                    pool.wait_ge(s_tabs, 2)
                    pool.wait_ge(s_adr, 6)
                    pool.wait_ge(s_ads, 192)
                else:
                    pool.wait_ge(s_dg, j * HG)
                for d in range(2):
                    c = j * 32 + d * H
                    ins = scaled(xdt[:, d, :], j, dt_[:, c:c + H])
                ins.then_inc(s_xdt, 1)

            pool.wait_ge(s_rt, 1)
            pool.wait_ge(s_h2s[0], 48)
            pool.wait_ge(s_h2s[1], 32)
            k_tiles = pool.value_load(ri[0:1, 60:61], min_val=16, max_val=25)

            def gather():
                pool.indirect_dma_start(xg, None, h2_dram,
                                        bass.IndirectOffsetOnAxis(ap=idx[:, 0:1], axis=0),
                                        bounds_check=TOK - 1, oob_is_err=False).then_inc(s_xg, 16)

            pool.tensor_copy(idx[:, 0:1], token_of[:, 0:1]).then_inc(s_idx, 1)
            pool.wait_ge(s_idx, 1)
            gather()
            with pool.Fori(0, k_tiles) as i:
                pool.wait_ge(s_xg, i * 16 + 16)
                pool.sem_inc(s_begun, 1)
                pool.tensor_copy(idx[:, 0:1], token_of[:, bass.ds(i + 1, 1)]).then_inc(s_idx, 1)
                pool.wait_ge(s_idx, i + 2)
                pool.wait_ge(s_xtp, i + 1)
                pool.sem_inc(s_begun, 1)
                gather()
            pool.wait_ge(s_yst, k_tiles * 16 + 16)
            pool.sem_inc(s_begun, 1)
            pool.wait_ge(s_zero, 16 * (MAX_TILES - 1 - E))
            for j in range(NJ):
                for a in range(2):
                    n = 2 * j + a
                    pool.indirect_dma_start(ygb[:, n, :], None, slot_out,
                                            bass.IndirectOffsetOnAxis(ap=ri[:, 40 + a * NJ + j:41 + a * NJ + j], axis=0),
                                            bounds_check=SLOTS - P - 1, oob_is_err=False).then_inc(s_yg[j], 16)

        @block.vector
        def _(dve):
            step = Steps(dve, s_dve)
            tt, ts, stt = dve.tensor_tensor, dve.tensor_scalar, dve.scalar_tensor_tensor
            dve.wait_ge(s_const, 64)
            dve.wait_ge(s_rs, 1)
            step(dve.reciprocal(stat[:, 0:NJ], stat[:, 0:NJ]))
            for j in range(NJ):
                ts(xt[:, j, :], xt[:, j, :], stat[:, j:j + 1], None, ALU.mult).then_inc(s_xn, 1)
            dve.wait_ge(s_ar, 1)
            tt(modB[:, :], psb[4][:, 0:16], vec[:, V_ADA:V_ADA + 16], ALU.add)
            step(tt(modA[:, :], psb[4][:, 16:32], vec[:, V_ADA + 16:V_ADA + 32], ALU.add))
            stt(modA[:, :], modA[:, :], 1.0, vec[:, V_N1:V_N1 + 16], ALU.add, ALU.mult).then_inc(s_mod, 1)
            dve.wait_ge(s_mod, 1)
            for k in range(KT):
                dve.wait_ge(s_xtr, k + 1)
                ts(hT[:, k, 0:CTX], psb[3 + 2 * (k % 3)][:, 0:CTX], modA[:, 2 * k:2 * k + 1], modB[:, 2 * k:2 * k + 1],
                   ALU.mult, ALU.add).then_inc(s_hc, 1)
            dve.wait_ge(s_dtp, 1)
            step(tt(dt_.rearrange("p (j h) -> p j h", j=NJ), psb[1][:, 0:160].rearrange("p (j h) -> p j h", j=NJ),
                    row[:, R_DTB:R_DTB + 32].unsqueeze(1).to_broadcast([P, NJ, 32]), ALU.add))
            dve.wait_ge(s_soft, 1)
            step(ts(sc0, dt_, -1.0, None, ALU.mult))
            tt(sc0, sc0, dt_, ALU.max).then_inc(s_soft, 1)
            dve.wait_ge(s_soft, 2)
            step(ts(dt_, dt_, 0.0, None, ALU.max))
            dve.wait_ge(s_soft, 3)
            ts(etot, sc1, 1.0, None, ALU.add).then_inc(s_soft, 1)
            dve.wait_ge(s_soft, 4)
            step(ts(sc0, etot, -1.0, None, ALU.add))
            step(tt(sc0, sc1, sc0, ALU.subtract))
            step(dve.reciprocal(sc1, etot))
            step(tt(sc0, sc0, sc1, ALU.mult))
            dve.wait_ge(s_soft, 5)
            step(tt(sc0, sc0, ncum, ALU.add))
            step(tt(dt_, dt_, sc0, ALU.add))
            step(tt(a_.rearrange("p (j h) -> p j h", j=NJ), dt_.rearrange("p (j h) -> p j h", j=NJ),
                    nega[:, :].unsqueeze(1).to_broadcast([P, NJ, 32]), ALU.mult))
            ts(a_, a_, -1.0, None, ALU.mult).then_inc(s_a, 1)
            def ada_half(u):
                q = u // 2
                if u % 2 == 0 and q >= 2:
                    dve.wait_ge(s_ada, q - 1)
                dve.wait_ge(s_adaw[u % 2], 16 * (u // 2 + 1))
                for kk in range(4):
                    k = 4 * (u % 2) + kk
                    for c in range(2):
                        a = acc[q % 2][:, c * 512:(c + 1) * 512]
                        w, s_c = adaw[u % 2][:, kk, :], silc[:, 2 * k + c:2 * k + c + 1]
                        if k:
                            dve.wait_ge(s_accs, 16 * q + 2 * k + c - 1)
                            ins = stt(a, w, s_c, a, ALU.mult, ALU.add)
                        else:
                            ins = ts(a, w, s_c, None, ALU.mult)
                        ins.then_inc(s_accs, 1)
                dve.wait_ge(s_accs, 16 * q + 8 * (u % 2) + 8)
                dve.sem_inc(s_acc, 1)

            def ada_rows_out(q):
                dve.wait_ge(s_ada, q + 1)
                dve.wait_ge(s_brow, 16 * (q + 1))
                if q >= 1:
                    dve.wait_ge(s_ads, 32 * q)
                for c in range(2):
                    o = orow[:, c * 512:(c + 1) * 512]
                    ins = tt(o, psb[c][0:1, :], brow, ALU.add)
                    if q // 2 == 2:
                        step(ins)
                        dve.wait_ge(s_n2, 16)
                        ins = stt(o, o, 1.0, n2row[:, (q % 2) * 512:(q % 2 + 1) * 512], ALU.add, ALU.mult)
                ins.then_inc(s_adr, 1)

            dve.wait_ge(s_silc, 1)
            ada_half(0)
            ada_half(1)
            dve.wait_ge(s_cum, 1)
            step(ts(ncum, psb[0][:, 0:160], -1.0, None, ALU.mult))
            tt(sc0, psb[0][:, 160:320], ncum, ALU.add)
            dve.tensor_copy(sc1, psb[0][:, 160:320]).then_inc(s_dif, 1)

            dve.wait_ge(s_dec, 1)
            tt(dtdec, dt_, dec, ALU.mult).then_inc(s_dtd, 1)
            for q in range(1, 6):
                ada_half(2 * q)
                ada_rows_out(q - 1)
                ada_half(2 * q + 1)
            ada_rows_out(5)

            dve.wait_ge(s_zero, 16 * (MAX_TILES - 1 - E))

            def token_major(t):
                dve.wait_ge(s_ttr, t + 1)
                dst = btok[:, :, t * N:(t + 1) * N] if t < 2 else xs[:, :, (t - 2) * P:(t - 1) * P]
                dve.tensor_copy(dst[:, 0, :], psb[1][:, 0:P])
                dve.tensor_copy(dst[:, 1:NJ, :], psb[0][:, :].rearrange("p (j n) -> p j n", n=P)).then_inc(s_tok, 1)

            for f in range(CONVF):
                dve.wait_ge(s_pad, f + 1)
                if f >= 2:
                    dve.wait_ge(s_cs, f - 1)
                for q in range(4):
                    wq = vec[:, V_CW + 4 * f + q:V_CW + 4 * f + q + 1]
                    if q == 0:
                        step(ts(cacc[f % 2], xpad[f % 2][:, 0:643], wq, None, ALU.mult))
                    else:
                        ins = stt(cacc[f % 2], xpad[f % 2][:, q:q + 643], wq, cacc[f % 2], ALU.mult, ALU.add)
                        if q < 3:
                            step(ins)
                        else:
                            ins.then_inc(s_conv, 1)
                if f == 4:
                    token_major(0)
                if f >= 5:
                    token_major(f - 4)
            token_major(8)
            token_major(9)
            for d in range(2):
                dve.wait_ge(s_tab, d + 1)
                dve.wait_ge(s_g, 1)
                t = tabT[d]
                for lo, hi, src in ((0, CTX, psb[3 + 2 * d][0:32, 0:CTX]), (CTX, TOK, psb[2 + 2 * d][0:32, :])):
                    if d == 0 and lo == 0:
                        dve.wait_ge(s_ads, 192)
                    r1, r2 = split_r[0][:, lo:hi], split_r[1][:, lo:hi]
                    step(dve.tensor_copy(t[0:32, lo:hi], src))
                    step(tt(r1, src, t[0:32, lo:hi], ALU.subtract))
                    step(dve.tensor_copy(mid[:, lo:hi], r1))
                    step(dve.tensor_copy(t[32:64, lo:hi], mid[:, lo:hi]))
                    step(tt(r2, r1, mid[:, lo:hi], ALU.subtract))
                    ins = dve.tensor_copy(t[64:96, lo:hi], r2)
                    if lo == 0:
                        step(ins)
                ins.then_inc(s_tabs, 1)
                dve.wait_ge(s_tabs, d + 1)
            dve.wait_ge(s_dec, 1)
            dve.wait_ge(s_st0, 32)
            dve.wait_ge(s_pu, 8)

            def heads(ap):
                return ap.rearrange("p (h d) -> p h d", d=HD)

            def state(n):
                d, j = XDD_ORDER[n]
                if j == 0:
                    return
                dve.wait_ge(s_sp, n + 1)
                b = (6, 0)[n % 2]
                si = j - 1 if d == 0 else 4 + j - 1
                so = si + 1 if d == 0 else si - 1
                c = j * 32 + d * H
                step(tt(heads(st[:, so, :]), heads(st[:, si, :]),
                        etot[:, c:c + H].unsqueeze(2).to_broadcast([P, H, HD]), ALU.mult))
                tt(st[:, so, 0:512], st[:, so, 0:512], psb[b][:, :], ALU.add)
                ins = tt(st[:, so, 512:1024], st[:, so, 512:1024], psb[b + 1][:, :], ALU.add)
                ins.then_inc(s_st, 1)
                dve.wait_ge(s_st, n - 1)

            for n in range(len(XDD_ORDER)):
                state(n)

            def decay_scores(i):
                j, hh = i // HG, 2 * (i % HG)
                dve.wait_ge(s_ex, i + 1)
                if i == 0:
                    dve.wait_ge(s_gs, 3)
                tt(wbuf(i)[:, :, :], wbuf(i)[:, :, :],
                   gT[:, j, hh // HG, :].unsqueeze(1).to_broadcast([P, 4, P]), ALU.mult).then_inc(s_w, 1)

            def silu_z(jg):
                dve.wait_ge(s_zt, jg + 1)
                stt(zbuf[jg % 2], zbuf[jg % 2], 1.0, psb[6][:, :], ALU.add, ALU.mult).then_inc(s_zs, 1)

            def per_head(ap):
                return ap.unsqueeze(2).to_broadcast([P, HG, HD])

            def begin_outputs(jg):
                j, g = jg // 2, jg % 2
                c = j * 32 + g * HG
                ins = tt(heads(yt[0]), heads(xs[:, j, g * 512:(g + 1) * 512]), per_head(dsum[:, g * HG:(g + 1) * HG]), ALU.mult)
                if j:
                    step(ins)
                    dve.wait_ge(s_off, jg - 1)
                    for d in range(2):
                        step(tt(heads(yt[1]), heads(psb[2 + d][:, :]), per_head(ecum[:, c + d * H:c + d * H + HG]),
                                ALU.mult))
                        ins = tt(yt[0], yt[0], yt[1], ALU.add)
                        if d == 0:
                            step(ins)
                ins.then_inc(s_yp, 1)

            def end_outputs(jg):
                j, g = jg // 2, jg % 2
                dve.wait_ge(s_yp, jg + 1)
                dve.wait_ge(s_dg, 4 * (jg + 1))
                step(tt(yt[0], yt[0], psb[jg % 2][:, :], ALU.add))
                dve.wait_ge(s_zs, jg + 1)
                stt(xs[:, j, g * 512:(g + 1) * 512], yt[0], 0.5, zbuf[jg % 2], ALU.mult, ALU.mult).then_inc(s_yc, 1)
                dve.wait_ge(s_yc, jg + 1)

            def copy_y(jg):
                if jg == 0:
                    dve.wait_ge(s_sout, 32)
                dve.wait_ge(s_ytr, jg + 1)
                j, k = jg // 2, 4 * (jg % 2)
                tt(yT[:, k:k + 4, j * P:(j + 1) * P], psb[7][:, :].rearrange("p (k t) -> p k t", k=4),
                   vec[:, V_SN + k:V_SN + k + 4].unsqueeze(2).to_broadcast([P, 4, P]), ALU.mult).then_inc(s_yT, 1)

            for i in range(NJ * HG):
                decay_scores(i)
                if i % 4 == 0:
                    silu_z(i // 4)
                    if i >= 8:
                        copy_y(i // 4 - 2)
                if i % 4 == 1 and i >= 4:
                    end_outputs(i // 4 - 1)
                if i % 4 == 3:
                    begin_outputs(i // 4)
            copy_y(2 * NJ - 2)
            end_outputs(2 * NJ - 1)
            dve.wait_ge(s_ys, 2 * NJ)
            sums = stat[:, 16:26].rearrange("p (j g) -> p j g", g=2)
            tt(stat[:, 5:10].unsqueeze(2), sums[:, :, 0:1], sums[:, :, 1:2], ALU.add).then_inc(s_yss, 1)
            copy_y(2 * NJ - 1)
            dve.wait_ge(s_rs, 2)
            step(dve.reciprocal(stat[:, 5:10], stat[:, 5:10]))

            dve.wait_ge(s_rowl, 32)
            dve.wait_ge(s_xr, 16 * NJ)

            def h2_copy(j):
                dve.wait_ge(s_h2t, j + 1)
                if j >= 1:
                    dve.wait_ge(s_lg, j)
                dve.tensor_copy(h2T[:, 4:8, :], psb[5][:, :].rearrange("p (k t) -> p k t", k=4)).then_inc(s_h2T, 1)

            room = [rw_a, 160]

            def new(*shape):
                n = int(np.prod(shape))
                room[1] += n
                v = room[0][:, room[1] - n:room[1]]
                return v if len(shape) == 1 else v.rearrange("p (a b) -> p a b", b=shape[1])

            def over(ap, n):
                return ap.unsqueeze(2).to_broadcast([P, ap.shape[1], n])

            def across(ap, n):
                return ap.unsqueeze(1).to_broadcast([P, n, ap.shape[1]])

            def largest(out, in_):
                step(dve.tensor_reduce(out, in_, AX_X, ALU.max))

            def total(out, in_):
                step(dve.tensor_reduce(out, in_, AX_X, ALU.add))

            chosen, weight, norm = [new(NJ, E), new(NJ, E)], [new(NJ), new(NJ)], new(NJ)
            scratch_from = room[1]

            def choose(j0, j1):
                nj = j1 - j0
                room[1] = scratch_from

                def je(ap):
                    return ap[:, j0 * E:j1 * E].rearrange("p (j e) -> p j e", e=E)

                dve.wait_ge(s_lg, j1)
                logits = je(psb[6])
                top = new(nj)
                largest(top, logits)
                tt(je(n_sh), logits, over(top, E), ALU.subtract).then_inc(s_lm, 1)
                dve.wait_ge(s_le, 2 if j0 else 1)
                probs, sel, tot = new(nj, E), new(nj, E), new(nj)
                total(tot, je(n_ex))
                step(dve.reciprocal(tot, tot))
                step(tt(probs, je(n_ex), over(tot, E), ALU.mult))
                step(tt(sel, probs, across(row[:, R_RB:R_RB + E], nj), ALU.add))
                s4 = sel.rearrange("p j (g e) -> p (j g) e", g=EG)
                pairs = new(nj * EG, 6)
                tt(pairs[:, :, 0:3], s4[:, :, 0:3], s4[:, :, 1:4], ALU.add)
                tt(pairs[:, :, 3:5], s4[:, :, 0:2], s4[:, :, 2:4], ALU.add)
                step(tt(pairs[:, :, 5:6], s4[:, :, 0:1], s4[:, :, 3:4], ALU.add))
                score, pick, in_group = new(nj * EG), new(nj, EG), new(nj, EG)
                largest(score, pairs)
                s5 = score.rearrange("p (j g) -> p j g", g=EG)
                largest(top, s5)
                step(tt(pick, s5, over(top, EG), ALU.is_equal))
                step(tt(pick, pick, across(cst[:, C_P4:C_P4 + EG], nj), ALU.mult))
                largest(top, pick)
                step(tt(in_group, pick, over(top, EG), ALU.is_equal))
                low, cand = new(nj * EG), new(nj, E)
                ing = in_group.rearrange("p j g -> p (j g)")
                step(ts(low, ing, BIG, -BIG, ALU.mult, ALU.add))
                c4 = cand.rearrange("p j (g e) -> p (j g) e", g=EG)
                step(tt(c4, s4, over(ing, EPG), ALU.mult))
                step(tt(c4, c4, over(low, EPG), ALU.add))
                prio = new(nj, E)
                for a in range(2):
                    ch = chosen[a][:, j0:j1, :]
                    largest(top, cand)
                    step(tt(prio, cand, over(top, E), ALU.is_equal))
                    step(tt(prio, prio, across(cst[:, C_P16:C_P16 + E], nj), ALU.mult))
                    largest(top, prio)
                    step(tt(ch, prio, over(top, E), ALU.is_equal))
                    if a == 0:
                        step(stt(cand, ch, -3 * BIG, cand, ALU.mult, ALU.add))
                tt(je(onehotb), chosen[0][:, j0:j1, :], chosen[1][:, j0:j1, :], ALU.add).then_inc(s_oh, 1)
                for a in range(2):
                    step(tt(prio, chosen[a][:, j0:j1, :], probs, ALU.mult))
                    total(weight[a][:, j0:j1], prio)

            for j in range(NJ):
                cd = min(j, 1)
                if j == NJ - 1:
                    choose(0, NJ - 2)
                for hf_ in range(2):
                    cols = slice(hf_ * 512, (hf_ + 1) * 512)
                    n = 2 * j + hf_
                    if hf_ and j >= 1:
                        h2_copy(j - 1)
                    dve.wait_ge(s_op, n + 1)
                    step(dve.tensor_copy(x1t, psb[2 + hf_][:, :]))
                    step(stt(x1t, psb[hf_][:, :], stat[:, 5 + j:6 + j], x1t, ALU.mult, ALU.add))
                    step(tt(x1t, x1t, g1row[:, cd, cols], ALU.mult))
                    tt(x1[:, j, cols], x1[:, j, cols], x1t, ALU.add).then_inc(s_x1, 1)
                    dve.wait_ge(s_x1, n + 1)
                if j == 0:
                    dve.wait_ge(s_row2, 16)
                dve.wait_ge(s_rs, 3 + j)
                r = stat[:, 10 + j:11 + j]
                step(dve.reciprocal(r, r))
                if j >= 2:
                    dve.wait_ge(s_h2s[j % 2], 16 * (j // 2))
                    dve.wait_ge(s_h2t, j - 1)
                step(stt(h2bufs[j % 2], x1[:, j, :], r, a2row[:, cd, :], ALU.mult, ALU.mult))
                tt(h2bufs[j % 2], h2bufs[j % 2], b2row[:, cd, :], ALU.add).then_inc(s_h2, 1)
                dve.wait_ge(s_h2, j + 1)

            h2_copy(NJ - 1)
            choose(NJ - 2, NJ)
            room[:] = [rw_b, 0]
            step(tt(norm, weight[0], weight[1], ALU.add))
            step(dve.reciprocal(norm, norm))
            for a in range(2):
                step(tt(gate[:, a * NJ:(a + 1) * NJ], weight[a], norm, ALU.mult))
            dve.wait_ge(s_g2b, 16)
            for i in range(2):
                dve.wait_ge(s_g2p, i + 1)
                tt(g2s[:, i, :], psb[(7, 3)[i]][0:2, :], g2b[:, i, :], ALU.add).then_inc(s_g2c, 1)
            dve.wait_ge(s_rk, 1)
            tiles, ends, base, steps = new(E), new(E), new(E), new(E, 4)
            step(tt(steps, over(psb[0][:, NJ * E:(NJ + 1) * E], 4), across(cst[:, C_STEP:C_STEP + 4], E), ALU.is_gt))
            total(tiles, steps)
            step(ts(tiles, tiles, 1.0, None, ALU.add))
            step(dve.tensor_tensor_scan(ends, ones[:, 0:E], tiles, 0.0, ALU.mult, ALU.add))
            step(tt(base, ends, tiles, ALU.subtract))
            step(ts(base, base, float(P), None, ALU.mult))
            slots, mine, place = new(NJ, E), new(NJ, E), new(2 * NJ)
            step(tt(slots, psb[0][:, 0:NJ * E].rearrange("p (j e) -> p j e", e=E), across(base, NJ), ALU.add))
            for a in range(2):
                step(tt(mine, chosen[a], slots, ALU.mult))
                total(place[:, a * NJ:(a + 1) * NJ], mine)
            reached, tile_of, pos = new(2 * NJ, MAX_TILES + 1), new(2 * NJ), new(2 * NJ)
            starts = cst[:, C_START:C_START + MAX_TILES + 1]
            step(tt(reached, over(place, MAX_TILES + 1), across(starts, 2 * NJ), ALU.is_ge))
            total(tile_of, reached)
            step(ts(tile_of, tile_of, -float(P), float(P), ALU.mult, ALU.add))
            step(tt(pos, place, tile_of, ALU.add))
            step(tt(in_tile, reached[:, :, 0:MAX_TILES], reached[:, :, 1:MAX_TILES + 1], ALU.subtract))
            tt(at_pos, over(pos, P), across(cst[:, C_POS:C_POS + P], 2 * NJ), ALU.is_equal)
            step(tt(in_tile, in_tile, over(cst[:, C_TOKEN:C_TOKEN + 2 * NJ], MAX_TILES), ALU.mult))
            dve.sem_inc(s_pos, 1)
            dve.tensor_copy(ri[:, 40:40 + 2 * NJ], place)
            past, owner = new(28, E), new(28)
            step(tt(past, across(ends, 28), over(cst[:, C_ITEM:C_ITEM + 28], E), ALU.is_le))
            total(owner, past)
            step(ts(owner, owner, float(E - 1), None, ALU.min))
            dve.tensor_copy(ri[:, 0:28], owner)
            dve.tensor_copy(ri[:, 60:61], ends[:, E - 1:E])
            dve.wait_ge(s_tk, 1)
            dve.tensor_copy(token_of[:, 0:MAX_TILES], psb[5][:, 0:MAX_TILES]).then_inc(s_rt, 1)

            dve.wait_ge(s_rt, 1)
            k_tiles = dve.value_load(ri[0:1, 60:61], min_val=16, max_val=25)
            dve.sem_inc(s_ac, 2)

            def copy_tokens(n):
                dve.wait_ge(s_xtp, n)
                dve.tensor_copy(xgT[:, 4:8, :], psb[3][:, :].rearrange("p (k t) -> p k t", k=4)).then_inc(s_xgT, 1)

            copy_tokens(1)
            with dve.Fori(0, k_tiles) as i:
                dve.wait_ge(s_dn, i * 2 + 2)
                for c in range(FT):
                    dve.wait_ge(s_sg, i * FT + (c + 1))
                    tt(aT[:, c, :], sg[c % 2], psb[c % 2][:, P:2 * P], ALU.mult).then_inc(s_ac, 1)
                copy_tokens(i + 2)
                dve.wait_ge(s_dn, i * 2 + 4)
                dve.wait_ge(s_yst, i * 16 + 16)
                dve.tensor_copy(yo[:, 512:1024], psb[7][:, :]).then_inc(s_yo, 1)

            dve.wait_ge(s_row2, 32)
            dve.wait_ge(s_fn, 16)

            def residual(j):
                cd = min(j, 1)
                dve.wait_ge(s_ya, j + 1)
                ya = ygb[:, 2 * j, :]
                yb = ygb[:, 2 * j + 1, :]
                step(stt(yb, yb, gate[:, NJ + j:NJ + j + 1], ya, ALU.mult, ALU.add))
                step(tt(yb, yb, g2row[:, cd, :], ALU.mult))
                tt(x1[:, j, :], x1[:, j, :], yb, ALU.add).then_inc(s_fin, 1)

            def final_norm(j):
                dve.wait_ge(s_rs, 3 + NJ + j)
                r = stat[:, j:j + 1]
                step(dve.reciprocal(r, r))
                if j >= 2:
                    dve.wait_ge(s_ost[j % 2], 16 * (j // 2))
                stt(fout[j % 2], x1[:, j, :], r, fnrow, ALU.mult, ALU.mult).then_inc(s_fo, 1)

            for j in range(NJ):
                residual(j)
                if j >= 1:
                    final_norm(j - 1)
            final_norm(NJ - 1)


def layout(a):
    f = np.float32
    p = np.arange(P)
    cst = np.zeros((P, C_ALL), f)
    cst[:, C_ID:C_ID + P] = np.eye(P)
    cst[:, C_TRIF:C_TRIF + P] = p[:, None] <= p[None]
    cst[:, C_TRIB:C_TRIB + P] = p[:, None] >= p[None]
    cst[:, C_ONES:C_ONES + P] = 1
    cst[:, C_P16:C_P16 + E] = E - np.arange(E)
    cst[:, C_P4:C_P4 + EG] = EG - np.arange(EG)
    cst[:, C_ITEM:C_ITEM + 28] = np.arange(28)
    cst[:, C_STEP:C_STEP + 4] = P * (1 + np.arange(4))
    cst[:, C_TOKEN:C_TOKEN + 2 * NJ] = p[:, None] + P * (np.arange(2 * NJ) % NJ)
    cst[:, C_START:C_START + MAX_TILES + 1] = P * np.arange(MAX_TILES + 1)
    cst[:, C_POS:C_POS + P] = p
    bc = np.zeros((P, B_ALL), f)
    bc[:, B_STRICT:B_STRICT + P] = p[:, None] < p[None]
    bc[:, B_MASK:B_MASK + P] = np.where(p[:, None] > p[None], -BIG, 0)
    bc[:, B_MASK + P:B_MASK + 2 * P] = np.where(p[:, None] < p[None], -BIG, 0)
    bc[:96, B_STACK:B_STACK + 32] = np.arange(96)[:, None] % 32 == np.arange(32)

    def cols(v, n):
        return np.asarray(v, f).reshape(n, P).T

    vec = np.zeros((P, V_ALL), f)
    vec[:, V_ADA:V_ADA + 96] = np.repeat(cols(a["b_ada"][0], 48), 2, axis=1)
    vec[:, V_N1:V_N1 + 16] = np.repeat(cols(a["norm1_w"][0], KT), 2, axis=1)
    vec[:, V_N2:V_N2 + 16] = np.repeat(cols(a["norm2_w"][0], KT), 2, axis=1)
    order = np.r_[D:D + 512, 0:D]
    vec[:, V_CW:V_CW + 48] = a["conv_w"][0][:, order].reshape(4, CONVF, P).transpose(2, 1, 0).reshape(P, 48)
    vec[:, V_CB:V_CB + CONVF] = cols(a["conv_b"][0][order], CONVF)
    vec[:, V_PS:V_PS + 8] = cols(a["pool_scale"][0], KT)
    vec[:, V_SN:V_SN + 8] = cols(a["ssd_norm_w"][0], KT)
    vec[:, V_C:V_C + 16] = np.stack([cols(a["c_ctx"], KT), cols(a["c"][0], KT)], axis=2).reshape(P, 16)
    row = np.concatenate([np.asarray(a["router_bias"], f), a["dt_bias"][0].reshape(-1), a["a_log"][0].reshape(-1),
                          a["d_skip"][0].reshape(-1)])[None]

    def count(n, w):
        i = np.arange(n)
        return np.clip(i + w // 2 - 1, 0, n - 1) - np.clip(i - w // 2, 0, n - 1) + 1

    inv = np.concatenate([np.concatenate([1 / count(CTX, w), (1 / np.outer(count(ROWS, w), count(GRID_W, w))).ravel()])
                          for w in WINDOWS]).astype(f)[None]
    w_ada, w_in, w_out = a["w_ada"][0], a["w_in"][0], a["w_out"][0]

    def chunk(w, c0):
        return w[:, c0:c0 + 512].reshape(KT, P, 512).transpose(1, 0, 2).reshape(P, CHUNK)

    x0 = D
    v0 = D + D + 512 + 32
    parts = [chunk(w_ada, 512 * i) for i in range(4)]
    parts += [chunk(w_in, c0) for c0 in (v0, v0 + 512, x0 + D, x0, x0 + 512, 0, 512)]
    w_late = np.stack([chunk(w_ada, 512 * q)[:, i * 2048:(i + 1) * 2048] for q in range(4, 10) for i in range(2)])
    parts += [chunk(w_out[c * D:(c + 1) * D], h * 512) for h in range(2) for c in range(2)]
    parts += [chunk(w_ada, 512 * q) for q in (10, 11)]
    w_dt = w_in[:, v0 - 32:v0].reshape(KT, P, 32).transpose(1, 0, 2).reshape(P, KT * 32)
    w_pool = a["pool_w"][0].reshape(4, 2, P, 256).transpose(2, 0, 1, 3).reshape(P, 2048)
    gu = np.stack([a["w_gate"][0], a["w_up"][0]], axis=1).reshape(E, 2, KT, P, FT, P)
    gu = gu.transpose(0, 4, 3, 1, 2, 5).reshape(E, FT, P, 2048)
    dn = a["w_down"][0].reshape(E, 2, 2, P, D).transpose(0, 1, 3, 2, 4).reshape(E, 2, P, 2048)
    return {
        "consts": cst, "bconsts": bc, "vecs": vec, "rows": row, "inv": inv,
        "w_late": w_late, "b_late": a["b_ada"][0][2 * D:].reshape(8, 512), "norm2": a["norm2_w"],
        "fnorm": a["final_norm_w"][None], "x": np.concatenate([a["x_prompt"][0], a["x_sample"][0]]),
        "states0": a["state_ssm"][0, 0].transpose(0, 3, 1, 2).reshape(2, N, D),
        "w_ring": np.stack(parts), "w_dt": w_dt, "w_pool": w_pool,
        "w_router": a["w_router"].reshape(KT, P, E).transpose(1, 0, 2).reshape(P, KT * E),
        "w_exp": np.concatenate([gu, dn], axis=1),
    }


_OUTS = {"y_out": (TOK, D), "s_out": (2, D, N)}


def kernel(**inputs):
    import concourse.bacc as bacc
    from concourse.bass_utils import run_bass_kernel_spmd

    nc = bacc.Bacc("TRN2", target_bir_lowering=False, num_devices=1)
    a = {k: np.asarray(v) for k, v in inputs.items()}
    arrays = {k: np.ascontiguousarray(v) for k, v in layout(a).items()}
    aps = {k: nc.dram_tensor(k, v.shape, mybir.dt.from_np(v.dtype), kind="ExternalInput").ap()
           for k, v in arrays.items()}
    for name, shape in _OUTS.items():
        aps[name] = nc.dram_tensor(name, shape, F32, kind="ExternalOutput").ap()
    trunk_kernel(nc, **aps)
    r = run_bass_kernel_spmd(nc, [arrays], core_ids=[0]).results[0]
    y, s = np.asarray(r["y_out"]), np.asarray(r["s_out"])
    return y[None, :CTX], y[None, CTX:], s.reshape(1, 1, 2, H, HD, N)
```

```python
from contextlib import ExitStack

import numpy as np

import concourse.bass as bass
import concourse.mybir as mybir
from concourse.alu_op_type import AluOpType as ALU

F32 = mybir.dt.float32
BF16 = mybir.dt.bfloat16
I32 = mybir.dt.int32
ACT = mybir.ActivationFunctionType
AX_X = mybir.AxisListType.X

P = 128
D = 1024
KT = D // P
CTX, LAT = 128, 512
TOK = CTX + LAT
NJ = TOK // P
GRID_W = 64
ROWS = LAT // GRID_W
H, HD, N = 16, 64, 128
HG = H // 2
E, EG, EPG = 16, 4, 4
FF = 512
FT = FF // P
CONVF = 12
WINDOWS = (2, 4, 8, 16)
EPS = 1e-6
BIG = 1e30
MAX_TILES = 26
SLOTS = MAX_TILES * P
RING = 3
CHUNK = 4096
WBUFS = 6
ADA_SUMS = (3, 4, 5, 6, 7, 9)

C_ID, C_TRIF, C_TRIB, C_ONES = 0, 128, 256, 384
C_P16, C_P4, C_ITEM, C_STEP, C_TOKEN, C_START, C_POS = 512, 528, 532, 560, 564, 574, 602
C_ALL = 730
B_STRICT, B_MASK, B_STACK, B_ALL = 0, 128, 384, 416
XDD_ORDER = ((0, 0), (1, 0), (0, 1), (1, 4), (0, 2), (1, 3), (0, 3), (1, 2))
V_ADA, V_N1, V_N2, V_CW, V_CB, V_PS, V_SN, V_C = 0, 96, 112, 128, 176, 188, 196, 204
V_ALL = 220
R_RB, R_DTB, R_ALOG, R_DSK = 0, 16, 48, 80
R_ALL = 112
INV_ALL = 4 * TOK


class Steps:

    def __init__(self, eng, sem):
        self.eng, self.sem, self.n = eng, sem, 0

    def __call__(self, ins):
        self.n += 1
        ins.then_inc(self.sem, 1)
        self.eng.wait_ge(self.sem, self.n)


def trunk_kernel(nc, consts, bconsts, vecs, rows, inv, norm2, fnorm, x, states0, w_ring, w_late, b_late, w_dt,
                 w_pool, w_router, w_exp, y_out, s_out):
    ctx = ExitStack()
    with ctx:
        def sb(name, shape, dt=F32):
            return ctx.enter_context(nc.sbuf_tensor(name, shape, dt))

        def sem(name):
            return ctx.enter_context(nc.semaphore(name))

        ada_rows = nc.dram_tensor("ada_rows", [4, 2, D], F32).ap()
        h2_dram = nc.dram_tensor("h2_dram", [TOK, D], F32).ap()
        slot_out = nc.dram_tensor("slot_out", [SLOTS - P, D], F32).ap()

        ring = sb("ring", [P, RING, CHUNK])
        ex = sb("ex", [P, 12288])
        yT = sb("yT", [P, KT, TOK])
        xs = sb("xs", [P, NJ, D])
        bcT = sb("bcT", [P, 4, TOK])
        btok = sb("btok", [P, NJ, 2 * N])
        gT = sb("gT", [P, NJ, 2, P])
        uT = sb("uT", [P, KT, TOK])
        hT = sb("hT", [P, KT, TOK])
        cst = sb("cst", [P, C_ALL])
        vec = sb("vec", [P, V_ALL])
        row = sb("row", [P, R_ALL])
        idb = sb("idb", [P, P], BF16)
        maskb = sb("maskb", [P, 2, P], BF16)
        strictb = sb("strictb", [P, P], BF16)
        onesb = sb("onesb", [P, P], BF16)
        stackb = sb("stackb", [96, 32], BF16)
        nstackb = sb("nstackb", [96, 32], BF16)
        silc = sb("silc", [P, 2 * KT])
        modA = sb("modA", [P, 2 * KT])
        modB = sb("modB", [P, 2 * KT])
        stat = sb("stat", [P, 27])
        eps_col = sb("eps_col", [P, 1])
        dts = sb("dts", [P, 8, NJ * 32])
        nega = sb("nega", [P, 32])
        dsum = sb("dsum", [P, H])

        ident = cst[:, C_ID:C_ID + P]
        trif = cst[:, C_TRIF:C_TRIF + P]
        trib = cst[:, C_TRIB:C_TRIB + P]
        ones = cst[:, C_ONES:C_ONES + P]
        dt_, a_, ncum, ecum, dec, etot, sc0, sc1 = (dts[:, i, :] for i in range(8))
        dtdec = dec

        xt = ex[:, 0:NJ * D].rearrange("p (j d) -> p j d", j=NJ)
        XP = 131 + 515
        xpad = [ex[:, i * XP:(i + 1) * XP] for i in range(2)]
        cacc = [ex[:, 1300 + i * XP:1300 + i * XP + 643] for i in range(2)]
        xsT = [ex[:, 2600 + i * TOK:2600 + (i + 1) * TOK] for i in range(2)]
        pa, pb_, pc = (ex[:, 3900 + i * 960:3900 + (i + 1) * 960] for i in range(3))
        arow = ex[0:2, 5120:5120 + 2048]
        brow = xs[0:1, 0:3, :].rearrange("p a n -> p (a n)")
        orow = [xs[0:1, 3 + i, :] for i in range(2)]
        n2row = ex[0:1, 7296:7296 + D]
        invb = ex[:, 12288 - INV_ALL:12288]
        dtrow = ex[0:32, 1300:1300 + TOK]
        wdt = gT[:, 0, :, :].rearrange("p a b -> p (a b)")
        st = ex[:, 0:8 * D].rearrange("p (i d) -> p i d", i=8)
        xdd = ex[:, 10240:10240 + 2 * D].rearrange("p (i d) -> p i d", i=2)
        hf = hT[:, :, :].rearrange("p k t -> p (k t)")
        uf = uT[:, :, :].rearrange("p k t -> p (k t)")
        zf = yT[:, :, :].rearrange("p k t -> p (k t)")
        bf_ = bcT[:, :, :].rearrange("p f t -> p (f t)")
        btf = btok[:, :, :].rearrange("p j n -> p (j n)")
        adaw = [zf[:, i * 2048:(i + 1) * 2048].rearrange("p (k c) -> p k c", k=4) for i in range(2)]
        acc = [zf[:, 4096:5120], ex[:, 2600:3624]]
        gT_pw = zf[:, 0:2048].rearrange("p (g k m) -> p g k m", g=4, k=2)
        bcst = hf[:, 0:B_ALL]
        tabT = [bf_[0:96, d * 320:(d + 1) * 320].bitcast(BF16) for d in range(2)]
        yt = [bf_[:, 640:1152], ex[:, 11776:12288]]
        wbufs = [ex[:, 8192 + i * 512:8192 + (i + 1) * 512].rearrange("p (h d t) -> p h d t", h=2, d=2)
                 for i in range(WBUFS)]
        sout = [zf[:, 2048 + d * D:2048 + (d + 1) * D] for d in range(2)]
        split_r = [ex[0:32, 8192 + i * TOK:8192 + (i + 1) * TOK] for i in range(2)]
        mid = zf[0:32, 4096:4416].bitcast(BF16)
        zbuf = [btf[:, 0:512], btf[:, 512:1024], ex[:, 11264:11776]]
        junk_x = uf[:, 0:D]
        junk_y = btf[:, 1024:1280].bitcast(BF16)
        junk_1 = dts[:, :, :].rearrange("p a b -> p (a b)")[:, 768:1280].bitcast(BF16)
        junk_z = zf[:, 2 * D:3 * D]
        zero_f = ex[:, 3900:3900 + D]
        MASK4 = maskb[:, :, :].unsqueeze(1).to_broadcast([P, 2, 2, P])

        def wbuf(i):
            return wbufs[i % WBUFS]

        def out_bank(j, hf_, c):
            return psb[6] if (j, hf_, c) == (0, 0, 1) else psb[2 * c + hf_]

        def pooled_banks(i):
            if i < 4:
                return (psb[1][:, 256:384], psb[0][:, :]) if i % 2 == 0 else (psb[7][:, 0:CTX], psb[6][:, :])
            return psb[3 + 2 * (i % 2)][:, 0:CTX], psb[2 + 2 * (i % 2)][:, :]

        psb = [ctx.enter_context(nc.psum_tensor(f"bank{i}", [P, 512], F32)) for i in range(8)]

        s_const = sem("constants_loaded")
        s_bconst = sem("bfloat16_constants_loaded")
        s_x = [sem(f"x_tile_{j}_loaded") for j in range(NJ)]
        s_ring = [sem(f"ring_{i}_loaded") for i in range(RING)]
        s_half = sem("ring_0_first_half_loaded")
        s_adaw = [sem(f"ada_half_{i}_loaded") for i in range(2)]
        s_brow = sem("ada_bias_loaded")
        s_n2 = sem("norm2_row_loaded")
        s_ar = sem("ada_rows_product")
        s_g2w = [sem(f"gate2_chunk_{i}_loaded") for i in range(2)]
        s_g2d = sem("gate2_rows_stored")
        s_g2p = sem("gate2_products")
        s_g2c = sem("gate2_rows_ready")
        s_g2b = sem("gate2_bias_loaded")
        s_arc = sem("ada_rows_on_chip")
        s_adr = sem("late_ada_rows_ready")
        s_ada = sem("ada_sums")
        s_accs = sem("ada_partial_sums")
        s_acc = sem("ada_half_summed")
        s_wo3 = sem("last_output_weights_loaded")
        s_used = sem("ring_chunks_used")
        s_wdt = sem("dt_weights_loaded")
        s_inv = sem("inverse_counts_loaded")
        s_pw = sem("pool_weights_loaded")
        s_st0 = sem("initial_states_loaded")
        s_cast = sem("constants_cast")
        s_rs = sem("rms_ready")
        s_dve = sem("dve_steps")
        s_pool = sem("pool_steps")
        s_silc = sem("silu_c_ready")
        s_mod = sem("modulation_ready")
        s_ss = sem("x_squares_summed")
        s_xn = sem("x_normalised")
        s_xtr = sem("x_transposed")
        s_hs = sem("h_latents_ready")
        s_hc = sem("h_context_ready")
        s_dtr = sem("dt_rows_product")
        s_dtc = sem("dt_rows_on_chip")
        s_dtp = sem("dt_token_major")
        s_soft = sem("softplus_handover")
        s_a = sem("decay_rates_ready")
        s_cum = sem("decay_sums")
        s_dif = sem("decay_exponents_ready")
        s_dtd = sem("dt_decays_ready")
        s_dec = sem("decays_ready")
        s_fm = sem("feature_tiles_projected")
        s_pad = sem("conv_inputs_copied")
        s_conv = sem("conv_summed")
        s_cs = sem("conv_activated")
        s_ttr = sem("conv_tiles_transposed")
        s_tok = sem("conv_tiles_token_major")
        s_vr = sem("v_copied")
        s_pu = sem("windows_pooled")
        s_z = sem("z_projected")
        s_zt = sem("tanh_of_half_z")
        s_zs = sem("z_activated")
        s_pm = sem("pool_products")
        s_u = sem("pool_scaled")
        s_tab = sem("decay_tables_summed")
        s_tabs = sem("decay_tables_split")
        s_g = sem("bc_products")
        s_gs = sem("bc_products_copied")
        s_xdd = sem("x_decayed")
        s_sp = sem("state_products")
        s_st = sem("states_ready")
        s_so = sem("context_states_copied")
        s_sout = sem("context_states_stored")
        s_wd = sem("decays_times_dt")
        s_e = sem("exponents_built")
        s_ex = sem("decays_exponentiated")
        s_w = sem("scores_decayed")
        s_dg = sem("diagonal_products")
        s_off = sem("state_outputs")
        s_yp = sem("ssd_state_outputs_read")
        s_yc = sem("ssd_outputs_combined")
        s_ys = sem("ssd_squares_summed")
        s_yss = sem("ssd_squares_joined")
        s_ytr = sem("ssd_outputs_transposed")
        s_yT = sem("ssd_outputs_ready")
        s_ads = [sem(f"ada_rows_{i}_stored") for i in range(2)]
        s_rowl = sem("ada_rows_loaded")
        s_row2 = sem("late_rows_loaded")
        s_xr = [sem("x_reloaded"), sem("last_x_tile_reloaded")]
        s_op = sem("output_products")
        s_x1 = sem("residual_ready")
        s_x1s = sem("residual_squares_summed")
        s_h2 = sem("h2_ready")
        s_h2s = [sem(f"h2_stored_{i}") for i in range(2)]
        s_h2t = sem("h2_transposed")
        s_h2T = sem("h2_feature_major")
        s_lg = sem("logits_ready")
        s_wr = sem("router_weights_loaded")
        s_lm = sem("logits_shifted")
        s_le = sem("logits_exponentiated")
        s_oh = sem("choices_ready")
        s_rk = sem("ranks_ready")
        s_rt = sem("routing_ready")
        s_zero = sem("unfilled_slot_rows_cleared")
        s_pos = sem("slot_positions_ready")
        s_tk = sem("slot_tokens_summed")
        s_w_in = [sem(f"expert_chunk_{c}_loaded") for c in range(6)]
        s_idx = sem("slot_tokens_loaded")
        s_xg = sem("tokens_gathered")
        s_begun = sem("gathers_begun")
        s_xtp = sem("gathered_transposed")
        s_xgT = sem("gathered_feature_major")
        s_gu = sem("gate_up_products")
        s_sg = sem("gates_activated")
        s_ac = sem("expert_activations")
        s_dn = sem("down_products")
        s_yo = sem("expert_outputs_copied")
        s_yst = sem("expert_outputs_stored")
        s_yg = [sem(f"expert_rows_gathered_{j}") for j in range(NJ)]
        s_ya = sem("first_rows_weighted")
        s_mix = sem("expert_rows_mixed")
        s_gm = sem("mixed_rows_gated")
        s_fin = sem("final_sum_ready")
        s_fss = sem("final_squares_summed")
        s_fo = sem("final_output_ready")
        s_ost = [sem(f"outputs_stored_{i}") for i in range(2)]
        s_fn = sem("final_norm_loaded")

        x1 = xs
        wo = [ring[:, 2, :], ring[:, 0, :], ring[:, 1, :], hf[:, 0:CHUNK]]
        g1row = ex[:, 0:2 * D].rearrange("p (c d) -> p c d", c=2)
        a2row = ex[:, 2 * D:4 * D].rearrange("p (c d) -> p c d", c=2)
        w_g2 = [ex[:, (4 + 4 * i) * D:(8 + 4 * i) * D] for i in range(2)]
        h2buf0 = hf[:, 4 * D:5 * D]
        b2row = bf_[:, 0:2 * D].rearrange("p (c d) -> p c d", c=2)
        g2b = uf[0:2, 3 * D:4 * D].rearrange("p (i n) -> p i n", n=512)
        g2s = uf[0:2, 4 * D:5 * D].rearrange("p (i n) -> p i n", n=512)
        x1t = bf_[:, 2 * D:2 * D + 512]
        gtf = gT[:, :, :, :].rearrange("p j g n -> p (j g n)")
        h2buf1 = btf[:, 0:D]
        h2bufs = [h2buf0, h2buf1]
        wrt = gtf[:, D:D + P].rearrange("p (k e) -> p k e", e=E)
        h2T = gtf[:, 0:D].rearrange("p (k t) -> p k t", k=KT)
        xg = zf[:, 0:D]
        xgT = zf[:, D:2 * D].rearrange("p (k t) -> p k t", k=KT)
        aT = zf[:, 2 * D:2 * D + FT * P].rearrange("p (k t) -> p k t", k=FT)
        sg = [zf[:, 2560 + i * P:2560 + (i + 1) * P] for i in range(2)]
        yo = zf[:, 3072:3072 + D]
        g2row = uf[:, 0:2 * D].rearrange("p (c d) -> p c d", c=2)
        fnrow = uf[:, 2 * D:3 * D]
        fout = [uf[:, 3 * D + i * D:3 * D + (i + 1) * D] for i in range(2)]
        ygb = ex[:, 0:2 * NJ * D].rearrange("p (n d) -> p n d", d=D)
        ri = sb("ri", [P, 64], I32)
        idx = sb("idx", [P, 2], I32)
        token_of = sb("token_of", [P, MAX_TILES + 1], I32)
        gate = sb("gate", [P, 2 * NJ])
        dtf = dts[:, :, :].rearrange("p a b -> p (a b)")
        rw_a, rw_b = dtf[:, 0:768], ring[:, 2, :]
        n_sh, n_ex = rw_a[:, 0:80], rw_a[:, 80:160]
        at_pos = zf[:, 2 * D:2 * D + 2 * NJ * P].rearrange("p (i n) -> p i n", n=P)
        in_tile = zf[:, 3328:3328 + 2 * NJ * MAX_TILES].rearrange("p (i n) -> p i n", n=MAX_TILES)
        onehotb = sb("onehotb", [P, NJ * E], BF16)

        block = ctx.enter_context(nc.Block())

        NCH = 14
        @block.sync
        def _(sp):
            sp.dma_start(cst[:], consts).then_inc(s_const, 16)
            sp.dma_start(vec[:], vecs).then_inc(s_const, 16)
            sp.dma_start(row[:], rows.to_broadcast([P, R_ALL])).then_inc(s_const, 16)

            def load_ring(n):
                if n >= RING:
                    sp.wait_ge(s_used, n - RING + 1)
                sp.dma_start(ring[:, n % RING, :], w_ring[n]).then_inc(s_ring[n % RING], 16)

            sp.dma_start(ring[:, 0, 0:2048], w_ring[0, :, 0:2048]).then_inc(s_half, 16)
            sp.dma_start(ring[:, 0, 2048:CHUNK], w_ring[0, :, 2048:CHUNK]).then_inc(s_ring[0], 16)
            sp.dma_start(bcst, bconsts).then_inc(s_bconst, 16)
            sp.dma_start(wdt, w_dt).then_inc(s_wdt, 16)
            load_ring(1)
            sp.dma_start(n2row, norm2).then_inc(s_n2, 16)
            sp.dma_start(brow, b_late[0:6, :].rearrange("(o q) n -> o (q n)", o=1)).then_inc(s_brow, 16)
            load_ring(2)

            def load_ada(u):
                if u >= 2:
                    sp.wait_ge(s_acc, u - 1)
                sp.dma_start(adaw[u % 2], w_late[u].rearrange("p (k c) -> p k c", k=4)).then_inc(s_adaw[u % 2], 16)

            sp.wait_ge(s_used, 1)
            sp.dma_start(ring[:, 0, 0:2048], w_ring[3, :, 0:2048]).then_inc(s_half, 16)
            for j in range(NJ):
                sp.dma_start(xt[:, j, :], x[j * P:(j + 1) * P, :]).then_inc(s_x[j], 16)
            sp.dma_start(ring[:, 0, 2048:CHUNK], w_ring[3, :, 2048:CHUNK]).then_inc(s_ring[0], 16)
            load_ring(4)
            load_ada(0)
            load_ada(1)
            sp.dma_start(invb, inv.to_broadcast([P, INV_ALL])).then_inc(s_inv, 16)
            for u in (2, 3):
                load_ada(u)
            load_ring(5)
            for u in range(4, 8):
                load_ada(u)
            load_ring(6)
            for u in range(8, 11):
                load_ada(u)
            load_ring(7)
            load_ada(11)
            for n in range(8, NCH):
                load_ring(n)
            sp.wait_ge(s_z, 2 * NJ)
            sp.dma_start(wo[3], w_ring[NCH]).then_inc(s_wo3, 16)
            for j in range(NJ):
                if j == NJ - 1:
                    sp.wait_ge(s_off, 2 * (NJ - 1))
                    sp.dma_start(g1row, ada_rows[0:1].to_broadcast([P, 2, D])).then_inc(s_rowl, 16)
                    sp.dma_start(a2row, ada_rows[2:3].to_broadcast([P, 2, D])).then_inc(s_rowl, 16)
                    sp.wait_ge(s_yc, 2 * NJ)
                    sp.wait_ge(s_ex, NJ * HG)
                    sp.dma_start(b2row, ada_rows[1:2].to_broadcast([P, 2, D])).then_inc(s_row2, 16)
                sp.wait_ge(s_ytr, 2 * (j + 1))
                sp.wait_ge(s_ys, 2 * (j + 1))
                sp.dma_start(x1[:, j, :], x[j * P:(j + 1) * P, :]).then_inc(s_xr[j // (NJ - 1)], 16)
            sp.wait_ge(s_dg, NJ * HG)
            sp.wait_ge(s_yc, 2 * NJ)
            sp.wait_ge(s_op, 2)
            for i in range(2):
                sp.dma_start(w_g2[i], w_ring[NCH + 1 + i]).then_inc(s_g2w[i], 16)
            sp.wait_ge(s_h2, NJ)
            for c in range(6):
                if c in (2, 4):
                    sp.wait_ge(s_g2p, c // 2)
                if c == 4:
                    sp.wait_ge(s_xg, 16)
                sp.dma_start(ex[:, c * 2048:(c + 1) * 2048], w_exp[0, c]).then_inc(s_w_in[c], 16)
            sp.wait_ge(s_rt, 1)
            k_tiles = sp.value_load(ri[0:1, 60:61], min_val=16, max_val=25)
            with sp.Fori(1, k_tiles) as i:
                e = sp.value_load(ri[0:1, bass.ds(i, 1)], min_val=0, max_val=E - 1)
                for c in range(6):
                    if c < FT:
                        sp.wait_ge(s_gu, i * FT + (c + 1 - FT))
                    else:
                        sp.wait_ge(s_dn, i * 2 + (c - FT + 1))
                    sp.dma_start(ex[:, c * 2048:(c + 1) * 2048], w_exp[e, c]).then_inc(s_w_in[c], 16)
            for j in range(NJ):
                sp.wait_ge(s_fo, j + 1)
                sp.dma_start(y_out[j * P:(j + 1) * P, :], fout[j % 2]).then_inc(s_ost[j % 2], 16)
            sp.wait_ge(s_ost[0], 48)
            sp.wait_ge(s_ost[1], 32)
            sp.wait_ge(s_sout, 32)

        @block.tensor
        def _(pe):
            pe.wait_ge(s_silc, 1)
            pe.wait_ge(s_const, 48)

            for n in range(4):
                if n in (1, 2):
                    pe.wait_ge(s_ring[n], 16)
                w = ring[:, n % RING, :].rearrange("p (k c) -> p k c", k=KT)
                for k in range(KT):
                    if n in (0, 3) and k % 4 == 0:
                        pe.wait_ge(s_ring[0] if k else s_half, 32 if n else 16)
                    mm = pe.matmul(psb[n][0:2, :], silc[:, 2 * k:2 * k + 2], w[:, k, :],
                                   start=(k == 0), stop=(k == KT - 1))
                mm.then_inc(s_used, 1)
            for m in range(16):
                if m % 4 == 0:
                    pe.wait_ge(s_arc, m // 4 + 1)
                mm = pe.transpose(psb[4][:, 2 * m:2 * m + 2], arow[:, m * P:(m + 1) * P], ident[0:2, 0:2])
            mm.then_inc(s_ar, 1)
            def project_features(f, k):
                n = 4 + f // 4
                if f % 4 == 0 and k == 0:
                    pe.wait_ge(s_ring[n % RING], 16 * (n // RING + 1))
                if f == 0:
                    pe.wait_ge(s_hs, k + 1)
                    pe.wait_ge(s_hc, k + 1)
                w = ring[:, n % RING, :].rearrange("p (k c) -> p k c", k=KT)
                q = 2 + 2 * (f % 3)
                for lo, hi, o in ((0, CTX, psb[q + 1][:, 0:CTX]), (CTX, TOK, psb[q][:, :])):
                    mm = pe.matmul(o, w[:, k, (f % 4) * P:(f % 4 + 1) * P], hT[:, k, lo:hi],
                                   start=(k == 0), stop=(k == KT - 1))
                return mm

            for j in range(NJ):
                pe.wait_ge(s_xn, j + 1)
            pe.wait_ge(s_arc, 4)
            for k in range(KT):
                if k == 1:
                    pe.wait_ge(s_mod, 1)
                if k >= 2:
                    pe.wait_ge(s_hs, k - 1)
                    pe.wait_ge(s_hc, k - 1)
                q = 6 - 2 * (k % 2)
                for j in range(NJ):
                    o = psb[q + 1][:, 0:P] if j == 0 else psb[q][:, (j - 1) * P:j * P]
                    mm = pe.transpose(o, xt[:, j, k * P:(k + 1) * P], ident)
                mm.then_inc(s_xtr, 1)
                if k:
                    project_features(0, k - 1)
            project_features(0, KT - 1).then_inc(s_fm, 1)

            def turn_conv(t):
                f = t if t < 2 else t + 2
                pe.wait_ge(s_cs, f + 1)
                if t == 0:
                    pe.wait_ge(s_adr, 6)
                if t >= 1:
                    pe.wait_ge(s_tok, t)
                src = bcT[:, t, :] if t < 2 else xsT[t % 2]
                for j in range(NJ):
                    o = psb[1][:, 0:P] if j == 0 else psb[0][:, (j - 1) * P:j * P]
                    mm = pe.transpose(o, src[:, j * P:(j + 1) * P], ident)
                mm.then_inc(s_ttr, 1)

            for f in range(20):
                if f >= 3:
                    pe.wait_ge(s_vr if f - 3 < KT else s_pad, f - 2 if f - 3 < KT else f - 2 - KT)
                if f:
                    for k in range(KT):
                        mm = project_features(f, k)
                    mm.then_inc(s_fm, 1)
                if f % 4 == 3:
                    pe.wait_ge(s_fm, f + 1)
                    pe.sem_inc(s_used, 1)
                if f == 0:
                    pe.wait_ge(s_wdt, 16)
                    for lo, hi, o in ((0, CTX, psb[1][0:32, 0:CTX]), (CTX, TOK, psb[0][0:32, :])):
                        for k in range(KT):
                            mm = pe.matmul(o, wdt[:, k * 32:(k + 1) * 32], hT[:, k, lo:hi],
                                           start=(k == 0), stop=(k == KT - 1))
                    mm.then_inc(s_dtr, 1)
                if f == 1:
                    pe.wait_ge(s_dtc, 1)
                    for j in range(NJ):
                        mm = pe.transpose(psb[0][:, j * 32:(j + 1) * 32], dtrow[:, j * P:(j + 1) * P], ident[0:32, 0:32])
                    mm.then_inc(s_dtp, 1)
                if f == 2:
                    pe.wait_ge(s_a, 1)
                    for j in range(NJ):
                        for d, tri in ((0, trif), (1, trib)):
                            c = j * 32 + d * H
                            pe.matmul(psb[0][:, c:c + H], tri, a_[:, c:c + H], start=True, stop=True)
                    pe.matmul(psb[0][:, 160:320], ones, a_, start=True, stop=True).then_inc(s_cum, 1)
                if f in ADA_SUMS:
                    q = ADA_SUMS.index(f)
                    pe.wait_ge(s_acc, 2 * (q + 1))
                    if q == 0:
                        pe.wait_ge(s_dif, 1)
                    else:
                        pe.wait_ge(s_adr, q)
                    for c in range(2):
                        mm = pe.matmul(psb[c][0:1, :], ones[:, 0:1],
                                       acc[q % 2][:, c * 512:(c + 1) * 512], start=True, stop=True)
                    mm.then_inc(s_ada, 1)
                if f == 11:
                    turn_conv(0)
                elif 13 <= f:
                    turn_conv(f - 12)
            def project_z(jg, ks):
                j, g = jg // 2, jg % 2
                w = ring[:, g, :].rearrange("p (k c) -> p k c", k=KT)
                if ks[0] == 0 and jg < 2:
                    pe.wait_ge(s_ring[g], 16 * 4)
                if ks[0] == 0 and jg >= 1:
                    pe.wait_ge(s_zs, jg)
                for k in ks:
                    mm = pe.matmul(psb[6][:, :], hT[:, k, j * P:(j + 1) * P], w[:, k, :],
                                   start=(k == 0), stop=(k == KT - 1), skip_group_check=True)
                if ks[-1] == KT - 1:
                    mm.then_inc(s_z, 1)

            pe.wait_ge(s_pad, CONVF)
            for d, tri in ((0, trif), (1, trib)):
                q = 2 + 2 * d
                for j in range(NJ):
                    o = psb[q + 1][0:32, 0:P] if j == 0 else psb[q][0:32, (j - 1) * P:j * P]
                    mm = pe.matmul(o, a_[:, j * 32:(j + 1) * 32], tri, start=True, stop=True)
                mm.then_inc(s_tab, 1)
            for j in range(NJ):
                for g in range(2):
                    i = 2 * j + g
                    if i == 8:
                        turn_conv(8)
                        turn_conv(9)
                        pe.wait_ge(s_tok, 10)
                    o = psb[6 + i // 4][:, (i % 4) * P:(i % 4 + 1) * P] if i < 8 else \
                        psb[1][:, (i % 4) * P:(i % 4 + 1) * P]
                    mm = pe.matmul(o, bcT[:, g, j * P:(j + 1) * P], bcT[:, 2 + g, j * P:(j + 1) * P],
                                   start=True, stop=True)
            mm.then_inc(s_g, 1)
            def pool_product(i):
                g, m = i // 2, i % 2
                ctx_out, lat_out = pooled_banks(i)
                if i < 2:
                    pe.wait_ge(s_gs, (1, 3)[i])
                elif 2 <= i < 4 or i >= 6:
                    pe.wait_ge(s_u, i - 1)
                elif i >= 4:
                    pe.wait_ge(s_so, 2 * (i - 3))
                for lo, hi, o in ((0, CTX, ctx_out), (CTX, TOK, lat_out)):
                    for kk in range(2):
                        mm = pe.matmul(o, gT_pw[:, g, kk, m * P:(m + 1) * P], uT[:, 2 * g + kk, lo:hi],
                                       start=(kk == 0), stop=(kk == 1))
                mm.then_inc(s_pm, 1)

            pe.wait_ge(s_pw, 16)
            pe.wait_ge(s_pu, 8)
            for i in range(4):
                pool_product(i)
            pe.wait_ge(s_tabs, 2)
            for n, (d, j) in enumerate(XDD_ORDER):
                pe.wait_ge(s_xdd, n + 1)
                if j == 0:
                    for i in range(8):
                        mm = pe.matmul(psb[2 + 2 * d + i // 4][:, (i % 4) * P:(i % 4 + 1) * P],
                                       xdd[:, n % 2, i * P:(i + 1) * P],
                                       btok[:, 0, (i // 4) * N:(i // 4 + 1) * N], start=True, stop=True)
                else:
                    if n < 4:
                        pe.wait_ge(s_u, 4)
                        pe.wait_ge(s_gs, 3)
                    else:
                        pe.wait_ge(s_st, n - 3)
                    for g in range(2):
                        mm = pe.matmul(psb[(6, 0)[n % 2] + g][:, :], btok[:, j, g * N:(g + 1) * N],
                                       xdd[:, n % 2, g * 512:(g + 1) * 512], start=True, stop=True)
                mm.then_inc(s_sp, 1)
                if 2 <= n < 6:
                    pool_product(n + 2)
            pe.wait_ge(s_st, 5)
            pe.wait_ge(s_u, 8)
            project_z(0, range(KT))

            def exponents(i):
                j, hh = i // HG, 2 * (i % HG)
                o = psb[4 + i % 2]
                if i >= 2:
                    pe.wait_ge(s_ex, i - 1)
                pe.matmul(o[:, :], idb[:, :], MASK4, start=True, stop=False, skip_group_check=True)
                o4 = o[:, :].rearrange("p (h d t) -> p h d t", h=2, d=2)
                for d in range(2):
                    c = d * H + hh
                    pe.matmul(o4[:, :, d, :], tabT[d][:, j * P:(j + 1) * P],
                              nstackb[:, c:c + 2].unsqueeze(2).to_broadcast([96, 2, P]), start=False, stop=False,
                              skip_group_check=True)
                for q in range(4):
                    h, d = hh + q // 2, q % 2
                    c = d * H + h
                    mm = pe.matmul(o[:, q * P:(q + 1) * P], stackb[:, c:c + 1].to_broadcast([96, P]),
                                   tabT[d][:, j * P:(j + 1) * P], start=False, stop=True,
                                   skip_group_check=True)
                mm.then_inc(s_e, 1)

            def diagonal(i):
                j, hh = i // HG, 2 * (i % HG)
                jg = 2 * j + hh // HG
                pe.wait_ge(s_w, i + 1)
                if i == 0:
                    pe.wait_ge(s_st, 6)
                if hh % HG == 0 and jg >= 2:
                    pe.wait_ge(s_yc, jg - 1)
                for q in range(2):
                    h = hh + q
                    mm = pe.matmul(psb[jg % 2][:, (h % HG) * HD:(h % HG + 1) * HD], wbuf(i)[:, q, 0, :],
                                   xs[:, j, h * HD:(h + 1) * HD], start=True, stop=True)
                mm.then_inc(s_dg, 1)

            def from_states(jg):
                j, g = jg // 2, jg % 2
                if jg >= 3:
                    pe.wait_ge(s_yp, jg)
                for d in range(2):
                    si = j - 1 if d == 0 else 4 + j - 1
                    mm = pe.matmul(psb[2 + d][:, :], bcT[:, 2 + g, j * P:(j + 1) * P],
                                   st[:, si, g * 512:(g + 1) * 512], start=True, stop=True)
                mm.then_inc(s_off, 1)

            def turn_y(jg):
                pe.wait_ge(s_yc, jg + 1)
                if jg >= 1:
                    pe.wait_ge(s_yT, jg)
                for q in range(4):
                    k = 4 * (jg % 2) + q
                    mm = pe.transpose(psb[7][:, q * P:(q + 1) * P], xs[:, jg // 2, k * P:(k + 1) * P], ident)
                mm.then_inc(s_ytr, 1)

            def project_part(j, hf_, c, ks=range(KT)):
                n = 2 * hf_ + c
                if j == 0 and ks[0] == 0:
                    if n == 3:
                        pe.wait_ge(s_wo3, 16)
                    else:
                        pe.wait_ge(s_ring[(11 + n) % RING], 16 * ((11 + n) // RING + 1))
                w = wo[n].rearrange("p (k c) -> p k c", k=KT)
                for k in ks:
                    mm = pe.matmul(out_bank(j, hf_, c)[:, :], (yT, uT)[c][:, k, j * P:(j + 1) * P], w[:, k, :],
                                   start=(k == 0), stop=(k == KT - 1), skip_group_check=True)
                return mm

            NS = NJ * HG
            for i in range(NS + 3):
                if i < NS:
                    exponents(i)
                    if i % 4 < 3 and i // 4 + 1 < 2 * NJ:
                        project_z(i // 4 + 1, (range(0, 3), range(3, 6), range(6, 8))[i % 4])
                        if i // 4 + 1 >= 2 * NJ - 2 and i % 4 == 2:
                            pe.wait_ge(s_z, i // 4 + 2)
                            pe.sem_inc(s_used, 1)
                if NS - 3 <= i < NS + 1:
                    if i == NS - 3:
                        pe.wait_ge(s_zs, 2 * NJ)
                    project_part(0, 0, 1, range(2 * (i - NS + 3), 2 * (i - NS + 4)))
                if i >= 3:
                    k = i - 3
                    diagonal(k)
                    if k % 4 == 0 and k // 4 >= 2:
                        from_states(k // 4)
                    if k % 4 == 1 and k // 4 >= 1:
                        turn_y(k // 4 - 1)

            def project_out(j, hf_):
                if j >= 1:
                    pe.wait_ge(s_x1, 2 * (j - 1) + hf_ + 1)
                if j:
                    project_part(j, hf_, 1)
                project_part(j, hf_, 0).then_inc(s_op, 1)

            pe.wait_ge(s_yp, 2 * NJ)
            project_part(0, 1, 1)
            turn_y(2 * NJ - 1)
            pe.wait_ge(s_yT, 2 * NJ)

            def turn_h2(j):
                pe.wait_ge(s_h2, j + 1)
                if j >= 1:
                    pe.wait_ge(s_h2T, 2 * j)
                for k in range(KT):
                    mm = pe.transpose(psb[4 + k // 4][:, (k % 4) * P:(k % 4 + 1) * P],
                                      h2bufs[j % 2][:, k * P:(k + 1) * P], ident)
                mm.then_inc(s_h2t, 1)

            def router(j):
                if j == 0:
                    pe.wait_ge(s_wr, 16)
                pe.wait_ge(s_h2T, 2 * (j + 1))
                for k in range(KT):
                    mm = pe.matmul(psb[6][:, j * E:(j + 1) * E], h2T[:, k, :], wrt[:, k, :],
                                   start=(k == 0), stop=(k == KT - 1))
                mm.then_inc(s_lg, 1)

            def gate2(i, ks):
                if i == 1:
                    pe.wait_ge(s_x1, 2 * NJ)
                pe.wait_ge(s_g2w[i], 16)
                w = w_g2[i].rearrange("p (k c) -> p k c", k=KT)
                for k in ks:
                    mm = pe.matmul(psb[(7, 3)[i]][0:2, :], silc[:, 2 * k:2 * k + 2], w[:, k, :],
                                   start=(k == 0), stop=(k == KT - 1))
                if ks[-1] == KT - 1:
                    mm.then_inc(s_g2p, 1)

            for j in range(NJ):
                project_out(j, 0)
                if j >= 1:
                    turn_h2(j - 1)
                project_out(j, 1)
                if j >= 1:
                    router(j - 1)
            gate2(0, range(0, 6))
            turn_h2(NJ - 1)
            router(NJ - 1)
            gate2(0, range(6, KT))
            gate2(1, range(0, 4))
            pe.wait_ge(s_oh, 2)
            for j in range(NJ):
                for i in range(j + 1):
                    pe.matmul(psb[0][:, j * E:(j + 1) * E], strictb[:, :] if i == j else onesb[:, :],
                              onehotb[:, i * E:(i + 1) * E], start=(i == 0), stop=(i == j))
            for i in range(NJ):
                mm = pe.matmul(psb[0][:, NJ * E:(NJ + 1) * E], onesb[:, :], onehotb[:, i * E:(i + 1) * E],
                               start=(i == 0), stop=(i == NJ - 1))
            mm.then_inc(s_rk, 1)

            gate2(1, range(4, KT))
            pe.wait_ge(s_pos, 1)
            for i in range(2 * NJ):
                mm = pe.matmul(psb[5][:, 0:MAX_TILES], at_pos[:, i, :], in_tile[:, i, :],
                               start=(i == 0), stop=(i == 2 * NJ - 1))
            mm.then_inc(s_tk, 1)

            pe.wait_ge(s_rt, 1)
            k_tiles = pe.value_load(ri[0:1, 60:61], min_val=16, max_val=25)

            def turn_tokens():
                for k in range(KT):
                    mm = pe.transpose(psb[2 + k // 4][:, (k % 4) * P:(k % 4 + 1) * P],
                                      xg[:, k * P:(k + 1) * P], ident)
                mm.then_inc(s_xtp, 1)

            pe.wait_ge(s_g2c, 2)
            pe.wait_ge(s_xg, 16)
            turn_tokens()
            pe.sem_inc(s_dn, 2)
            with pe.Fori(0, k_tiles) as i:
                pe.wait_ge(s_xgT, i * 2 + 2)
                for c in range(FT):
                    pe.wait_ge(s_w_in[c], i * 16 + 16)
                    pe.wait_ge(s_ac, i * FT + (c + 1))
                    w = ex[:, c * 2048:(c + 1) * 2048].rearrange("p (a k f) -> p a k f", a=2, k=KT)
                    for a in range(2):
                        for k in range(KT):
                            mm = pe.matmul(psb[c % 2][:, a * P:(a + 1) * P], w[:, a, k, :], xgT[:, k, :],
                                           start=(k == 0), stop=(k == KT - 1))
                    mm.then_inc(s_gu, 1)
                pe.wait_ge(s_xg, i * 16 + 32)
                turn_tokens()
                pe.wait_ge(s_ac, i * FT + (FT + 2))
                pe.wait_ge(s_yo, i * 2 + 2)
                for c in range(2):
                    pe.wait_ge(s_w_in[FT + c], i * 16 + 16)
                    w = ex[:, (FT + c) * 2048:(FT + c + 1) * 2048].rearrange("p (k d) -> p k d", k=2)
                    for k in range(2):
                        for hf_ in range(2):
                            mm = pe.matmul(psb[6 + hf_][:, :], aT[:, 2 * c + k, :],
                                           w[:, k, hf_ * 512:(hf_ + 1) * 512],
                                           start=(c == 0 and k == 0), stop=(c == 1 and k == 1),
                                           skip_group_check=True)
                    mm.then_inc(s_dn, 1)

        @block.scalar
        def _(act):
            def rms(col, n=1):
                r = stat[:, col:col + n]
                act.activation(r, r, ACT.Sqrt, scale=1.0 / D, bias=eps_col[:, :]).then_inc(s_rs, 1)

            def warm(func):
                act.activation(stat[:, 26:27], eps_col[:, :], func)

            act.wait_ge(s_const, 48)
            act.activation(silc[:, :], vec[:, V_C:V_C + 16], ACT.Silu).then_inc(s_silc, 1)
            act.activation(nega[:, :], row[:, R_ALOG:R_ALOG + 32], ACT.Exp).then_inc(s_soft, 1)
            for j in range(NJ):
                act.wait_ge(s_x[j], 16)
                act.activation(junk_x, xt[:, j, :], ACT.Square, accum_out=stat[:, j:j + 1]).then_inc(s_ss, 1)
                act.wait_ge(s_ss, j + 1)
            act.wait_ge(s_cast, 1)
            rms(0, NJ)
            for n in range(4):
                act.wait_ge(s_used, n + 1)
                act.activation(arow[:, n * 512:(n + 1) * 512], psb[n][0:2, :], ACT.Copy).then_inc(s_arc, 1)
            act.wait_ge(s_mod, 1)
            act.wait_ge(s_cast, 1)
            for k in range(KT):
                act.wait_ge(s_xtr, k + 1)
                act.activation(hT[:, k, CTX:TOK], psb[6 - 2 * (k % 2)][:, :], ACT.Identity,
                               bias=modB[:, 2 * k + 1:2 * k + 2], scale=modA[:, 2 * k + 1:2 * k + 2]).then_inc(s_hs, 1)

            def silu_conv(f):
                act.wait_ge(s_conv, f + 1)
                t = f if f < 2 else f - 2
                dst = bcT[:, f, :] if f < 4 else xsT[t % 2]
                if f >= 6:
                    act.wait_ge(s_ttr, t - 1)
                act.activation(dst[:, 0:CTX], cacc[f % 2][:, 0:CTX], ACT.Silu, bias=vec[:, V_CB + f:V_CB + f + 1])
                act.activation(dst[:, CTX:TOK], cacc[f % 2][:, 131:643], ACT.Silu,
                               bias=vec[:, V_CB + f:V_CB + f + 1]).then_inc(s_cs, 1)

            def store_ada(q):
                act.wait_ge(s_adr, q + 1)
                for c in range(2):
                    act.dma_start(ada_rows[q // 2, c:c + 1, (q % 2) * 512:(q % 2 + 1) * 512],
                                  orow[q % 2][:, c * 512:(c + 1) * 512]).then_inc(s_ads[q % 2], 16)

            for f in range(20):
                if f - 2 in ADA_SUMS:
                    store_ada(ADA_SUMS.index(f - 2))
                act.wait_ge(s_fm, f + 1)
                q = 2 + 2 * (f % 3)
                if f < KT:
                    act.activation(uT[:, f, 0:CTX], psb[q + 1][:, 0:CTX], ACT.Copy)
                    act.activation(uT[:, f, CTX:TOK], psb[q][:, :], ACT.Copy).then_inc(s_vr, 1)
                else:
                    g = f - KT
                    if g == 0:
                        act.wait_ge(s_cast, 2)
                    if g >= 2:
                        act.wait_ge(s_conv, g - 1)
                    act.activation(xpad[g % 2][:, 1:1 + CTX], psb[q + 1][:, 0:CTX], ACT.Copy)
                    act.activation(xpad[g % 2][:, 132:132 + LAT], psb[q][:, :], ACT.Copy).then_inc(s_pad, 1)
                if f == 0:
                    act.wait_ge(s_dtr, 1)
                    act.activation(dtrow[:, 0:CTX], psb[1][0:32, 0:CTX], ACT.Copy)
                    act.activation(dtrow[:, CTX:TOK], psb[0][0:32, :], ACT.Copy).then_inc(s_dtc, 1)
                if f == 1:
                    act.wait_ge(s_soft, 2)
                    act.activation(sc1, sc0, ACT.Exp, scale=-1.0).then_inc(s_soft, 1)
                    act.wait_ge(s_soft, 4)
                    act.activation(ncum, etot, ACT.Ln).then_inc(s_soft, 1)
                if f == 3:
                    act.wait_ge(s_dif, 1)
                    act.activation(ecum, ncum, ACT.Exp, scale=-1.0)
                    act.activation(dec, sc0, ACT.Exp)
                    act.activation(etot, sc1, ACT.Exp).then_inc(s_dec, 1)
                if f > KT:
                    silu_conv(f - 1 - KT)
            silu_conv(CONVF - 1)
            act.wait_ge(s_tok, 10)
            for i in range(2):
                act.wait_ge(s_ads[i], 96)
            for d in range(2):
                act.dma_start(st[:, 0 if d == 0 else 7, :], states0[d]).then_inc(s_st0, 16)
            act.wait_ge(s_g, 1)
            gv = gT[:, :, :, :].rearrange("p j g n -> p (j g n)")
            act.activation(gv[:, 1024:1280], psb[1][:, 0:256], ACT.Copy).then_inc(s_gs, 1)
            act.activation(gv[:, 0:512], psb[6][:, :], ACT.Copy).then_inc(s_gs, 1)
            act.activation(gv[:, 512:1024], psb[7][:, :], ACT.Copy).then_inc(s_gs, 1)
            def scale_pooled(i):
                act.wait_ge(s_pm, i + 1)
                scale = vec[:, V_PS + i:V_PS + i + 1]
                ctx_in, lat_in = pooled_banks(i)
                if i % 2 == 0:
                    act.wait_ge(s_pm, i + 2)
                act.activation(uT[:, i, 0:CTX], ctx_in, ACT.Copy, scale=scale)
                act.activation(uT[:, i, CTX:TOK], lat_in, ACT.Copy, scale=scale).then_inc(s_u, 1)

            for i in range(4):
                scale_pooled(i)
            for n, (d, j) in enumerate(XDD_ORDER):
                if j == 0:
                    act.wait_ge(s_sp, n + 1)
                    for i in range(2):
                        act.activation(sout[d][:, i * 512:(i + 1) * 512], psb[2 + 2 * d + i][:, :],
                                       ACT.Copy).then_inc(s_so, 1)
                    act.wait_ge(s_so, 2 * (d + 1))
                    act.dma_start(s_out[d].rearrange("(i p) n -> p i n", p=P),
                                  sout[d].rearrange("p (i n) -> p i n", n=N)).then_inc(s_sout, 16)
            for i in range(4, 8):
                scale_pooled(i)

            def tanh_z(jg):
                act.wait_ge(s_z, jg + 1)
                if jg >= 3:
                    act.wait_ge(s_yc, jg - 2)
                act.activation(zbuf[jg % 3], psb[6][:, :], ACT.Tanh, scale=0.5).then_inc(s_zt, 1)

            def exps(i):
                j, hh = i // HG, 2 * (i % HG)
                act.wait_ge(s_e, i + 1)
                if i >= WBUFS:
                    act.wait_ge(s_dg, i - WBUFS + 1)
                act.activation(wbuf(i)[:, :, :, :], psb[4 + i % 2][:, :].rearrange("p (h d t) -> p h d t", h=2, d=2),
                               ACT.Exp).then_inc(s_ex, 1)

            def square_y(jg):
                act.wait_ge(s_yc, jg + 1)
                if jg >= 1:
                    act.wait_ge(s_ys, jg)
                act.activation(junk_y, xs[:, jg // 2, (jg % 2) * 512:(jg % 2 + 1) * 512], ACT.Square,
                               accum_out=stat[:, 16 + jg:17 + jg]).then_inc(s_ys, 1)

            tanh_z(0)
            for i in range(NJ * HG):
                if i % 4 == 3 and i // 4 + 1 < 2 * NJ:
                    tanh_z(i // 4 + 1)
                exps(i)
                if i % 4 == 0 and i >= 8:
                    square_y(i // 4 - 2)
            square_y(2 * NJ - 2)
            square_y(2 * NJ - 1)
            warm(ACT.Sqrt)
            act.wait_ge(s_yss, 1)
            rms(5, NJ)

            act.dma_start(wrt[:, :, :], w_router.rearrange("p (k e) -> p k e", k=KT)).then_inc(s_wr, 16)

            def copy_h2(j):
                act.wait_ge(s_h2t, j + 1)
                if j >= 1:
                    act.wait_ge(s_lg, j)
                act.activation(h2T[:, 0:4, :], psb[4][:, :].rearrange("p (k t) -> p k t", k=4),
                               ACT.Copy).then_inc(s_h2T, 1)
                act.dma_start(h2_dram[j * P:(j + 1) * P, :], h2bufs[j % 2]).then_inc(s_h2s[j % 2], 16)

            def exp_logits(part):
                act.wait_ge(s_lm, part + 1)
                lo, hi = (0, (NJ - 2) * E, NJ * E)[part:part + 2]
                act.activation(n_ex[:, lo:hi], n_sh[:, lo:hi], ACT.Exp).then_inc(s_le, 1)

            for j in range(NJ):
                if j == NJ - 1:
                    exp_logits(0)
                    warm(ACT.Sqrt)
                if j >= 1:
                    copy_h2(j - 1)
                act.wait_ge(s_x1, 2 * (j + 1))
                act.activation(junk_1, x1[:, j, :], ACT.Square, accum_out=stat[:, 10 + j:11 + j]).then_inc(s_x1s, 1)
                act.wait_ge(s_x1s, j + 1)
                rms(10 + j)
            warm(ACT.Exp)
            copy_h2(NJ - 1)
            act.dma_start(fnrow, fnorm.to_broadcast([P, D])).then_inc(s_fn, 16)
            act.dma_start(g2b, b_late[6:8, :].unsqueeze(0).to_broadcast([2, 2, 512])).then_inc(s_g2b, 16)
            exp_logits(1)
            warm(ACT.Silu)
            act.wait_ge(s_g2c, 2)
            act.dma_start(ada_rows[3, :, :].rearrange("c (i n) -> c i n", n=512), g2s).then_inc(s_g2d, 16)
            act.wait_ge(s_g2d, 16)
            act.dma_start(g2row, ada_rows[3:4].to_broadcast([P, 2, D])).then_inc(s_row2, 16)

            act.wait_ge(s_rt, 1)
            k_tiles = act.value_load(ri[0:1, 60:61], min_val=16, max_val=25)

            def copy_tokens(n):
                act.wait_ge(s_xtp, n)
                act.activation(xgT[:, 0:4, :], psb[2][:, :].rearrange("p (k t) -> p k t", k=4),
                               ACT.Copy).then_inc(s_xgT, 1)

            copy_tokens(1)
            act.sem_inc(s_yo, 2)
            act.sem_inc(s_yst, 16)
            with act.Fori(0, k_tiles) as i:
                for c in range(FT):
                    act.wait_ge(s_gu, i * FT + (c + 1))
                    act.wait_ge(s_ac, i * FT + (c + 1))
                    act.activation(sg[c % 2], psb[c % 2][:, 0:P], ACT.Silu).then_inc(s_sg, 1)
                copy_tokens(i + 2)
                act.wait_ge(s_dn, i * 2 + 4)
                act.wait_ge(s_yst, i * 16 + 16)
                act.activation(yo[:, 0:512], psb[6][:, :], ACT.Copy).then_inc(s_yo, 1)
                act.wait_ge(s_yo, i * 2 + 4)
                act.dma_start(slot_out[bass.ds(i * P, P), :], yo).then_inc(s_yst, 16)
            warm(ACT.Sqrt)
            act.wait_ge(s_yst, k_tiles * 16 + 16)

            def weigh(j):
                act.wait_ge(s_yg[j], 32)
                ya = ygb[:, 2 * j, :]
                act.activation(ya, ya, ACT.Copy, scale=gate[:, j:j + 1]).then_inc(s_ya, 1)

            for j in range(NJ - 1):
                weigh(j)
            for j in range(NJ):
                if j == 1:
                    weigh(NJ - 1)
                act.wait_ge(s_fin, j + 1)
                act.activation(junk_z, x1[:, j, :], ACT.Square, accum_out=stat[:, j:j + 1]).then_inc(s_fss, 1)
                act.wait_ge(s_fss, j + 1)
                rms(j)

        @block.gpsimd
        def _(pool):
            step = Steps(pool, s_pool)
            pool.wait_ge(s_const, 48)
            pool.tensor_copy(idb[:, :], ident)
            pool.wait_ge(s_bconst, 16)
            pool.tensor_copy(maskb[:, :, :], bcst[:, B_MASK:B_MASK + 256].rearrange("p (a b) -> p a b", a=2))
            pool.tensor_copy(strictb[:, :], bcst[:, B_STRICT:B_STRICT + P])
            pool.tensor_copy(onesb[:, :], ones)
            pool.tensor_copy(stackb[:, :], bcst[0:96, B_STACK:B_STACK + 32])
            pool.tensor_scalar(nstackb[:, :], bcst[0:96, B_STACK:B_STACK + 32], -1.0, None, ALU.mult)
            pool.memset(eps_col[:, :], EPS)
            pool.tensor_tensor(dsum[:, :], row[:, R_DSK:R_DSK + H], row[:, R_DSK + H:R_DSK + 2 * H],
                               ALU.add).then_inc(s_cast, 1)
            pool.wait_ge(s_hs, KT)
            pool.wait_ge(s_hc, KT)
            pool.memset(xpad[0], 0.0)
            pool.memset(xpad[1], 0.0).then_inc(s_cast, 1)
            pool.wait_ge(s_cast, 1)
            pool.wait_ge(s_inv, 16)
            iv = [(invb[:, g * TOK:g * TOK + CTX], invb[:, g * TOK + CTX:(g + 1) * TOK]) for g in range(4)]
            for f in range(8):
                g = f // 2
                w = WINDOWS[g]
                lw = g + 1
                v = uT[:, f, :]
                pool.wait_ge(s_vr, f + 1)
                L = CTX + w - 1
                step(pool.memset(pa[:, 0:L], 0.0))
                step(pool.tensor_copy(pa[:, w // 2:w // 2 + CTX], v[:, 0:CTX]))
                src, dst = pa, pb_
                for q in range(lw):
                    L -= 1 << q
                    step(pool.tensor_tensor(dst[:, 0:L], src[:, 0:L], src[:, (1 << q):(1 << q) + L], ALU.add))
                    src, dst = dst, (pc if dst is pb_ else pb_)
                step(pool.tensor_tensor(dst[:, 0:CTX], src[:, 0:CTX], iv[g][0], ALU.mult))
                step(pool.tensor_tensor(uT[:, f, 0:CTX], dst[:, 0:CTX], v[:, 0:CTX], ALU.subtract))
                L = GRID_W + w - 1

                def grid(b, n, ww=None):
                    ww = ww or L0
                    return b[:, 0:n * ww].rearrange("p (r c) -> p r c", r=n)

                L0 = L
                vg = v[:, CTX:TOK].rearrange("p (r c) -> p r c", r=ROWS)
                step(pool.memset(pa[:, 0:ROWS * L0], 0.0))
                step(pool.tensor_copy(grid(pa, ROWS)[:, :, w // 2:w // 2 + GRID_W], vg))
                src, dst = pa, pb_
                for q in range(lw):
                    L -= 1 << q
                    s3, d3 = grid(src, ROWS), grid(dst, ROWS)
                    step(pool.tensor_tensor(d3[:, :, 0:L], s3[:, :, 0:L], s3[:, :, (1 << q):(1 << q) + L], ALU.add))
                    src, dst = dst, (pc if dst is pb_ else pb_)
                col = grid(src, ROWS)[:, :, 0:GRID_W]
                if w // 2 >= ROWS:
                    n = ROWS // 2
                    s3 = col
                    while n:
                        d3 = grid(dst, n, GRID_W)
                        step(pool.tensor_tensor(d3, s3[:, 0:n, :], s3[:, n:2 * n, :], ALU.add))
                        s3 = d3
                        src, dst = dst, (pc if dst is pb_ else pb_)
                        n //= 2
                    total = s3.to_broadcast([P, ROWS, GRID_W])
                else:
                    n = ROWS + w - 1
                    step(pool.memset(pa[:, 0:n * GRID_W], 0.0))
                    step(pool.tensor_copy(grid(pa, n, GRID_W)[:, w // 2:w // 2 + ROWS, :], col))
                    src, dst = pa, pb_
                    for q in range(lw):
                        n -= 1 << q
                        s1, d1 = src[:, 0:(n + (1 << q)) * GRID_W], dst[:, 0:n * GRID_W]
                        step(pool.tensor_tensor(d1, s1[:, 0:n * GRID_W], s1[:, (1 << q) * GRID_W:], ALU.add))
                        src, dst = dst, (pc if dst is pb_ else pb_)
                    total = grid(src, ROWS, GRID_W)
                m3 = grid(dst, ROWS, GRID_W)
                step(pool.tensor_tensor(m3, total, iv[g][1].rearrange("p (r c) -> p r c", r=ROWS), ALU.mult))
                pool.tensor_tensor(uT[:, f, CTX:TOK].rearrange("p (r c) -> p r c", r=ROWS), m3, vg,
                                   ALU.subtract).then_inc(s_pu, 1)
                pool.wait_ge(s_pu, f + 1)
            step(pool.memset(zero_f, 0.0))
            for t in range(E, MAX_TILES - 1):
                pool.dma_start(slot_out[t * P:(t + 1) * P, :], zero_f).then_inc(s_zero, 16)

            pool.wait_ge(s_adr, 6)
            pool.dma_start(gT_pw, w_pool.rearrange("p (g k m) -> p g k m", g=4, k=2)).then_inc(s_pw, 16)

            def scaled(out, x_, factors):
                return pool.tensor_tensor(out.rearrange("p (h d) -> p h d", d=HD),
                                          x_.rearrange("p (h d) -> p h d", d=HD),
                                          factors.unsqueeze(2).to_broadcast([P, factors.shape[1], HD]), ALU.mult)

            pool.wait_ge(s_tok, 10)
            pool.wait_ge(s_dtd, 1)
            for n, (d, j) in enumerate(XDD_ORDER):
                if n >= 2:
                    pool.wait_ge(s_sp, n - 1)
                c = j * 32 + d * H
                scaled(xdd[:, n % 2, :], xs[:, j, :], dtdec[:, c:c + H]).then_inc(s_xdd, 1)
            for i in range(NJ * HG):
                j, hh = i // HG, 2 * (i % HG)
                pool.wait_ge(s_ex, i + 1)
                dt_h = dt_[:, j * 32:(j + 1) * 32].rearrange("p (d h) -> p h d", d=2)[:, hh:hh + 2, :]
                pool.tensor_tensor(wbuf(i)[:, :, :, :], wbuf(i)[:, :, :, :],
                                   dt_h.unsqueeze(3).to_broadcast([P, 2, 2, P]), ALU.mult).then_inc(s_wd, 1)

            pool.wait_ge(s_rt, 1)
            pool.wait_ge(s_h2s[0], 48)
            pool.wait_ge(s_h2s[1], 32)

            def gather(numbers):
                pool.indirect_dma_start(xg, None, h2_dram,
                                        bass.IndirectOffsetOnAxis(ap=numbers, axis=0),
                                        bounds_check=TOK - 1, oob_is_err=False).then_inc(s_xg, 16)

            gather(token_of[:, 0:1])
            k_tiles = pool.value_load(ri[0:1, 60:61], min_val=16, max_val=25)
            with pool.Fori(0, k_tiles) as i:
                pool.wait_ge(s_xg, i * 16 + 16)
                pool.sem_inc(s_begun, 1)
                pool.tensor_copy(idx[:, 0:1], token_of[:, bass.ds(i + 1, 1)]).then_inc(s_idx, 1)
                pool.wait_ge(s_idx, i + 1)
                pool.wait_ge(s_xtp, i + 1)
                pool.sem_inc(s_begun, 1)
                gather(idx[:, 0:1])
            pool.wait_ge(s_yst, k_tiles * 16 + 16)
            pool.sem_inc(s_begun, 1)
            pool.wait_ge(s_zero, 16 * (MAX_TILES - 1 - E))
            for j in range(NJ):
                for a in range(2):
                    n = 2 * j + a
                    pool.indirect_dma_start(ygb[:, n, :], None, slot_out,
                                            bass.IndirectOffsetOnAxis(ap=ri[:, 40 + a * NJ + j:41 + a * NJ + j], axis=0),
                                            bounds_check=SLOTS - P - 1, oob_is_err=False).then_inc(s_yg[j], 16)
            pool.wait_ge(s_row2, 32)
            for j in range(NJ - 1):
                pool.wait_ge(s_mix, j + 1)
                yb = ygb[:, 2 * j + 1, :]
                pool.tensor_tensor(yb, yb, g2row[:, min(j, 1), :], ALU.mult).then_inc(s_gm, 1)

        @block.vector
        def _(dve):
            step = Steps(dve, s_dve)
            tt, ts, stt = dve.tensor_tensor, dve.tensor_scalar, dve.scalar_tensor_tensor
            dve.wait_ge(s_const, 48)
            dve.wait_ge(s_rs, 1)
            step(dve.reciprocal(stat[:, 0:NJ], stat[:, 0:NJ]))
            for j in range(NJ):
                ts(xt[:, j, :], xt[:, j, :], stat[:, j:j + 1], None, ALU.mult).then_inc(s_xn, 1)
            dve.wait_ge(s_ar, 1)
            tt(modB[:, :], psb[4][:, 0:16], vec[:, V_ADA:V_ADA + 16], ALU.add)
            step(tt(modA[:, :], psb[4][:, 16:32], vec[:, V_ADA + 16:V_ADA + 32], ALU.add))
            stt(modA[:, :], modA[:, :], 1.0, vec[:, V_N1:V_N1 + 16], ALU.add, ALU.mult).then_inc(s_mod, 1)
            dve.wait_ge(s_mod, 1)
            for k in range(KT):
                dve.wait_ge(s_xtr, k + 1)
                ts(hT[:, k, 0:CTX], psb[7 - 2 * (k % 2)][:, 0:CTX], modA[:, 2 * k:2 * k + 1], modB[:, 2 * k:2 * k + 1],
                   ALU.mult, ALU.add).then_inc(s_hc, 1)
            def ada_half(u):
                q = u // 2
                if u % 2 == 0 and q >= 2:
                    dve.wait_ge(s_ada, q - 1)
                dve.wait_ge(s_adaw[u % 2], 16 * (u // 2 + 1))
                for kk in range(4):
                    k = 4 * (u % 2) + kk
                    for c in range(2):
                        a = acc[q % 2][:, c * 512:(c + 1) * 512]
                        w, s_c = adaw[u % 2][:, kk, :], silc[:, 2 * k + c:2 * k + c + 1]
                        if k:
                            dve.wait_ge(s_accs, 16 * q + 2 * k + c - 1)
                            ins = stt(a, w, s_c, a, ALU.mult, ALU.add)
                        else:
                            ins = ts(a, w, s_c, None, ALU.mult)
                        ins.then_inc(s_accs, 1)
                dve.wait_ge(s_accs, 16 * q + 8 * (u % 2) + 8)
                dve.sem_inc(s_acc, 1)

            dve.wait_ge(s_silc, 1)
            for u in range(4):
                ada_half(u)
            dve.wait_ge(s_dtp, 1)
            step(tt(dt_.rearrange("p (j h) -> p j h", j=NJ), psb[0][:, 0:160].rearrange("p (j h) -> p j h", j=NJ),
                    row[:, R_DTB:R_DTB + 32].unsqueeze(1).to_broadcast([P, NJ, 32]), ALU.add))
            dve.wait_ge(s_soft, 1)
            step(ts(sc0, dt_, -1.0, None, ALU.mult))
            tt(sc0, sc0, dt_, ALU.max).then_inc(s_soft, 1)
            dve.wait_ge(s_soft, 2)
            step(ts(dt_, dt_, 0.0, None, ALU.max))
            dve.wait_ge(s_soft, 3)
            ts(etot, sc1, 1.0, None, ALU.add).then_inc(s_soft, 1)
            dve.wait_ge(s_soft, 4)
            step(ts(sc0, etot, -1.0, None, ALU.add))
            step(tt(sc0, sc1, sc0, ALU.subtract))
            step(dve.reciprocal(sc1, etot))
            step(tt(sc0, sc0, sc1, ALU.mult))
            dve.wait_ge(s_soft, 5)
            step(tt(sc0, sc0, ncum, ALU.add))
            step(tt(dt_, dt_, sc0, ALU.add))
            step(tt(a_.rearrange("p (j h) -> p j h", j=NJ), dt_.rearrange("p (j h) -> p j h", j=NJ),
                    nega[:, :].unsqueeze(1).to_broadcast([P, NJ, 32]), ALU.mult))
            ts(a_, a_, -1.0, None, ALU.mult).then_inc(s_a, 1)
            def ada_rows_out(q):
                dve.wait_ge(s_ada, q + 1)
                dve.wait_ge(s_brow, 16)
                if q >= 2:
                    dve.wait_ge(s_ads[q % 2], 32 * (q // 2))
                for c in range(2):
                    o = orow[q % 2][:, c * 512:(c + 1) * 512]
                    ins = tt(o, psb[c][0:1, :], brow[:, q * 512:(q + 1) * 512], ALU.add)
                    if q // 2 == 2:
                        step(ins)
                        dve.wait_ge(s_n2, 16)
                        ins = stt(o, o, 1.0, n2row[:, (q % 2) * 512:(q % 2 + 1) * 512], ALU.add, ALU.mult)
                ins.then_inc(s_adr, 1)

            dve.wait_ge(s_cum, 1)
            step(ts(ncum, psb[0][:, 0:160], -1.0, None, ALU.mult))
            tt(sc0, psb[0][:, 160:320], ncum, ALU.add)
            dve.tensor_copy(sc1, psb[0][:, 160:320]).then_inc(s_dif, 1)

            dve.wait_ge(s_dec, 1)
            tt(dtdec, dt_, dec, ALU.mult).then_inc(s_dtd, 1)
            for q in range(1, 6):
                if q >= 2:
                    ada_half(2 * q)
                    ada_half(2 * q + 1)
                ada_rows_out(q - 1)
            ada_rows_out(5)


            def token_major(t):
                dve.wait_ge(s_ttr, t + 1)
                if t == 2:
                    for i in range(2):
                        dve.wait_ge(s_ads[i], 96)
                dst = btok[:, :, t * N:(t + 1) * N] if t < 2 else xs[:, :, (t - 2) * P:(t - 1) * P]
                dve.tensor_copy(dst[:, 0, :], psb[1][:, 0:P])
                dve.tensor_copy(dst[:, 1:NJ, :], psb[0][:, :].rearrange("p (j n) -> p j n", n=P)).then_inc(s_tok, 1)

            for f in range(CONVF):
                dve.wait_ge(s_pad, f + 1)
                if f >= 2:
                    dve.wait_ge(s_cs, f - 1)
                for q in range(4):
                    wq = vec[:, V_CW + 4 * f + q:V_CW + 4 * f + q + 1]
                    if q == 0:
                        step(ts(cacc[f % 2], xpad[f % 2][:, 0:643], wq, None, ALU.mult))
                    else:
                        ins = stt(cacc[f % 2], xpad[f % 2][:, q:q + 643], wq, cacc[f % 2], ALU.mult, ALU.add)
                        if q < 3:
                            step(ins)
                        else:
                            ins.then_inc(s_conv, 1)
                if f == 4:
                    token_major(0)
                if f >= 5:
                    token_major(f - 4)
            token_major(8)
            token_major(9)
            for d in range(2):
                dve.wait_ge(s_tab, d + 1)
                dve.wait_ge(s_g, 1)
                t = tabT[d]
                for lo, hi, src in ((0, CTX, psb[3 + 2 * d][0:32, 0:CTX]), (CTX, TOK, psb[2 + 2 * d][0:32, :])):
                    if d == 0 and lo == 0:
                        for i in range(2):
                            dve.wait_ge(s_ads[i], 96)
                    r1, r2 = split_r[0][:, lo:hi], split_r[1][:, lo:hi]
                    step(dve.tensor_copy(t[0:32, lo:hi], src))
                    step(tt(r1, src, t[0:32, lo:hi], ALU.subtract))
                    step(dve.tensor_copy(mid[:, lo:hi], r1))
                    step(dve.tensor_copy(t[32:64, lo:hi], mid[:, lo:hi]))
                    step(tt(r2, r1, mid[:, lo:hi], ALU.subtract))
                    ins = dve.tensor_copy(t[64:96, lo:hi], r2)
                    if lo == 0:
                        step(ins)
                ins.then_inc(s_tabs, 1)
                dve.wait_ge(s_tabs, d + 1)
            dve.wait_ge(s_dec, 1)
            dve.wait_ge(s_st0, 32)
            dve.wait_ge(s_zero, 16 * (MAX_TILES - 1 - E))

            def heads(ap):
                return ap.rearrange("p (h d) -> p h d", d=HD)

            def state(n):
                d, j = XDD_ORDER[n]
                if j == 0:
                    return
                dve.wait_ge(s_sp, n + 1)
                b = (6, 0)[n % 2]
                si = j - 1 if d == 0 else 4 + j - 1
                so = si + 1 if d == 0 else si - 1
                c = j * 32 + d * H
                step(tt(heads(st[:, so, :]), heads(st[:, si, :]),
                        etot[:, c:c + H].unsqueeze(2).to_broadcast([P, H, HD]), ALU.mult))
                tt(st[:, so, 0:512], st[:, so, 0:512], psb[b][:, :], ALU.add)
                ins = tt(st[:, so, 512:1024], st[:, so, 512:1024], psb[b + 1][:, :], ALU.add)
                ins.then_inc(s_st, 1)
                dve.wait_ge(s_st, n - 1)

            for n in range(len(XDD_ORDER)):
                state(n)

            def decay_scores(i):
                j, hh = i // HG, 2 * (i % HG)
                dve.wait_ge(s_wd, i + 1)
                if i == 0:
                    dve.wait_ge(s_gs, 3)
                w = wbuf(i)
                step(tt(w.rearrange("p h d t -> p (h d) t"), w.rearrange("p h d t -> p (h d) t"),
                        gT[:, j, hh // HG, :].unsqueeze(1).to_broadcast([P, 4, P]), ALU.mult))
                tt(w[:, :, 0, :], w[:, :, 0, :], w[:, :, 1, :], ALU.add).then_inc(s_w, 1)

            def silu_z(jg):
                dve.wait_ge(s_zt, jg + 1)
                stt(zbuf[jg % 3], zbuf[jg % 3], 1.0, psb[6][:, :], ALU.add, ALU.mult).then_inc(s_zs, 1)

            def per_head(ap):
                return ap.unsqueeze(2).to_broadcast([P, HG, HD])

            def begin_outputs(jg):
                j, g = jg // 2, jg % 2
                c = j * 32 + g * HG
                ins = tt(heads(yt[0]), heads(xs[:, j, g * 512:(g + 1) * 512]),
                         per_head(dsum[:, g * HG:(g + 1) * HG]), ALU.mult)
                if j:
                    step(ins)
                    dve.wait_ge(s_off, jg - 1)
                    for d in range(2):
                        step(tt(heads(yt[1]), heads(psb[2 + d][:, :]), per_head(ecum[:, c + d * H:c + d * H + HG]),
                                ALU.mult))
                        ins = tt(yt[0], yt[0], yt[1], ALU.add)
                        if d == 0:
                            step(ins)
                ins.then_inc(s_yp, 1)

            def end_outputs(jg):
                j, g = jg // 2, jg % 2
                dve.wait_ge(s_yp, jg + 1)
                dve.wait_ge(s_dg, 4 * (jg + 1))
                step(tt(yt[0], yt[0], psb[jg % 2][:, :], ALU.add))
                dve.wait_ge(s_zs, jg + 1)
                stt(xs[:, j, g * 512:(g + 1) * 512], yt[0], 0.5, zbuf[jg % 3], ALU.mult, ALU.mult).then_inc(s_yc, 1)
                dve.wait_ge(s_yc, jg + 1)

            def copy_y(jg):
                if jg == 0:
                    dve.wait_ge(s_sout, 32)
                dve.wait_ge(s_ytr, jg + 1)
                j, k = jg // 2, 4 * (jg % 2)
                tt(yT[:, k:k + 4, j * P:(j + 1) * P], psb[7][:, :].rearrange("p (k t) -> p k t", k=4),
                   vec[:, V_SN + k:V_SN + k + 4].unsqueeze(2).to_broadcast([P, 4, P]), ALU.mult).then_inc(s_yT, 1)

            silu_z(0)
            for i in range(NJ * HG):
                if i % 4 == 3 and i // 4 + 1 < 2 * NJ:
                    silu_z(i // 4 + 1)
                decay_scores(i)
                if i % 4 == 1 and i >= 8:
                    copy_y(i // 4 - 2)
                if i % 4 == 2 and i >= 4:
                    end_outputs(i // 4 - 1)
                if i % 4 == 3:
                    begin_outputs(i // 4)
            copy_y(2 * NJ - 2)
            end_outputs(2 * NJ - 1)
            dve.wait_ge(s_ys, 2 * NJ)
            sums = stat[:, 16:26].rearrange("p (j g) -> p j g", g=2)
            tt(stat[:, 5:10].unsqueeze(2), sums[:, :, 0:1], sums[:, :, 1:2], ALU.add).then_inc(s_yss, 1)
            copy_y(2 * NJ - 1)
            dve.wait_ge(s_rs, 2)
            step(dve.reciprocal(stat[:, 5:10], stat[:, 5:10]))

            dve.wait_ge(s_rowl, 32)
            dve.wait_ge(s_xr[0], 16 * (NJ - 1))

            def h2_copy(j):
                dve.wait_ge(s_h2t, j + 1)
                if j >= 1:
                    dve.wait_ge(s_lg, j)
                dve.tensor_copy(h2T[:, 4:8, :], psb[5][:, :].rearrange("p (k t) -> p k t", k=4)).then_inc(s_h2T, 1)

            room = [rw_a, 160]

            def new(*shape):
                n = int(np.prod(shape))
                room[1] += n
                v = room[0][:, room[1] - n:room[1]]
                return v if len(shape) == 1 else v.rearrange("p (a b) -> p a b", b=shape[1])

            def over(ap, n):
                return ap.unsqueeze(2).to_broadcast([P, ap.shape[1], n])

            def across(ap, n):
                return ap.unsqueeze(1).to_broadcast([P, n, ap.shape[1]])

            def largest(out, in_):
                step(dve.tensor_reduce(out, in_, AX_X, ALU.max))

            def total(out, in_):
                step(dve.tensor_reduce(out, in_, AX_X, ALU.add))

            chosen, weight, norm = [new(NJ, E), new(NJ, E)], [new(NJ), new(NJ)], new(NJ)
            scratch_from = room[1]

            def choose(j0, j1):
                nj = j1 - j0
                room[1] = scratch_from

                def je(ap):
                    return ap[:, j0 * E:j1 * E].rearrange("p (j e) -> p j e", e=E)

                dve.wait_ge(s_lg, j1)
                logits = je(psb[6])
                top = new(nj)
                largest(top, logits)
                tt(je(n_sh), logits, over(top, E), ALU.subtract).then_inc(s_lm, 1)
                dve.wait_ge(s_le, 2 if j0 else 1)
                probs, sel, tot = new(nj, E), new(nj, E), new(nj)
                total(tot, je(n_ex))
                step(dve.reciprocal(tot, tot))
                step(tt(probs, je(n_ex), over(tot, E), ALU.mult))
                step(tt(sel, probs, across(row[:, R_RB:R_RB + E], nj), ALU.add))
                s4 = sel.rearrange("p j (g e) -> p (j g) e", g=EG)
                pairs = new(nj * EG, 6)
                tt(pairs[:, :, 0:3], s4[:, :, 0:3], s4[:, :, 1:4], ALU.add)
                tt(pairs[:, :, 3:5], s4[:, :, 0:2], s4[:, :, 2:4], ALU.add)
                step(tt(pairs[:, :, 5:6], s4[:, :, 0:1], s4[:, :, 3:4], ALU.add))
                score, pick, in_group = new(nj * EG), new(nj, EG), new(nj, EG)
                largest(score, pairs)
                s5 = score.rearrange("p (j g) -> p j g", g=EG)
                largest(top, s5)
                step(tt(pick, s5, over(top, EG), ALU.is_equal))
                step(tt(pick, pick, across(cst[:, C_P4:C_P4 + EG], nj), ALU.mult))
                largest(top, pick)
                step(tt(in_group, pick, over(top, EG), ALU.is_equal))
                low, cand = new(nj * EG), new(nj, E)
                ing = in_group.rearrange("p j g -> p (j g)")
                step(ts(low, ing, BIG, -BIG, ALU.mult, ALU.add))
                c4 = cand.rearrange("p j (g e) -> p (j g) e", g=EG)
                step(tt(c4, s4, over(ing, EPG), ALU.mult))
                step(tt(c4, c4, over(low, EPG), ALU.add))
                prio = new(nj, E)
                for a in range(2):
                    ch = chosen[a][:, j0:j1, :]
                    largest(top, cand)
                    step(tt(prio, cand, over(top, E), ALU.is_equal))
                    step(tt(prio, prio, across(cst[:, C_P16:C_P16 + E], nj), ALU.mult))
                    largest(top, prio)
                    step(tt(ch, prio, over(top, E), ALU.is_equal))
                    if a == 0:
                        step(stt(cand, ch, -3 * BIG, cand, ALU.mult, ALU.add))
                tt(je(onehotb), chosen[0][:, j0:j1, :], chosen[1][:, j0:j1, :], ALU.add).then_inc(s_oh, 1)
                for a in range(2):
                    step(tt(prio, chosen[a][:, j0:j1, :], probs, ALU.mult))
                    total(weight[a][:, j0:j1], prio)

            for j in range(NJ):
                cd = min(j, 1)
                if j == NJ - 1:
                    choose(0, NJ - 2)
                    dve.wait_ge(s_xr[1], 16)
                for hf_ in range(2):
                    cols = slice(hf_ * 512, (hf_ + 1) * 512)
                    n = 2 * j + hf_
                    if hf_ and j >= 1:
                        h2_copy(j - 1)
                    dve.wait_ge(s_op, n + 1)
                    step(dve.tensor_copy(x1t, out_bank(j, hf_, 1)[:, :]))
                    step(stt(x1t, psb[hf_][:, :], stat[:, 5 + j:6 + j], x1t, ALU.mult, ALU.add))
                    step(tt(x1t, x1t, g1row[:, cd, cols], ALU.mult))
                    tt(x1[:, j, cols], x1[:, j, cols], x1t, ALU.add).then_inc(s_x1, 1)
                    dve.wait_ge(s_x1, n + 1)
                if j == 0:
                    dve.wait_ge(s_row2, 16)
                dve.wait_ge(s_rs, 3 + j)
                r = stat[:, 10 + j:11 + j]
                step(dve.reciprocal(r, r))
                if j >= 2:
                    dve.wait_ge(s_h2s[j % 2], 16 * (j // 2))
                    dve.wait_ge(s_h2t, j - 1)
                step(stt(h2bufs[j % 2], x1[:, j, :], r, a2row[:, cd, :], ALU.mult, ALU.mult))
                tt(h2bufs[j % 2], h2bufs[j % 2], b2row[:, cd, :], ALU.add).then_inc(s_h2, 1)
                dve.wait_ge(s_h2, j + 1)

            h2_copy(NJ - 1)
            choose(NJ - 2, NJ)
            room[:] = [rw_b, 0]
            step(tt(norm, weight[0], weight[1], ALU.add))
            step(dve.reciprocal(norm, norm))
            for a in range(2):
                step(tt(gate[:, a * NJ:(a + 1) * NJ], weight[a], norm, ALU.mult))
            dve.wait_ge(s_rk, 1)
            tiles, ends, base, steps = new(E), new(E), new(E), new(E, 4)
            step(tt(steps, over(psb[0][:, NJ * E:(NJ + 1) * E], 4), across(cst[:, C_STEP:C_STEP + 4], E), ALU.is_gt))
            total(tiles, steps)
            step(ts(tiles, tiles, 1.0, None, ALU.add))
            step(dve.tensor_tensor_scan(ends, ones[:, 0:E], tiles, 0.0, ALU.mult, ALU.add))
            step(tt(base, ends, tiles, ALU.subtract))
            step(ts(base, base, float(P), None, ALU.mult))
            slots, mine, place = new(NJ, E), new(NJ, E), new(2 * NJ)
            step(tt(slots, psb[0][:, 0:NJ * E].rearrange("p (j e) -> p j e", e=E), across(base, NJ), ALU.add))
            for a in range(2):
                step(tt(mine, chosen[a], slots, ALU.mult))
                total(place[:, a * NJ:(a + 1) * NJ], mine)
            reached, tile_of, pos = new(2 * NJ, MAX_TILES + 1), new(2 * NJ), new(2 * NJ)
            starts = cst[:, C_START:C_START + MAX_TILES + 1]
            step(tt(reached, over(place, MAX_TILES + 1), across(starts, 2 * NJ), ALU.is_ge))
            total(tile_of, reached)
            step(ts(tile_of, tile_of, -float(P), float(P), ALU.mult, ALU.add))
            step(tt(pos, place, tile_of, ALU.add))
            step(tt(in_tile, reached[:, :, 0:MAX_TILES], reached[:, :, 1:MAX_TILES + 1], ALU.subtract))
            tt(at_pos, over(pos, P), across(cst[:, C_POS:C_POS + P], 2 * NJ), ALU.is_equal)
            step(tt(in_tile, in_tile, over(cst[:, C_TOKEN:C_TOKEN + 2 * NJ], MAX_TILES), ALU.mult))
            dve.sem_inc(s_pos, 1)
            dve.tensor_copy(ri[:, 40:40 + 2 * NJ], place)
            past, owner = new(28, E), new(28)
            step(tt(past, across(ends, 28), over(cst[:, C_ITEM:C_ITEM + 28], E), ALU.is_le))
            total(owner, past)
            step(ts(owner, owner, float(E - 1), None, ALU.min))
            dve.tensor_copy(ri[:, 0:28], owner)
            dve.tensor_copy(ri[:, 60:61], ends[:, E - 1:E])
            dve.wait_ge(s_tk, 1)
            dve.tensor_copy(token_of[:, 0:MAX_TILES], psb[5][:, 0:MAX_TILES]).then_inc(s_rt, 1)
            dve.wait_ge(s_g2b, 16)
            for i in range(2):
                dve.wait_ge(s_g2p, i + 1)
                tt(g2s[:, i, :], psb[(7, 3)[i]][0:2, :], g2b[:, i, :], ALU.add).then_inc(s_g2c, 1)

            dve.wait_ge(s_rt, 1)
            k_tiles = dve.value_load(ri[0:1, 60:61], min_val=16, max_val=25)
            dve.sem_inc(s_ac, 2)

            def copy_tokens(n):
                dve.wait_ge(s_xtp, n)
                dve.tensor_copy(xgT[:, 4:8, :], psb[3][:, :].rearrange("p (k t) -> p k t", k=4)).then_inc(s_xgT, 1)

            copy_tokens(1)
            with dve.Fori(0, k_tiles) as i:
                dve.wait_ge(s_dn, i * 2 + 2)
                for c in range(FT):
                    dve.wait_ge(s_sg, i * FT + (c + 1))
                    tt(aT[:, c, :], sg[c % 2], psb[c % 2][:, P:2 * P], ALU.mult).then_inc(s_ac, 1)
                copy_tokens(i + 2)
                dve.wait_ge(s_dn, i * 2 + 4)
                dve.wait_ge(s_yst, i * 16 + 16)
                dve.tensor_copy(yo[:, 512:1024], psb[7][:, :]).then_inc(s_yo, 1)

            dve.wait_ge(s_row2, 32)
            dve.wait_ge(s_fn, 16)

            def mix(j):
                dve.wait_ge(s_ya, j + 1)
                ya = ygb[:, 2 * j, :]
                yb = ygb[:, 2 * j + 1, :]
                stt(yb, yb, gate[:, NJ + j:NJ + j + 1], ya, ALU.mult, ALU.add).then_inc(s_mix, 1)

            def residual(j):
                yb = ygb[:, 2 * j + 1, :]
                if j < NJ - 1:
                    dve.wait_ge(s_gm, j + 1)
                else:
                    dve.wait_ge(s_mix, NJ)
                    step(tt(yb, yb, g2row[:, 1, :], ALU.mult))
                tt(x1[:, j, :], x1[:, j, :], yb, ALU.add).then_inc(s_fin, 1)

            def final_norm(j):
                dve.wait_ge(s_rs, 3 + NJ + j)
                r = stat[:, j:j + 1]
                step(dve.reciprocal(r, r))
                if j >= 2:
                    dve.wait_ge(s_ost[j % 2], 16 * (j // 2))
                stt(fout[j % 2], x1[:, j, :], r, fnrow, ALU.mult, ALU.mult).then_inc(s_fo, 1)

            for j in range(NJ):
                mix(j)
                if j >= 2:
                    residual(j - 2)
                if j >= 3:
                    final_norm(j - 3)
            residual(NJ - 2)
            final_norm(NJ - 3)
            residual(NJ - 1)
            final_norm(NJ - 2)
            final_norm(NJ - 1)


def layout(a):
    f = np.float32
    p = np.arange(P)
    cst = np.zeros((P, C_ALL), f)
    cst[:, C_ID:C_ID + P] = np.eye(P)
    cst[:, C_TRIF:C_TRIF + P] = p[:, None] <= p[None]
    cst[:, C_TRIB:C_TRIB + P] = p[:, None] >= p[None]
    cst[:, C_ONES:C_ONES + P] = 1
    cst[:, C_P16:C_P16 + E] = E - np.arange(E)
    cst[:, C_P4:C_P4 + EG] = EG - np.arange(EG)
    cst[:, C_ITEM:C_ITEM + 28] = np.arange(28)
    cst[:, C_STEP:C_STEP + 4] = P * (1 + np.arange(4))
    cst[:, C_TOKEN:C_TOKEN + 2 * NJ] = p[:, None] + P * (np.arange(2 * NJ) % NJ)
    cst[:, C_START:C_START + MAX_TILES + 1] = P * np.arange(MAX_TILES + 1)
    cst[:, C_POS:C_POS + P] = p
    bc = np.zeros((P, B_ALL), f)
    bc[:, B_STRICT:B_STRICT + P] = p[:, None] < p[None]
    bc[:, B_MASK:B_MASK + P] = np.where(p[:, None] > p[None], -BIG, 0)
    bc[:, B_MASK + P:B_MASK + 2 * P] = np.where(p[:, None] < p[None], -BIG, 0)
    bc[:96, B_STACK:B_STACK + 32] = np.arange(96)[:, None] % 32 == np.arange(32)

    def cols(v, n):
        return np.asarray(v, f).reshape(n, P).T

    vec = np.zeros((P, V_ALL), f)
    vec[:, V_ADA:V_ADA + 96] = np.repeat(cols(a["b_ada"][0], 48), 2, axis=1)
    vec[:, V_N1:V_N1 + 16] = np.repeat(cols(a["norm1_w"][0], KT), 2, axis=1)
    vec[:, V_N2:V_N2 + 16] = np.repeat(cols(a["norm2_w"][0], KT), 2, axis=1)
    order = np.r_[D:D + 512, 0:D]
    vec[:, V_CW:V_CW + 48] = a["conv_w"][0][:, order].reshape(4, CONVF, P).transpose(2, 1, 0).reshape(P, 48)
    vec[:, V_CB:V_CB + CONVF] = cols(a["conv_b"][0][order], CONVF)
    vec[:, V_PS:V_PS + 8] = cols(a["pool_scale"][0], KT)
    vec[:, V_SN:V_SN + 8] = cols(a["ssd_norm_w"][0], KT)
    vec[:, V_C:V_C + 16] = np.stack([cols(a["c_ctx"], KT), cols(a["c"][0], KT)], axis=2).reshape(P, 16)
    row = np.concatenate([np.asarray(a["router_bias"], f), a["dt_bias"][0].reshape(-1), a["a_log"][0].reshape(-1),
                          a["d_skip"][0].reshape(-1)])[None]

    def count(n, w):
        i = np.arange(n)
        return np.clip(i + w // 2 - 1, 0, n - 1) - np.clip(i - w // 2, 0, n - 1) + 1

    inv = np.concatenate([np.concatenate([1 / count(CTX, w), (1 / np.outer(count(ROWS, w), count(GRID_W, w))).ravel()])
                          for w in WINDOWS]).astype(f)[None]
    w_ada, w_in, w_out = a["w_ada"][0], a["w_in"][0], a["w_out"][0]

    def chunk(w, c0):
        return w[:, c0:c0 + 512].reshape(KT, P, 512).transpose(1, 0, 2).reshape(P, CHUNK)

    x0 = D
    v0 = D + D + 512 + 32
    parts = [chunk(w_ada, 512 * i) for i in range(4)]
    parts += [chunk(w_in, c0) for c0 in (v0, v0 + 512, x0 + D, x0, x0 + 512, 0, 512)]
    w_late = np.stack([chunk(w_ada, 512 * q)[:, i * 2048:(i + 1) * 2048] for q in range(4, 10) for i in range(2)])
    parts += [chunk(w_out[c * D:(c + 1) * D], h * 512) for h in range(2) for c in range(2)]
    parts += [chunk(w_ada, 512 * q) for q in (10, 11)]
    w_dt = w_in[:, v0 - 32:v0].reshape(KT, P, 32).transpose(1, 0, 2).reshape(P, KT * 32)
    w_pool = a["pool_w"][0].reshape(4, 2, P, 256).transpose(2, 0, 1, 3).reshape(P, 2048)
    gu = np.stack([a["w_gate"][0], a["w_up"][0]], axis=1).reshape(E, 2, KT, P, FT, P)
    gu = gu.transpose(0, 4, 3, 1, 2, 5).reshape(E, FT, P, 2048)
    dn = a["w_down"][0].reshape(E, 2, 2, P, D).transpose(0, 1, 3, 2, 4).reshape(E, 2, P, 2048)
    return {
        "consts": cst, "bconsts": bc, "vecs": vec, "rows": row, "inv": inv,
        "w_late": w_late, "b_late": a["b_ada"][0][2 * D:].reshape(8, 512), "norm2": a["norm2_w"],
        "fnorm": a["final_norm_w"][None], "x": np.concatenate([a["x_prompt"][0], a["x_sample"][0]]),
        "states0": a["state_ssm"][0, 0].transpose(0, 3, 1, 2).reshape(2, N, D),
        "w_ring": np.stack(parts), "w_dt": w_dt, "w_pool": w_pool,
        "w_router": a["w_router"].reshape(KT, P, E).transpose(1, 0, 2).reshape(P, KT * E),
        "w_exp": np.concatenate([gu, dn], axis=1),
    }


_OUTS = {"y_out": (TOK, D), "s_out": (2, D, N)}


def kernel(**inputs):
    import concourse.bacc as bacc
    from concourse.bass_utils import run_bass_kernel_spmd

    nc = bacc.Bacc("TRN2", target_bir_lowering=False, num_devices=1)
    a = {k: np.asarray(v) for k, v in inputs.items()}
    arrays = {k: np.ascontiguousarray(v) for k, v in layout(a).items()}
    aps = {k: nc.dram_tensor(k, v.shape, mybir.dt.from_np(v.dtype), kind="ExternalInput").ap()
           for k, v in arrays.items()}
    for name, shape in _OUTS.items():
        aps[name] = nc.dram_tensor(name, shape, F32, kind="ExternalOutput").ap()
    trunk_kernel(nc, **aps)
    r = run_bass_kernel_spmd(nc, [arrays], core_ids=[0]).results[0]
    y, s = np.asarray(r["y_out"]), np.asarray(r["s_out"])
    return y[None, :CTX], y[None, CTX:], s.reshape(1, 1, 2, H, HD, N)
```
